# Optimizing a Trainium2 kernel written in Bass

```python
import math
import jax, jax.numpy as jnp
from jax import lax
import numpy as np

D_MODEL = 1024
BATCH = 1
SEQ = 512
DEPTH = 2

CHUNK = 64
N_META = 16
N_A_LAYERS = DEPTH // 2
N_B_LAYERS = DEPTH - N_A_LAYERS
CONV_W = 3
HEAD_DIM = 64
N_HEADS = D_MODEL // (2 * HEAD_DIM)
ROT_DIM = HEAD_DIM // 4
ROPE_THETA = 500000.0
Q_BLOCK = 128
N_GROUPS = 4
EXPERTS_PER_GROUP = 8
N_EXPERTS = N_GROUPS * EXPERTS_PER_GROUP
TOP_K = 2
D_EXPERT = 512
ROW_BLOCK = 128
EPS = 1e-6

kernel_name = "yoco_shortconv_diffattn_hiermoe"

def rmsnorm(x, g):
    xf = x.astype(jnp.float32)
    y = xf * lax.rsqrt(jnp.mean(xf * xf, axis=-1, keepdims=True) + EPS) * g.astype(jnp.float32)
    return y.astype(x.dtype)

def partial_rotary(x, pos):
    half = ROT_DIM // 2
    inv_freq = ROPE_THETA ** (-jnp.arange(half, dtype=jnp.float32) * 2.0 / ROT_DIM)
    ang = pos.astype(jnp.float32)[:, None] * inv_freq[None, :]
    ang = ang.reshape((1, ang.shape[0]) + (1,) * (x.ndim - 3) + (half,))
    cos, sin = jnp.cos(ang), jnp.sin(ang)
    xf = x.astype(jnp.float32)
    x1, x2, rest = xf[..., :half], xf[..., half:ROT_DIM], xf[..., ROT_DIM:]
    out = jnp.concatenate([x1 * cos - x2 * sin, x2 * cos + x1 * sin, rest], axis=-1)
    return out.astype(x.dtype)

def short_conv_mixer(hn, w_in, conv_w, w_out):
    d = hn.shape[-1]
    b_gate, c_gate, u = jnp.split(hn @ w_in, 3, axis=-1)
    z = lax.conv_general_dilated(
        c_gate * u, conv_w[:, None, :].astype(hn.dtype), window_strides=(1,),
        padding=[(CONV_W - 1, 0)], dimension_numbers=("NWC", "WIO", "NWC"),
        feature_group_count=d)
    return (b_gate * z) @ w_out

def grouped_experts(xf, expert, gate, w_gate, w_up, w_down):
    t, d = xf.shape
    a = t * TOP_K
    n_blk = a // ROW_BLOCK + N_EXPERTS
    rows = n_blk * ROW_BLOCK
    e_flat = expert.reshape(-1)
    order = jnp.argsort(e_flat)
    e_sorted = e_flat[order]
    counts = jnp.bincount(e_flat, length=N_EXPERTS)
    padded = (counts + ROW_BLOCK - 1) // ROW_BLOCK * ROW_BLOCK
    ends = jnp.cumsum(padded)
    pad_start = ends - padded
    start = jnp.cumsum(counts) - counts
    dest = pad_start[e_sorted] + (jnp.arange(a) - start[e_sorted])
    src_tok = order // TOP_K
    buf = jnp.zeros((rows, d), xf.dtype).at[dest].set(xf[src_tok])
    row_w = jnp.zeros((rows,), jnp.float32).at[dest].set(gate.reshape(-1)[order])
    row_tok = jnp.zeros((rows,), jnp.int32).at[dest].set(src_tok.astype(jnp.int32))
    blk_expert = jnp.minimum(
        jnp.searchsorted(ends, jnp.arange(n_blk) * ROW_BLOCK, side="right"), N_EXPERTS - 1)

    def run_block(args):
        xb, e = args
        return (jax.nn.silu(xb @ w_gate[e]) * (xb @ w_up[e])) @ w_down[e]

    yb = lax.map(run_block, (buf.reshape(n_blk, ROW_BLOCK, d), blk_expert))
    y = yb.reshape(rows, d) * row_w[:, None].astype(xf.dtype)
    return jax.ops.segment_sum(y, row_tok, num_segments=t)

def hier_moe(hn, w_rg, b_rg, w_re, b_re, w_gate, w_up, w_down):
    shp = hn.shape
    xf = hn.reshape(-1, shp[-1])
    t = xf.shape[0]
    lg = (xf @ w_rg).astype(jnp.float32) + b_rg.astype(jnp.float32)
    grp = jnp.argmax(lg, axis=-1)
    p_grp = jnp.take_along_axis(jax.nn.softmax(lg, axis=-1), grp[:, None], axis=-1)
    le = ((xf @ w_re).astype(jnp.float32) + b_re.astype(jnp.float32)).reshape(
        t, N_GROUPS, EXPERTS_PER_GROUP)
    le = jnp.take_along_axis(le, grp[:, None, None], axis=1)[:, 0]
    top_v, top_i = lax.top_k(le, TOP_K)
    gate = p_grp * jax.nn.softmax(top_v, axis=-1)
    expert = grp[:, None].astype(jnp.int32) * EXPERTS_PER_GROUP + top_i.astype(jnp.int32)
    return grouped_experts(xf, expert, gate, w_gate, w_up, w_down).reshape(shp)

def lambda_init(layer_idx):
    return 0.8 - 0.6 * math.exp(-0.3 * layer_idx)

def diff_attention(hn, w_q, lam_p, subln_g, w_out, kk, v, key_chunk, lam_init):
    bsz, seq, _ = hn.shape
    n_blk = seq // Q_BLOCK
    q = (hn @ w_q).reshape(bsz, seq, N_HEADS, 2, HEAD_DIM)
    q = partial_rotary(q, N_META + jnp.arange(seq)) * (HEAD_DIM ** -0.5)
    q = q.reshape(bsz, n_blk, Q_BLOCK, N_HEADS, 2, HEAD_DIM).transpose(1, 4, 0, 3, 2, 5)
    q_chunk = (1 + jnp.arange(seq) // CHUNK).reshape(n_blk, Q_BLOCK)
    lp = lam_p.astype(jnp.float32)
    lam = jnp.exp(jnp.sum(lp[0] * lp[1])) - jnp.exp(jnp.sum(lp[2] * lp[3])) + lam_init

    def attend(args):
        qb, qc = args
        visible = key_chunk[None, :] <= qc[:, None]
        s = jnp.einsum("nbhqd,nbhkd->nbhqk", qb, kk, preferred_element_type=jnp.float32)
        p = jax.nn.softmax(jnp.where(visible, s, jnp.finfo(jnp.float32).min), axis=-1)
        a = p[0] - lam * p[1]
        return jnp.einsum("bhqk,bhkd->bhqd", a.astype(v.dtype), v)

    o = lax.map(attend, (q, q_chunk))
    o = o.transpose(1, 0, 3, 2, 4).reshape(bsz, seq, N_HEADS, 2 * HEAD_DIM)
    o = rmsnorm(o, subln_g) * (1.0 - lam_init)
    return o.reshape(bsz, seq, N_HEADS * 2 * HEAD_DIM) @ w_out

def setup_inputs(seed: int = 0) -> dict:
    key = jax.random.key(seed)
    ks = jax.random.split(key, 24)
    d, f, e = D_MODEL, D_EXPERT, N_EXPERTS
    nrm = lambda k, shp, s: jax.random.normal(k, shp, jnp.float32) * s
    gain = lambda k, shp: 1.0 + 0.02 * jax.random.normal(k, shp, jnp.float32)
    return {
        "x": jax.random.normal(ks[0], (BATCH, SEQ, d), jnp.float32),
        "meta_tokens": nrm(ks[1], (N_META, d), 1.0),
        "a_norm": gain(ks[2], (N_A_LAYERS, d)),
        "a_w_in": nrm(ks[3], (N_A_LAYERS, d, 3 * d), d ** -0.5),
        "a_conv": nrm(ks[4], (N_A_LAYERS, CONV_W, d), CONV_W ** -0.5),
        "a_w_out": nrm(ks[5], (N_A_LAYERS, d, d), d ** -0.5),
        "kv_norm": gain(ks[6], (d,)),
        "w_kv": nrm(ks[7], (d, 2 * d), d ** -0.5),
        "b_norm": gain(ks[8], (N_B_LAYERS, d)),
        "b_w_q": nrm(ks[9], (N_B_LAYERS, d, d), d ** -0.5),
        "b_lambda": nrm(ks[10], (N_B_LAYERS, 4, HEAD_DIM), 0.1),
        "b_subln": gain(ks[11], (N_B_LAYERS, 2 * HEAD_DIM)),
        "b_w_out": nrm(ks[12], (N_B_LAYERS, d, d), d ** -0.5),
        "ffn_norm": gain(ks[13], (DEPTH, d)),
        "r_group": nrm(ks[14], (DEPTH, d, N_GROUPS), d ** -0.5),
        "r_group_b": nrm(ks[15], (DEPTH, N_GROUPS), 0.01),
        "r_expert": nrm(ks[16], (DEPTH, d, e), d ** -0.5),
        "r_expert_b": nrm(ks[17], (DEPTH, e), 0.01),
        "e_gate": nrm(ks[18], (DEPTH, e, d, f), d ** -0.5),
        "e_up": nrm(ks[19], (DEPTH, e, d, f), d ** -0.5),
        "e_down": nrm(ks[20], (DEPTH, e, f, d), f ** -0.5),
        "final_norm": gain(ks[21], (d,)),
    }

def reference(x, meta_tokens, a_norm, a_w_in, a_conv, a_w_out, kv_norm, w_kv, b_norm, b_w_q,
              b_lambda, b_subln, b_w_out, ffn_norm, r_group, r_group_b, r_expert, r_expert_b,
              e_gate, e_up, e_down, final_norm):
    bsz, seq, d = x.shape
    length = seq + N_META
    meta = jnp.broadcast_to(meta_tokens.astype(x.dtype)[None], (bsz, N_META, d))
    h = jnp.concatenate([meta, x], axis=1)
    layer = 0
    for i in range(N_A_LAYERS):
        h = h + short_conv_mixer(rmsnorm(h, a_norm[i]), a_w_in[i], a_conv[i], a_w_out[i])
        h = h + hier_moe(rmsnorm(h, ffn_norm[layer]), r_group[layer], r_group_b[layer],
                         r_expert[layer], r_expert_b[layer], e_gate[layer], e_up[layer],
                         e_down[layer])
        layer += 1
    kv = rmsnorm(h, kv_norm) @ w_kv
    k = kv[..., :d].reshape(bsz, length, N_HEADS, 2, HEAD_DIM)
    k = partial_rotary(k, jnp.arange(length)).transpose(3, 0, 2, 1, 4)
    v = kv[..., d:].reshape(bsz, length, N_HEADS, 2 * HEAD_DIM).transpose(0, 2, 1, 3)
    pos = jnp.arange(length)
    key_chunk = jnp.where(pos < N_META, 0, 1 + (pos - N_META) // CHUNK)
    h = h[:, N_META:]
    for j in range(N_B_LAYERS):
        h = h + diff_attention(rmsnorm(h, b_norm[j]), b_w_q[j], b_lambda[j], b_subln[j],
                               b_w_out[j], k, v, key_chunk, lambda_init(layer))
        h = h + hier_moe(rmsnorm(h, ffn_norm[layer]), r_group[layer], r_group_b[layer],
                         r_expert[layer], r_expert_b[layer], e_gate[layer], e_up[layer],
                         e_down[layer])
        layer += 1
    return rmsnorm(h, final_norm)


_drawn_inputs = setup_inputs


def setup_inputs(seed=0):
    import zlib

    import numpy as np

    out = dict(_drawn_inputs(seed))
    spreads = {}
    factors = {'b_norm': 3.684,
     'b_subln': 4.117,
     'r_group_b': 8.0,
     'r_expert_b': 3.019,
     'final_norm': 2.749}
    for name, (base, spread) in spreads.items():
        noise = np.random.default_rng([zlib.crc32(name.encode()), seed]).standard_normal(out[name].shape)
        drawn = base * np.exp(spread * noise) if base else spread * noise
        out[name] = __import__('jax').numpy.asarray(drawn.astype(out[name].dtype))
    for name, factor in factors.items():
        out[name] = (out[name] * factor).astype(out[name].dtype)
    return out
```

```python
import math
from contextlib import ExitStack

import concourse.bass as bass
from concourse import mybir

F32 = mybir.dt.float32
U32 = mybir.dt.uint32
I32 = mybir.dt.int32
ALU = mybir.AluOpType
ACT = mybir.ActivationFunctionType
AX = mybir.AxisListType.X

P = 128
D = 1024
KC = D // P
SEQ, META = 512, 16
NX = SEQ // P
LEN = SEQ + META
HALF = LEN // 2
W = 512
FE = 512
FC = FE // P
G, EPG = 4, 8
E = G * EPG
HD, NH = 64, 8
ROT = HD // 4
EPS = 1e-6
LAM_INIT = 0.8 - 0.6 * math.exp(-0.3)

C = 64
NBLK = -(-LEN // C)
STRIDE = NBLK * C
SPREAD = 1024
EMPTY = 4 * SPREAD - 1
MAXMORE = 16

MORE_STEPS = 2 * MAXMORE + 5

RING = 6
UNIT = KC * W
U_IN, U_AOUT, U_MOE0 = 0, 6, 8
U_KV = U_MOE0 + 3 * E
U_Q = U_KV + 4
U_BOUT = U_Q + 2
U_MOE1 = U_BOUT + 2
U_MOE = (U_MOE0, U_MOE1)
PAIRS = E // 2

CONST = {}
_at = 0
for _name, _n in (("ident", P), ("upper", P), ("ones", P), ("iota", E), ("iota100", EPG),
                  ("more", (NBLK - 1) * E), ("cos", 5 * ROT), ("sin", 5 * ROT), ("row", 10), ("eps", 1), ("minus_half", NH)):
    CONST[_name] = (_at, _n)
    _at += _n
NCONST = _at


def rows(t):
    return P if t < NX else META


def cols(t):
    return (META + t * P, META + (t + 1) * P) if t < NX else (0, META)


class Tally:

    def __init__(self, eng, sem):
        self.eng, self.sem, self.n = eng, sem, 0

    def order(self, ins):
        ins.then_inc(self.sem, 1)
        self.n += 1
        self.eng.wait_ge(self.sem, self.n)


def build(nc, x, meta_tokens, a_norm, a_w_in, a_conv, a_w_out, kv_norm, w_kv, b_norm, b_w_q, b_lambda, b_subln,
          b_w_out, ffn_norm, r_group, r_group_b, r_expert, r_expert_b, e_gate, e_up, e_down, final_norm, table, out):
    with ExitStack() as ctx:
        def sb(name, shape, dt=F32):
            return ctx.enter_context(nc.sbuf_tensor(name, shape, dt))

        def sem(name):
            return ctx.enter_context(nc.semaphore(name))

        hn_dram = [nc.dram_tensor(f"hn_rows{l}", [(LEN, SEQ)[l], D], F32).ap() for l in range(2)]
        y_dram = [nc.dram_tensor(f"expert_rows{l}", [2 * SPREAD, D], F32).ap() for l in range(2)]
        slot_dram = [nc.dram_tensor(f"slot_table{l}", [E * STRIDE, 1], F32).ap() for l in range(2)]

        ring = sb("ring", [P, RING, UNIT])
        h = sb("h", [P, NX + 1, D])
        act17 = sb("act17", [P, KC * LEN])
        arena = sb("arena", [P, 2 * KC * LEN + (NX + 1) * D])
        nat = sb("nat", [P, 2, D])
        knat = sb("knat", [P, 2, W])
        const = sb("const", [P, NCONST])
        gain = sb("gain", [P, 5, KC])
        conv = sb("conv", [P, 3 * KC])
        wr = sb("wr", [P, 2, KC, G + E])
        rbias = sb("rbias", [P, 2, G + E])
        subln = sb("subln", [P, P])
        lam = sb("lam", [P, 8])
        ssq = sb("ssq", [P, 8])
        rstd = sb("rstd", [P, 8])
        gate = sb("gate", [P, 2, NX + 1])
        dest = sb("dest", [P, 2 * (NX + 1)], U32)
        src_rows = sb("src_rows", [P, NBLK * E], U32)
        src_row = src_rows[0:C, :]
        dst_row = sb("dst_row", [C, NBLK * E], U32)
        src_now = sb("src_now", [C, 2], U32)
        dst_now = sb("dst_now", [C, 2], U32)
        counted = sb("counted", [1, E])
        n_more = sb("n_more", [1, 2])
        n_more_i = sb("n_more_i", [1, 1], I32)
        more_i = sb("more_i", [1, 2, MAXMORE], I32)
        small = sb("small", [P, 64])
        rope = src_rows[:, 0:16 * ROT].bitcast(F32)

        actT = act17[:, :].rearrange("p (k n) -> p k n", k=KC)
        y_out = act17[:, 0:2 * D].rearrange("p (b n) -> p b n", b=2)
        xT = act17[:, 2 * D:2 * D + 2 * KC * C].rearrange("p (b n) -> p b n", b=2)
        hT = act17[:, 3072:3584].rearrange("p (b n) -> p b n", b=2)
        silu = act17[:, 3584:4096].rearrange("p (b n) -> p b n", b=2)
        logit = act17[:, 0:180].rearrange("p (t n) -> p t n", t=NX + 1)
        chosen = act17[:, 192:512].rearrange("p (c n) -> p c n", n=E)
        work = act17[:, 512:832].rearrange("p (c n) -> p c n", n=E)
        member = act17[:, 832:992].rearrange("p (c n) -> p c n", n=E)
        slots = act17[0:E, 1024:1024 + STRIDE]
        leg = act17[:, 1600:1640].rearrange("p (t n) -> p t n", n=EPG)
        hot = act17[:, 1640:1720].rearrange("p (k t n) -> p k t n", k=2, n=EPG)
        cand = act17[:, 1720:1760].rearrange("p (t n) -> p t n", n=EPG)
        rv = act17[:, 1760:1860].rearrange("p (c t) -> p c t", t=NX + 1)
        scan = act17[0:1, 0:(NBLK - 1) * E]
        spread = act17[0:1, 3072:3072 + 256]

        kT = arena[:, 0:KC * LEN].rearrange("p (k n) -> p k n", k=KC)
        V = arena[:, KC * LEN:KC * LEN + 5 * D].rearrange("p (t n) -> p t n", n=D)
        third = arena[:, KC * LEN + 5 * D:]
        actT2 = third.rearrange("p (k n) -> p k n", k=KC)
        y_in = arena[:, 0:8 * D].rearrange("p (s c n) -> p s c n", s=4, c=2)
        more_w = arena[:, 0:3 * UNIT].rearrange("p (u n) -> p u n", u=3)
        stage = arena[:, 0:1600]
        stage_r = stage[:, 0:2 * KC * (G + E)].rearrange("p (l n) -> p l n", l=2)
        stage_lam = stage[:, 576:832]
        stage_conv = stage[0:3 * KC, 832:960]
        stage_empty = stage[0:E, 960:960 + STRIDE]
        va = KC * LEN
        c_gate = arena[:, va:va + 2 * LEN].rearrange("p (b n) -> p b n", b=2)
        cu = arena[:, va + 2 * LEN:va + 3 * LEN + 2]
        z = arena[:, va + 3 * LEN + 2:va + 4 * LEN + 2]
        prob = third[:, 0:4 * LEN].rearrange("p (b c n) -> p b c n", b=2, c=2)
        probT = third[:, 4 * LEN:4 * LEN + 10 * P].rearrange("p (b n) -> p b n", b=2)
        final_gain = knat[:, :, :].rearrange("p b n -> p (b n)")
        square = final_gain

        def cst(name, r=P):
            a, n = CONST[name]
            return const[0:r, a:a + n]

        ident = cst("ident")

        ps = ctx.enter_context(nc.psum_tensor("ps", [P, 8, W], F32))
        flat = ps[:, :, :].rearrange("p b n -> p (b n)")

        x_landed = [sem(f"x_landed{t}") for t in range(NX + 1)]
        const_landed = sem("const_landed")
        param_landed = sem("param_landed")
        ring_landed = [sem(f"ring_landed{s}") for s in range(RING)]
        unit_used = sem("unit_used")
        passed = sem("passed")
        dve_step, act_step = sem("dve_step"), sem("act_step")
        params_ready, conv_turned, conv_ready = sem("params_ready"), sem("conv_turned"), sem("conv_ready")
        empty_set, empty_stored = sem("empty_set"), sem("empty_stored")
        lam_ready, lam_exp = sem("lam_ready"), sem("lam_exp")
        squared = [sem(f"squared{n}") for n in range(5)]
        scaled = [sem(f"scaled{n}") for n in range(5)]
        rstd_ready = [sem(f"rstd_ready{n}") for n in range(5)]
        turned = [sem(f"turned{n}") for n in range(4)]
        turned_out = [sem(f"turned_out{n}") for n in range(4)]
        in_done, c_copied, u_taken, b_taken = sem("in_done"), sem("c_copied"), sem("u_taken"), sem("b_taken")
        out_done = [sem(f"out_done{l}") for l in range(2)]
        mixed = [sem(f"mixed{l}") for l in range(2)]
        logits_done = [sem(f"logits_done{l}") for l in range(2)]
        hn_stored = [[sem(f"hn_stored{l}{b}") for b in range(2)] for l in range(2)]
        shifted, exped = sem("shifted"), sem("exped")
        members, ranked = sem("members"), sem("ranked")
        placed, more_known = sem("placed"), sem("more_known")
        slots_stored = [sem(f"slots_stored{l}") for l in range(2)]
        slots_landed = sem("slots_landed")
        slots_turned, rows_ready = sem("slots_turned"), sem("rows_ready")
        gathered = [[sem(f"gathered{l}{b}") for b in range(2)] for l in range(2)]
        scattered = [[sem(f"scattered{l}{b}") for b in range(2)] for l in range(2)]
        index_set = [sem(f"index_set{l}") for l in range(2)]
        x_turned, xT_ready = [sem(f"x_turned{l}") for l in range(2)], [sem(f"xT_ready{l}") for l in range(2)]
        silu_ready, hT_ready = [sem(f"silu_ready{l}") for l in range(2)], [sem(f"hT_ready{l}") for l in range(2)]
        y_ready = [sem(f"y_ready{l}") for l in range(2)]
        more_steps = [sem(f"more_steps{l}") for l in range(2)]
        more_index = [sem(f"more_index{l}") for l in range(2)]
        more_gathered, more_w_landed = [sem(f"more_gathered{l}") for l in range(2)], [sem(f"more_w_landed{l}") for l in range(2)]
        more_turned, more_xT = [sem(f"more_turned{l}") for l in range(2)], [sem(f"more_xT{l}") for l in range(2)]
        more_up, more_silu = [sem(f"more_up{l}") for l in range(2)], [sem(f"more_silu{l}") for l in range(2)]
        more_hT, more_down = [sem(f"more_hT{l}") for l in range(2)], [sem(f"more_down{l}") for l in range(2)]
        more_y, more_scattered = [sem(f"more_y{l}") for l in range(2)], [sem(f"more_scattered{l}") for l in range(2)]
        y_landed = [[sem(f"y_landed{l}{s}") for s in range(4)] for l in range(2)]
        combined = [sem(f"combined{l}") for l in range(2)]
        proj_done, proj_copied = sem("proj_done"), sem("proj_copied")
        roped, rot_turned, rot_copied = sem("roped"), sem("rot_turned"), sem("rot_copied")
        scores_done, max_ready, exp_done = sem("scores_done"), sem("max_ready"), sem("exp_done")
        a_ready, a_turned, aT_copied, av_done = sem("a_ready"), sem("a_turned"), sem("aT_copied"), sem("av_done")
        o_copied, o_squared, o_ready = sem("o_copied"), sem("o_squared"), sem("o_ready")
        heads_meaned, heads_rooted = sem("heads_meaned"), sem("heads_rooted")
        o_turned, oT_copied = sem("o_turned"), sem("oT_copied")
        final_landed, final_ready = sem("final_landed"), sem("final_ready")
        stored = [sem(f"stored{b}") for b in range(2)]

        block = ctx.enter_context(nc.Block())

        N_PARAM = 15

        def tiles_of(layer):
            return NX + 1 if layer == 0 else NX

        JOBS = ([("k", f, t) for f in range(2) for t in range(NX + 1)]
                + [("v", f, t) for f in range(2) for t in range(NX + 1)]
                + [("q", f, t) for f in range(2) for t in range(NX)])
        ROT_JOBS = [p for p, j in enumerate(JOBS) if j[0] != "v"]
        STEPS = [(i, hh) for i in range(NX) for hh in range(NH)]

        def keys(i):
            return META + P * (i + 1)

        def score_view(n):
            i = STEPS[n][0]
            if i < NX - 1:
                return ps[:, 2 * (n % 2):2 * (n % 2) + 2, 0:keys(i)]
            return flat[:, 0:4 * W].rearrange("p (c n) -> p c n", c=2)[:, :, 0:keys(i)]

        def landed(eng, n):
            eng.wait_ge(ring_landed[n % RING], 16 * (n // RING + 1))

        def expert_unit(layer, q, u, j):
            n = U_MOE[layer] + 3 * u + j
            return n % RING, 16 * (n // RING + 1) + 16 * q

        def bcast(ap, n, at):
            return ap.unsqueeze(at).to_broadcast([*ap.shape[:at], n, *ap.shape[at:]])

        def load_more(eng, layer):
            eng.wait_ge(more_known, layer + 1)
            return eng.value_load(n_more_i[0:1, 0:1], min_val=0, max_val=MAXMORE)

        @block.sync
        def _(sp):
            def unit(n, src, **k):
                if n >= RING:
                    sp.wait_ge(unit_used, n - RING + 1)
                sp.dma_start(ring[:, n % RING, :].rearrange("p (k n) -> p k n", **k), src).then_inc(ring_landed[n % RING], 16)

            sp.dma_start(h[:, 0, :], x[0, 0:P, :]).then_inc(x_landed[0], 16)
            sp.dma_start(const[:, :], table).then_inc(const_landed, 16)
            sp.dma_start(gain[:, 0, :], a_norm[0].rearrange("(p k) -> p k", k=KC)).then_inc(const_landed, 16)
            for t in range(1, NX):
                sp.dma_start(h[:, t, :], x[0, t * P:(t + 1) * P, :]).then_inc(x_landed[t], 16)
            sp.dma_start(h[0:META, NX, :], meta_tokens).then_inc(x_landed[NX], 16)

            w_in = a_w_in[0].rearrange("(p k) n -> p k n", k=KC)
            for f in range(2):
                for s, part in enumerate((1, 2, 0)):
                    unit(U_IN + 3 * f + s, w_in[:, :, part * D + f * W:part * D + (f + 1) * W], k=KC)
            w_o = a_w_out[0].rearrange("(k p) n -> p k n", p=P)
            for f in range(2):
                unit(U_AOUT + f, w_o[:, :, f * W:(f + 1) * W], k=KC)

            def experts(layer):
                with sp.Fori(0, PAIRS) as q:
                    for u in range(2):
                        for j, w in enumerate((e_gate, e_up, e_down)):
                            n = U_MOE[layer] + 3 * u + j
                            sp.wait_ge(unit_used, q * 6 + (n - RING + 1))
                            src = w[layer, bass.ds(q * 2 + u, 1)].rearrange("o a b -> (o a) b")
                            src = src.rearrange("(p k) n -> p k n", k=KC) if j < 2 else src.rearrange("(f p) n -> p f n", p=P)
                            dst = ring[:, n % RING, :].rearrange("p (k n) -> p k n", k=KC if j < 2 else FC)
                            sp.dma_start(dst, src).then_inc(ring_landed[n % RING], 16)
                more = load_more(sp, layer)
                with sp.If(more > 0):
                    sp.wait_ge(more_steps[layer], MORE_STEPS)
                    with sp.Fori(0, more) as b:
                        ex = sp.value_load(more_i[0:1, 1, bass.ds(b, 1)], min_val=0, max_val=E - 1)
                        sp.wait_ge(more_down[layer], b + 1)
                        for j, w in enumerate((e_gate, e_up, e_down)):
                            src = w[layer, bass.ds(ex, 1)].rearrange("o a b -> (o a) b")
                            src = src.rearrange("(p k) n -> p k n", k=KC) if j < 2 else src.rearrange("(f p) n -> p f n", p=P)
                            dst = more_w[:, j, :].rearrange("p (k n) -> p k n", k=KC if j < 2 else FC)
                            sp.dma_start(dst, src).then_inc(more_w_landed[layer], 16)
                sp.nop()

            experts(0)
            wkv = w_kv.rearrange("(p k) n -> p k n", k=KC)
            for f in range(4):
                unit(U_KV + f, wkv[:, :, f * W:(f + 1) * W], k=KC)
            wq = b_w_q[0].rearrange("(p k) n -> p k n", k=KC)
            for f in range(2):
                unit(U_Q + f, wq[:, :, f * W:(f + 1) * W], k=KC)
            wo = b_w_out[0].rearrange("(k p) n -> p k n", p=P)
            for f in range(2):
                unit(U_BOUT + f, wo[:, :, f * W:(f + 1) * W], k=KC)
            experts(1)
            sp.wait_ge(o_ready, NX)
            sp.dma_start(final_gain, final_norm.partition_broadcast(P)).then_inc(final_landed, 16)
            for t in range(NX):
                sp.wait_ge(final_ready, t + 1)
                sp.dma_start(out[0, t * P:(t + 1) * P, :], nat[:, t % 2, :]).then_inc(stored[t % 2], 16)
            for b in range(2):
                sp.wait_ge(stored[b], 16 * NX // 2)

        @block.gpsimd
        def _(pool):
            def alone():
                pool.sem_inc(passed, 1)

            nc.gpsimd.memset(stage_empty, float(EMPTY)).then_inc(empty_set, 1)
            pool.wait_ge(empty_set, 1)
            for l in range(2):
                pool.dma_start(slot_dram[l].rearrange("(e s) o -> e (s o)", s=STRIDE), stage_empty).then_inc(empty_stored, 16)
            pool.wait_ge(param_landed, 16 * N_PARAM)
            for l in range(2):
                a = l * KC * (G + E)
                nc.gpsimd.tensor_copy(wr[:, l, :, 0:G], stage[:, a:a + KC * G].rearrange("p (k n) -> p k n", k=KC)).then_inc(params_ready, 1)
                nc.gpsimd.tensor_copy(wr[:, l, :, G:], stage[:, a + KC * G:a + KC * (G + E)].rearrange("p (k n) -> p k n", k=KC)).then_inc(params_ready, 1)
            pool.wait_ge(empty_stored, 32)

            def moe(layer):
                nt = tiles_of(layer)
                for t in range(nt):
                    pool.wait_ge(scaled[1 + 2 * layer], t + 1)
                    pool.dma_start(hn_dram[layer][t * P:t * P + rows(t), :], nat[0:rows(t), t % 2, :]).then_inc(hn_stored[layer][t % 2], 16)
                pool.wait_ge(placed, layer + 1)
                for k in range(2):
                    for t in range(nt):
                        c = k * nt + t
                        pool.indirect_dma_start(
                            slot_dram[layer], bass.IndirectOffsetOnAxis(dest[0:rows(t), c:c + 1], 0),
                            cst("row")[0:rows(t), 5 * k + t:5 * k + t + 1], None).then_inc(slots_stored[layer], 16)
                pool.wait_ge(slots_stored[layer], 16 * 2 * nt)
                pool.dma_start(slots, slot_dram[layer].rearrange("(e s) o -> e (s o)", s=STRIDE)).then_inc(slots_landed, 16)
                for b in range(2):
                    pool.wait_ge(hn_stored[layer][b], 16 * ((nt + 1 - b) // 2))
                pool.wait_ge(rows_ready, 2 * layer + 2)

                def gather(b, column, n):
                    nc.gpsimd.tensor_copy(src_now[:, b:b + 1], src_row[:, bass.ds(column, 1)]).then_inc(index_set[layer], 1)
                    pool.wait_ge(index_set[layer], n + 1)
                    alone()
                    pool.indirect_dma_start(nat[0:C, b, :], None, hn_dram[layer], bass.IndirectOffsetOnAxis(src_now[:, b:b + 1], 0),
                                            bounds_check=(LEN, SEQ)[layer] - 1, oob_is_err=False).then_inc(gathered[layer][b], 16)

                def pair(q, first, last):
                    for u in range(2):
                        n = q * 4 + 2 + 2 * u if not last else q * 4 + 2 + u
                        pool.wait_ge(y_ready[layer], q * 2 + u + 1)
                        if not first:
                            pool.wait_ge(scattered[layer][u], q * 16)
                        nc.gpsimd.tensor_copy(dst_now[:, u:u + 1], dst_row[:, bass.ds(q * 2 + u, 1)]).then_inc(index_set[layer], 1)
                        pool.wait_ge(index_set[layer], n + 1)
                        alone()
                        pool.indirect_dma_start(y_dram[layer], bass.IndirectOffsetOnAxis(dst_now[:, u:u + 1], 0), y_out[0:C, u, :], None,
                                                bounds_check=2 * SPREAD - 1, oob_is_err=False).then_inc(scattered[layer][u], 16)
                        if not last:
                            pool.wait_ge(x_turned[layer], q * 2 + u + 1)
                            gather(u, q * 2 + u + 2, n + 1)

                gather(0, 0, 0)
                gather(1, 1, 1)
                pair(0, True, False)
                with pool.Fori(1, PAIRS - 1) as q:
                    pair(q, False, False)
                pair(PAIRS - 1, False, True)
                for b in range(2):
                    pool.wait_ge(scattered[layer][b], 16 * PAIRS)

                more = load_more(pool, layer)
                with pool.If(more > 0):
                    pool.wait_ge(more_steps[layer], MORE_STEPS)
                    with pool.Fori(0, more) as b:
                        column = pool.value_load(more_i[0:1, 0, bass.ds(b, 1)], min_val=E, max_val=NBLK * E - 1)
                        nc.gpsimd.tensor_copy(src_now[:, 0:1], src_row[:, bass.ds(column, 1)]).then_inc(more_index[layer], 1)
                        nc.gpsimd.tensor_copy(dst_now[:, 0:1], dst_row[:, bass.ds(column, 1)]).then_inc(more_index[layer], 1)
                        pool.wait_ge(more_index[layer], b * 2 + 2)
                        alone()
                        pool.indirect_dma_start(nat[0:C, 0, :], None, hn_dram[layer], bass.IndirectOffsetOnAxis(src_now[:, 0:1], 0),
                                                bounds_check=(LEN, SEQ)[layer] - 1, oob_is_err=False).then_inc(more_gathered[layer], 16)
                        pool.wait_ge(more_y[layer], b + 1)
                        alone()
                        pool.indirect_dma_start(y_dram[layer], bass.IndirectOffsetOnAxis(dst_now[:, 0:1], 0), y_out[0:C, 0, :], None,
                                                bounds_check=2 * SPREAD - 1, oob_is_err=False).then_inc(more_scattered[layer], 16)
                        pool.wait_ge(more_scattered[layer], b * 16 + 16)
                pool.nop()
                for t in range(nt):
                    if t >= 4:
                        pool.wait_ge(combined[layer], t - 3)
                    for k in range(2):
                        pool.dma_start(y_in[0:rows(t), t % 4, k, :], y_dram[layer][k * SPREAD + t * P:k * SPREAD + t * P + rows(t), :]
                                       ).then_inc(y_landed[layer][t % 4], 16)

            moe(0)
            for i in range(NX):
                pool.wait_ge(heads_meaned, i + 1)
                nc.gpsimd.tensor_tensor(small[:, 32:40], small[:, 24:32], cst("minus_half"), ALU.pow).then_inc(heads_rooted, 1)
            moe(1)

        @block.scalar
        def _(act):
            step = Tally(act, act_step)
            for i, g in enumerate((ffn_norm[0], kv_norm, ffn_norm[1], b_norm[0])):
                act.dma_start(gain[:, 1 + i, :], g.rearrange("(p k) -> p k", k=KC)).then_inc(param_landed, 16)
            for l in range(2):
                a = l * KC * (G + E)
                act.dma_start(stage[:, a:a + KC * G], r_group[l].rearrange("(p k) n -> p (k n)", k=KC)).then_inc(param_landed, 16)
                act.dma_start(stage[:, a + KC * G:a + KC * (G + E)], r_expert[l].rearrange("(p k) n -> p (k n)", k=KC)).then_inc(param_landed, 16)
                act.dma_start(rbias[:, l, 0:G], r_group_b[l].partition_broadcast(P)).then_inc(param_landed, 16)
                act.dma_start(rbias[:, l, G:], r_expert_b[l].partition_broadcast(P)).then_inc(param_landed, 16)
            act.dma_start(stage_conv, a_conv[0].rearrange("w (j p) -> (w j) p", p=P)).then_inc(param_landed, 16)
            act.dma_start(subln[:, :], b_subln[0].partition_broadcast(P)).then_inc(param_landed, 16)
            act.dma_start(stage_lam, b_lambda[0].rearrange("a b -> (a b)").partition_broadcast(P)).then_inc(param_landed, 16)

            def root_mean_square(phase, t):
                r = rows(t)
                step.order(nc.scalar.activation(nat[0:r, t % 2, :], h[0:r, t, :], ACT.Square, scale=1.0 / math.sqrt(D),
                                                accum_out=ssq[0:r, t:t + 1]))
                nc.scalar.activation(ssq[0:r, t:t + 1], ssq[0:r, t:t + 1], ACT.Sqrt, bias=cst("eps", r)).then_inc(squared[phase], 1)

            def norm_tile(phase, t):
                r = rows(t)
                if t >= 2:
                    act.wait_ge(turned[phase], t - 1)
                    if phase in (1, 3):
                        act.wait_ge(hn_stored[(phase - 1) // 2][t % 2], 16 * (t // 2))
                root_mean_square(phase, t)
                act.wait_ge(rstd_ready[phase], t + 1)
                nc.scalar.activation(nat[0:r, t % 2, :], h[0:r, t, :], ACT.Copy, scale=rstd[0:r, t:t + 1]).then_inc(scaled[phase], 1)

            act.wait_ge(const_landed, 32)
            for t in range(NX + 1):
                act.wait_ge(x_landed[t], 16)
                norm_tile(0, t)

            for j in range(KC):
                act.wait_ge(in_done, 3 * j + 1)
                if j >= 2:
                    act.wait_ge(u_taken, j - 1)
                g = 2 * ((3 * j) % 4)
                nc.scalar.copy(c_gate[:, j % 2, :].rearrange("p (a n) -> p a n", a=2), ps[:, g:g + 2, 0:HALF]).then_inc(c_copied, 1)

            def moe(layer):
                for t in range(tiles_of(layer)):
                    act.wait_ge(mixed[layer], t + 1)
                    norm_tile(1 + 2 * layer, t)
                for k in range(2):
                    act.wait_ge(shifted, 2 * layer + k + 1)
                    e_view = (cand[:, 0:tiles_of(layer), 0:G], rv[:, 3, 0:tiles_of(layer)])[k]
                    nc.scalar.activation(e_view, e_view, ACT.Exp).then_inc(exped, 1)

                def pair(q, first):
                    for u in range(2):
                        base = U_MOE[layer] + 3 * u
                        act.wait_ge(unit_used, q * 6 + base + 1)
                        nc.scalar.activation(silu[:, u, :], ps[:, 2 + u, 0:FC * C], ACT.Silu).then_inc(silu_ready[layer], 1)
                        act.wait_ge(unit_used, q * 6 + base + 3)
                        if not first:
                            act.wait_ge(scattered[layer][u], q * 16)
                        nc.scalar.copy(y_out[0:C, u, :], flat[0:C, 6 * W:8 * W]).then_inc(y_ready[layer], 1)

                pair(0, True)
                with act.Fori(1, PAIRS) as q:
                    pair(q, False)
                more = load_more(act, layer)
                with act.If(more > 0):
                    act.wait_ge(scattered[layer][0], 16 * PAIRS)
                    with act.Fori(0, more) as b:
                        act.wait_ge(more_up[layer], b + 1)
                        nc.scalar.activation(silu[:, 0, :], ps[:, 2, 0:FC * C], ACT.Silu).then_inc(more_silu[layer], 1)
                        act.wait_ge(more_down[layer], b + 2)
                        nc.scalar.copy(y_out[0:C, 0, :], flat[0:C, 6 * W:8 * W]).then_inc(more_y[layer], 1)
                act.nop()

            moe(0)
            for t in range(NX + 1):
                act.wait_ge(combined[0], t + 1)
                norm_tile(2, t)
                if t == 0:
                    act.wait_ge(lam_ready, 1)
                    nc.scalar.activation(lam[:, 2:4], lam[:, 0:2], ACT.Exp).then_inc(lam_exp, 1)
            for p, (kind, f, t) in enumerate(JOBS):
                r = rows(t)
                act.wait_ge(proj_done, p + 1)
                if kind == "v":
                    dst = V[0:r, t, f * W:(f + 1) * W]
                else:
                    n = ROT_JOBS.index(p)
                    if n >= 2:
                        act.wait_ge(rot_turned, n - 1)
                    dst = knat[0:r, n % 2, :]
                nc.scalar.copy(dst, ps[0:r, 4 + p % 4, :]).then_inc(proj_copied, 1)

            def copy_aT(n):
                i = STEPS[n][0]
                act.wait_ge(a_turned, n + 1)
                if n >= 2:
                    act.wait_ge(av_done, n - 1)
                nc.scalar.copy(probT[:, n % 2, 0:(i + 1) * P], flat[:, 4 * W:4 * W + (i + 1) * P]).then_inc(aT_copied, 1)
                nc.scalar.copy(probT[0:META, n % 2, 4 * P:5 * P], flat[0:META, 5 * W:5 * W + P]).then_inc(aT_copied, 1)

            def copy_o(i):
                act.wait_ge(av_done, NH * (i + 1))
                if i >= 2:
                    act.wait_ge(o_turned, i - 1)
                nc.scalar.copy(nat[:, i % 2, :], flat[:, 6 * W:8 * W]).then_inc(o_copied, 1)
                act.wait_ge(o_copied, i + 1)
                if i == 0:
                    act.wait_ge(rot_turned, len(ROT_JOBS))
                if i >= 1:
                    act.wait_ge(o_ready, i)
                nc.scalar.activation(square, nat[:, i % 2, :], ACT.Square).then_inc(o_squared, 1)

            for n, (i, hh) in enumerate(STEPS):
                if n >= NH + 2 and n % NH == 2:
                    copy_o(n // NH - 1)
                act.wait_ge(max_ready, n + 1)
                if n >= 2:
                    act.wait_ge(a_turned, n - 1)
                s = score_view(n)
                for c in range(2):
                    nc.scalar.activation(prob[:, n % 2, c, 0:keys(i)], s[:, c, :], ACT.Exp, bias=small[:, 4 + 2 * (n % 2) + c:5 + 2 * (n % 2) + c],
                                         scale=HD ** -0.5, accum_out=small[:, 8 + 2 * (n % 2) + c:9 + 2 * (n % 2) + c]).then_inc(exp_done, 1)
                if n >= 1:
                    copy_aT(n - 1)
            copy_aT(len(STEPS) - 1)
            copy_o(NX - 1)

            moe(1)
            for t in range(NX):
                act.wait_ge(combined[1], t + 1)
                if t >= 2:
                    act.wait_ge(stored[t % 2], 16 * (t // 2))
                root_mean_square(4, t)

        @block.tensor
        def _(pe):
            mm = nc.tensor.matmul

            def turn(phase, t, free):
                r = rows(t)
                pe.wait_ge(scaled[phase], t + 1)
                if t >= 1:
                    pe.wait_ge(turned_out[phase], free(t))
                for k in range(KC):
                    last = nc.tensor.transpose(flat[:, k * P:k * P + r], nat[0:r, t % 2, k:D:KC], ident[0:r, 0:r])
                last.then_inc(turned[phase], 1)

            pe.wait_ge(const_landed, 32)
            for t in range(NX + 1):
                turn(0, t, lambda t: t)
            pe.wait_ge(param_landed, 16 * N_PARAM)
            nc.tensor.transpose(ps[:, 2, 0:3 * KC], stage_conv, ident[0:3 * KC, 0:3 * KC]).then_inc(conv_turned, 1)
            pe.wait_ge(turned_out[0], NX + 1)
            pe.wait_ge(conv_ready, 1)

            for j in range(KC):
                for s in range(3):
                    g = 3 * j + s
                    n = U_IN + 3 * (j // 4) + s
                    if j % 4 == 0:
                        landed(pe, n)
                    if g >= 4:
                        jj, ss = divmod(g - 4, 3)
                        pe.wait_ge((c_copied, u_taken, b_taken)[ss], jj + 1)
                    b = 2 * (g % 4)
                    w = ring[:, n % RING, :].rearrange("p (k n) -> p k n", k=KC)
                    for k in range(KC):
                        for a in range(2):
                            last = mm(ps[:, b + a, 0:HALF], w[:, k, (j % 4) * P:(j % 4 + 1) * P], actT[:, k, a * HALF:(a + 1) * HALF],
                                      start=(k == 0), stop=(k == KC - 1))
                    last.then_inc(in_done, 1)
                    if j % 4 == 3:
                        pe.wait_ge(in_done, g + 1)
                        pe.sem_inc(unit_used, 1)

            def out_proj(layer, t, src, col0):
                r, n = rows(t), (U_AOUT, U_BOUT)[layer]
                if t == 0:
                    if layer == 0:
                        pe.wait_ge(b_taken, KC)
                    landed(pe, n)
                    landed(pe, n + 1)
                if t >= 2:
                    pe.wait_ge(mixed[layer], t - 1)
                b = 4 + 2 * (t % 2)
                for f in range(2):
                    w = ring[:, (n + f) % RING, :].rearrange("p (k n) -> p k n", k=KC)
                    for k in range(KC):
                        last = mm(ps[0:r, b + f, :], src[:, k, col0:col0 + r], w[:, k, :], start=(k == 0), stop=(k == KC - 1))
                last.then_inc(out_done[layer], 1)

            def logits(layer, t):
                r = rows(t)
                pe.wait_ge(turned_out[1 + 2 * layer], t + 1)
                a = cols(t)[0]
                for k in range(KC):
                    last = mm(ps[0:r, 2, t * (G + E):(t + 1) * (G + E)], actT[:, k, a:a + r], wr[:, layer, k, :],
                              start=(k == 0), stop=(k == KC - 1))
                last.then_inc(logits_done[layer], 1)

            def gate_up(b, gate_w, up_w, between=None, after=None):
                for w, bank, note in ((gate_w, 2 + b, between), (up_w, 4 + b, after)):
                    note[0]()
                    for f in range(FC):
                        for k in range(KC):
                            last = mm(ps[:, bank, f * C:(f + 1) * C], w[:, k, f * P:(f + 1) * P], xT[:, b, k * C:(k + 1) * C],
                                      start=(k == 0), stop=(k == KC - 1))
                    if note[1] is not None:
                        last.then_inc(note[1], 1)

            def turn_block(b):
                pe.sem_inc(passed, 1)
                for k in range(KC):
                    last = nc.tensor.transpose(ps[:, b, k * C:(k + 1) * C], nat[0:C, b, k:D:KC], ident[0:C, 0:C])
                return last

            def down(b, w):
                for f in range(2):
                    for c in range(FC):
                        last = mm(ps[0:C, 6 + f, :], hT[:, b, c * C:(c + 1) * C], w[:, c, f * W:(f + 1) * W], start=(c == 0), stop=(c == FC - 1))
                return last

            def moe(layer, src, col):
                nt = tiles_of(layer)
                ph = 1 + 2 * layer
                for t in range(nt):
                    out_proj(layer, t, src, col(t))
                    if t == nt - 1:
                        pe.wait_ge(out_done[layer], nt)
                        pe.sem_inc(unit_used, 2)
                    if t == 0:
                        pe.wait_ge(params_ready, 4)
                    if t >= 1:
                        turn(ph, t - 1, lambda t: t)
                    if t >= 2:
                        logits(layer, t - 2)
                turn(ph, nt - 1, lambda t: t)
                logits(layer, nt - 2)
                logits(layer, nt - 1)

                pe.wait_ge(members, layer + 1)
                for i in range(nt + 1):
                    for j in range(min(i + 1, nt)):
                        r = rows(j)
                        lhs = cst("upper", r) if j == i else cst("ones", r)
                        last = mm(ps[:, 3, i * E:(i + 1) * E], lhs, member[0:r, j, :], start=(j == 0), stop=(j == min(i + 1, nt) - 1))
                last.then_inc(ranked, 1)
                pe.wait_ge(slots_landed, 16 * (layer + 1))
                for b in range(NBLK):
                    last = nc.tensor.transpose(ps[0:C, 2, b * E:(b + 1) * E], slots[:, b * C:(b + 1) * C], ident[0:E, 0:E])
                last.then_inc(slots_turned, 1)

                def pair(q, first, last_pair):
                    for u in range(2):
                        slot, value = zip(*(expert_unit(layer, q, u, j) for j in range(3)))
                        w = [ring[:, slot[j], :].rearrange("p (k n) -> p k n", k=KC if j < 2 else FC) for j in range(3)]
                        pe.wait_ge(xT_ready[layer], q * 2 + u + 1)
                        gate_up(u, w[0], w[1], (lambda: pe.wait_ge(ring_landed[slot[0]], value[0]), unit_used),
                                (lambda: pe.wait_ge(ring_landed[slot[1]], value[1]), unit_used))
                        if not (last_pair and u == 1):
                            pe.wait_ge(gathered[layer][1 - u], q * 16 + 16 * (1 + u))
                            turn_block(1 - u).then_inc(x_turned[layer], 1)
                        pe.wait_ge(ring_landed[slot[2]], value[2])
                        pe.wait_ge(hT_ready[layer], q * 2 + u + 1)
                        if not (first and u == 0):
                            pe.wait_ge(y_ready[layer], q * 2 + u)
                        down(u, w[2]).then_inc(unit_used, 1)

                pe.wait_ge(gathered[layer][0], 16)
                turn_block(0).then_inc(x_turned[layer], 1)
                pair(0, True, False)
                with pe.Fori(1, PAIRS - 1) as q:
                    pair(q, False, False)
                pair(PAIRS - 1, False, True)

                more = load_more(pe, layer)
                with pe.If(more > 0):
                    pe.wait_ge(y_ready[layer], E)
                    pe.sem_inc(more_down[layer], 1)
                    w = [more_w[:, j, :].rearrange("p (k n) -> p k n", k=KC if j < 2 else FC) for j in range(3)]
                    with pe.Fori(0, more) as b:
                        pe.wait_ge(more_gathered[layer], b * 16 + 16)
                        turn_block(0).then_inc(more_turned[layer], 1)
                        pe.wait_ge(more_xT[layer], b + 1)
                        pe.wait_ge(more_w_landed[layer], b * 48 + 48)
                        gate_up(0, w[0], w[1], (lambda: None, None), (lambda: None, more_up[layer]))
                        pe.wait_ge(more_hT[layer], b + 1)
                        down(0, w[2]).then_inc(more_down[layer], 1)
                pe.nop()

            moe(0, actT2, lambda t: cols(t)[0])

            def project(p):
                kind, f, t = JOBS[p]
                r = rows(t)
                n = {"k": U_KV, "v": U_KV + 2, "q": U_Q}[kind] + f
                src, a = (actT2, t * P) if kind == "q" else (actT, cols(t)[0])
                if t == 0:
                    landed(pe, n)
                if p >= 4:
                    pe.wait_ge(proj_copied, p - 3)
                if kind == "k" and f == 0:
                    pe.wait_ge(turned_out[2], min(2 * t + 2, 2 * NX + 1))
                w = ring[:, n % RING, :].rearrange("p (k n) -> p k n", k=KC)
                for k in range(KC):
                    last = mm(ps[0:r, 4 + p % 4, :], src[:, k, a:a + r], w[:, k, :], start=(k == 0), stop=(k == KC - 1))
                last.then_inc(proj_done, 1)
                if t == (NX - 1 if kind == "q" else NX):
                    pe.wait_ge(proj_done, p + 1)
                    pe.sem_inc(unit_used, 1)

            def turn_rot(n):
                _, f, t = JOBS[ROT_JOBS[n]]
                r = rows(t)
                pe.wait_ge(roped, n + 1)
                if n >= 2:
                    pe.wait_ge(rot_copied, n - 1)
                for c in range(4):
                    last = nc.tensor.transpose(ps[:, 2 + n % 2, c * P:c * P + r], knat[0:r, n % 2, c * P:(c + 1) * P], ident[0:r, 0:r])
                last.then_inc(rot_turned, 1)

            turn(2, 0, None)
            turn(2, 1, lambda t: 2 * t)
            nrot = 0
            for p in range(len(JOBS)):
                project(p)
                if p + 2 <= NX:
                    turn(2, p + 2, lambda t: 2 * t)
                while p >= NX - 1 and nrot < len(ROT_JOBS) and ROT_JOBS[nrot] <= p - 1:
                    turn_rot(nrot)
                    nrot += 1
            while nrot < len(ROT_JOBS):
                turn_rot(nrot)
                nrot += 1

            def scores(n):
                i, hh = STEPS[n]
                if i < NX - 1:
                    if n >= 2:
                        pe.wait_ge(exp_done, 2 * (n - 1))
                else:
                    pe.wait_ge(exp_done, 2 * n)
                s = score_view(n)
                for c in range(2):
                    q = actT[c * HD:(c + 1) * HD, hh, i * P:(i + 1) * P]
                    for a in range(0, keys(i), W):
                        b = min(a + W, keys(i))
                        last = mm(s[:, c, a:b], q, kT[c * HD:(c + 1) * HD, hh, a:b], start=True, stop=True)
                last.then_inc(scores_done, 1)

            def turn_a(n):
                i = STEPS[n][0]
                pe.wait_ge(a_ready, n + 1)
                if n >= 1:
                    pe.wait_ge(aT_copied, 2 * n)
                for j in range(i + 1):
                    nc.tensor.transpose(flat[:, 4 * W + j * P:4 * W + (j + 1) * P], prob[:, n % 2, 0, META + j * P:META + (j + 1) * P], ident)
                nc.tensor.transpose(ps[0:META, 5, 0:P], prob[:, n % 2, 0, 0:META], ident).then_inc(a_turned, 1)

            def weigh(n):
                i, hh = STEPS[n]
                pe.wait_ge(aT_copied, 2 * n + 2)
                if hh == 0 and i >= 1:
                    pe.wait_ge(o_copied, i)
                o = flat[:, 6 * W + hh * P:6 * W + (hh + 1) * P]
                mm(o, probT[0:META, n % 2, 4 * P:5 * P], V[0:META, NX, hh * P:(hh + 1) * P], start=True, stop=False)
                for j in range(i + 1):
                    last = mm(o, probT[:, n % 2, j * P:(j + 1) * P], V[:, j, hh * P:(hh + 1) * P], start=False, stop=(j == i))
                last.then_inc(av_done, 1)

            def turn_o(i):
                pe.wait_ge(o_ready, i + 1)
                for k in range(KC):
                    last = nc.tensor.transpose(flat[:, 4 * W + k * P:4 * W + (k + 1) * P], nat[:, i % 2, k * P:(k + 1) * P], ident)
                last.then_inc(o_turned, 1)

            pe.wait_ge(rot_copied, len(ROT_JOBS))
            pe.wait_ge(proj_copied, len(JOBS))
            last_n = len(STEPS) - 1
            for n in range(len(STEPS) + 2):
                if n <= last_n:
                    scores(n)
                if n >= 2:
                    weigh(n - 2)
                if n >= NH + 5 and n % NH == 5:
                    turn_o(n // NH - 1)
                    pe.wait_ge(oT_copied, n // NH)
                if 1 <= n <= last_n + 1:
                    turn_a(n - 1)
            turn_o(NX - 1)
            pe.wait_ge(oT_copied, NX)
            pe.wait_ge(o_copied, NX)
            moe(1, actT, lambda t: t * P)

        @block.vector
        def _(dve):
            v = nc.vector
            step = Tally(dve, dve_step)
            order = step.order

            def rstd_tile(phase, t):
                r = rows(t)
                dve.wait_ge(squared[phase], t + 1)
                v.reciprocal(rstd[0:r, t:t + 1], ssq[0:r, t:t + 1]).then_inc(rstd_ready[phase], 1)

            def gained(dst, t, g):
                r = rows(t)
                return v.tensor_tensor(dst, flat[:, 0:KC * P].rearrange("p (k n) -> p k n", k=KC)[:, :, 0:r],
                                       bcast(gain[:, g, :], r, 2), ALU.mult)

            dve.wait_ge(const_landed, 32)
            for t in range(NX + 1):
                rstd_tile(0, t)
                dve.wait_ge(turned[0], t + 1)
                gained(actT[:, :, cols(t)[0]:cols(t)[1]], t, 0).then_inc(turned_out[0], 1)
            dve.wait_ge(conv_turned, 1)
            v.tensor_copy(conv[:, :], ps[:, 2, 0:3 * KC]).then_inc(conv_ready, 1)
            dve.wait_ge(param_landed, 16 * N_PARAM)
            lp = stage_lam.rearrange("p (a b d) -> p a b d", a=2, b=2)
            order(v.tensor_tensor(lp[:, :, 0, :], lp[:, :, 0, :], lp[:, :, 1, :], ALU.mult))
            v.tensor_reduce(lam[:, 0:2], lp[:, :, 0, :], AX, ALU.add).then_inc(lam_ready, 1)
            order(v.tensor_scalar(subln[:, :], subln[:, :], 1.0 - LAM_INIT, None, ALU.mult))

            order(v.memset(cu[:, 0:2], 0.0))
            dve.wait_ge(conv_ready, 1)
            halves = lambda ap: ap.rearrange("p (a n) -> p a n", a=2)
            for j in range(KC):
                g = 3 * j + 1
                b = 2 * (g % 4)
                dve.wait_ge(c_copied, j + 1)
                dve.wait_ge(in_done, g + 1)
                v.tensor_tensor(halves(cu[:, 2:]), halves(c_gate[:, j % 2, :]), ps[:, b:b + 2, 0:HALF], ALU.mult).then_inc(u_taken, 1)
                dve.wait_ge(u_taken, j + 1)
                order(v.tensor_scalar(z, cu[:, 0:LEN], conv[:, j:j + 1], None, ALU.mult))
                for k in (1, 2):
                    order(v.scalar_tensor_tensor(z, cu[:, k:k + LEN], conv[:, k * KC + j:k * KC + j + 1], z, ALU.mult, ALU.add))
                b = 2 * ((g + 1) % 4)
                dve.wait_ge(in_done, g + 2)
                v.tensor_tensor(halves(actT2[:, j, :]), halves(z), ps[:, b:b + 2, 0:HALF], ALU.mult).then_inc(b_taken, 1)
                dve.wait_ge(b_taken, j + 1)

            def first_max(vals, n, width, top, index, onehot):
                tmp = work[:, 0:n, 0:width]
                iota = bcast(cst("iota")[:, 0:width], n, 1)
                order(v.tensor_reduce(top, vals, AX, ALU.max))
                order(v.tensor_tensor(tmp, vals, bcast(top, width, 2), ALU.is_equal))
                order(v.scalar_tensor_tensor(tmp, tmp, -100.0, bcast(cst("iota100")[:, 0:width], n, 1), ALU.mult, ALU.add))
                order(v.tensor_reduce(index, tmp, AX, ALU.min))
                order(v.tensor_tensor(onehot, iota, bcast(index, width, 2), ALU.is_equal))

            def moe(layer):
                nt = tiles_of(layer)
                ph = 1 + 2 * layer

                def add_tile(t):
                    r, b = rows(t), 4 + 2 * (t % 2)
                    dve.wait_ge(out_done[layer], t + 1)
                    v.tensor_tensor(h[0:r, t, :], h[0:r, t, :], flat[0:r, b * W:(b + 2) * W], ALU.add).then_inc(mixed[layer], 1)

                def norm_rest(t):
                    rstd_tile(ph, t)
                    dve.wait_ge(turned[ph], t + 1)
                    gained(actT[:, :, cols(t)[0]:cols(t)[1]], t, ph).then_inc(turned_out[ph], 1)

                for t in range(nt):
                    add_tile(t)
                    norm_rest(t)

                dve.wait_ge(logits_done[layer], nt)
                lg = ps[:, 2, 0:nt * (G + E)].rearrange("p (t n) -> p t n", t=nt)
                if nt > NX:
                    order(v.memset(logit[:, NX, :], 0.0))
                    v.tensor_tensor(logit[0:META, NX, :], lg[0:META, NX, :], rbias[0:META, layer, :], ALU.add).then_inc(dve_step, 1)
                    step.n += 1
                order(v.tensor_tensor(logit[:, 0:NX, :], lg[:, 0:NX, :], bcast(rbias[:, layer, :], NX, 1), ALU.add))
                L = logit[:, 0:nt, :]
                gtop, gidx, psum_g, e1 = rv[:, 0, 0:nt], rv[:, 1, 0:nt], rv[:, 2, 0:nt], rv[:, 3, 0:nt]
                v0, v1, i0, i1, pg = (rv[:, c, 0:nt] for c in range(4, 9))
                ghot = hot[:, 0, 0:nt, 0:G]
                first_max(L[:, :, 0:G], nt, G, gtop, gidx, ghot)
                ex = cand[:, 0:nt, 0:G]
                v.tensor_tensor(ex, L[:, :, 0:G], bcast(gtop, G, 2), ALU.subtract).then_inc(shifted, 1)
                prod = work[:, 0:nt, :]
                order(v.tensor_tensor(prod.rearrange("p t (g e) -> p t g e", g=G), L[:, :, G:].rearrange("p t (g e) -> p t g e", g=G),
                                      bcast(ghot, EPG, 3), ALU.mult))
                sel = leg[:, 0:nt, :]
                order(v.tensor_reduce(sel, prod.rearrange("p t (g e) -> p t e g", g=G), AX, ALU.add))
                oh = hot[:, 0, 0:nt, :]
                first_max(sel, nt, EPG, v0, i0, oh)
                order(v.scalar_tensor_tensor(sel, oh, -3.0e38, sel, ALU.mult, ALU.add))
                first_max(sel, nt, EPG, v1, i1, oh)
                v.tensor_tensor(e1, v1, v0, ALU.subtract).then_inc(shifted, 1)
                eid = rv[:, 10:12, 0:nt]
                for k, ik in enumerate((i0, i1)):
                    order(v.scalar_tensor_tensor(eid[:, k, :], gidx, float(EPG), ik, ALU.mult, ALU.add))
                ch = chosen[:, 0:2 * nt, :]
                for k in range(2):
                    order(v.tensor_tensor(ch[:, k * nt:(k + 1) * nt, :], bcast(cst("iota"), nt, 1), bcast(eid[:, k, :], E, 2), ALU.is_equal))
                v.tensor_tensor(member[:, 0:nt, :], ch[:, 0:nt, :], ch[:, nt:2 * nt, :], ALU.add).then_inc(members, 1)
                dve.wait_ge(exped, 2 * layer + 1)
                order(v.tensor_reduce(psum_g, ex, AX, ALU.add))
                order(v.reciprocal(pg, psum_g))
                dve.wait_ge(exped, 2 * layer + 2)
                den = rv[:, 9, 0:nt]
                order(v.tensor_scalar(den, e1, 1.0, None, ALU.add))
                order(v.reciprocal(den, den))
                order(v.tensor_tensor(gate[:, 0, 0:nt], pg, den, ALU.mult))
                order(v.tensor_tensor(gate[:, 1, 0:nt], gate[:, 0, 0:nt], e1, ALU.mult))
                dve.wait_ge(ranked, layer + 1)
                rank = ps[:, 3, 0:nt * E].rearrange("p (t e) -> p t e", t=nt)
                for k in range(2):
                    order(v.tensor_tensor(work[:, k * nt:(k + 1) * nt, :], ch[:, k * nt:(k + 1) * nt, :], rank, ALU.mult))
                rk = rv[:, 12:14, 0:nt]
                for k in range(2):
                    order(v.tensor_reduce(rk[:, k, :], work[:, k * nt:(k + 1) * nt, :], AX, ALU.add))
                    order(v.scalar_tensor_tensor(rk[:, k, :], eid[:, k, :], float(STRIDE), rk[:, k, :], ALU.mult, ALU.add))
                    order(v.tensor_copy(dest[:, k * nt:(k + 1) * nt], rk[:, k, :]))
                dve.sem_inc(placed, 1)
                order(v.tensor_copy(counted[:, :], ps[0:1, 3, nt * E:(nt + 1) * E]))
                flags = spread.rearrange("p (b e) -> p b e", e=E)
                order(v.tensor_tensor(flags, cst("more", 1).rearrange("p (b e) -> p b e", e=E), bcast(counted[:, :], NBLK - 1, 1), ALU.is_lt))
                order(v.tensor_reduce(n_more[:, 0:1], spread, AX, ALU.add))
                v.tensor_copy(n_more_i[:, :], n_more[:, 0:1]).then_inc(more_known, 1)
                dve.wait_ge(slots_turned, layer + 1)
                tab = ps[0:C, 2, 0:NBLK * E]
                order(v.tensor_scalar(arena[0:C, 0:NBLK * E], tab, float(SPREAD), float(SPREAD), ALU.is_ge, ALU.mult))
                v.tensor_copy(dst_row[:, :], tab).then_inc(rows_ready, 1)
                v.tensor_tensor(src_row[:, :], tab, arena[0:C, 0:NBLK * E], ALU.subtract).then_inc(rows_ready, 1)

                def take_x(b):
                    return v.tensor_tensor(xT[:, b, :].rearrange("p (k n) -> p k n", k=KC), ps[:, b, :].rearrange("p (k n) -> p k n", k=KC),
                                           bcast(gain[:, ph, :], C, 2), ALU.mult)

                def pair(q, last):
                    for u in range(2):
                        dve.wait_ge(silu_ready[layer], q * 2 + u + 1)
                        dve.wait_ge(unit_used, q * 6 + U_MOE[layer] + 3 * u + 2)
                        v.tensor_tensor(hT[:, u, :], silu[:, u, :], ps[:, 4 + u, 0:FC * C], ALU.mult).then_inc(hT_ready[layer], 1)
                        if not (last and u == 1):
                            dve.wait_ge(x_turned[layer], q * 2 + u + 2)
                            take_x(1 - u).then_inc(xT_ready[layer], 1)

                dve.wait_ge(x_turned[layer], 1)
                take_x(0).then_inc(xT_ready[layer], 1)
                with dve.Fori(0, PAIRS - 1) as q:
                    pair(q, False)
                pair(PAIRS - 1, True)

                dve.wait_ge(more_known, layer + 1)
                more = load_more(dve, layer)
                with dve.If(more > 0):
                    dve.wait_ge(scattered[layer][0], 16 * PAIRS)
                    dve.wait_ge(scattered[layer][1], 16 * PAIRS)
                    run = scan
                    n0 = 0
                    more_order = more_steps[layer]
                    def mo(ins):
                        nonlocal n0
                        ins.then_inc(more_order, 1)
                        n0 += 1
                        dve.wait_ge(more_order, n0)
                    mo(v.tensor_tensor(flags, cst("more", 1).rearrange("p (b e) -> p b e", e=E), bcast(counted[:, :], NBLK - 1, 1), ALU.is_lt))
                    mo(v.tensor_tensor_scan(run, spread, spread, 0.0, ALU.add, ALU.bypass))
                    for b in range(MAXMORE):
                        mo(v.tensor_scalar(spread, run, float(b), None, ALU.is_le))
                        mo(v.tensor_reduce(small[0:1, 16 + b:17 + b], spread, AX, ALU.add))
                    mo(v.tensor_scalar(small[0:1, 32:32 + MAXMORE], small[0:1, 16:16 + MAXMORE], float(E), None, ALU.add))
                    mo(v.tensor_copy(more_i[:, 0, :], small[0:1, 32:32 + MAXMORE]))
                    mo(v.tensor_scalar(more_i[:, 1, :], more_i[:, 0, :], E - 1, None, ALU.bitwise_and))
                    assert n0 == MORE_STEPS
                    with dve.Fori(0, more) as b:
                        dve.wait_ge(more_turned[layer], b + 1)
                        take_x(0).then_inc(more_xT[layer], 1)
                        dve.wait_ge(more_silu[layer], b + 1)
                        v.tensor_tensor(hT[:, 0, :], silu[:, 0, :], ps[:, 4, 0:FC * C], ALU.mult).then_inc(more_hT[layer], 1)
                dve.nop()

            def combine(layer, t):
                r, n = rows(t), t % 4
                dve.wait_ge(y_landed[layer][n], 32 * (t // 4 + 1))
                order(v.scalar_tensor_tensor(h[0:r, t, :], y_in[0:r, n, 0, :], gate[0:r, 0, t:t + 1], h[0:r, t, :], ALU.mult, ALU.add))
                v.scalar_tensor_tensor(h[0:r, t, :], y_in[0:r, n, 1, :], gate[0:r, 1, t:t + 1], h[0:r, t, :], ALU.mult, ALU.add
                                       ).then_inc(combined[layer], 1)

            moe(0)

            for t in range(NX + 1):
                combine(0, t)
                rstd_tile(2, t)
                dve.wait_ge(turned[2], t + 1)
                gained(actT[:, :, cols(t)[0]:cols(t)[1]], t, 2).then_inc(turned_out[2], 1)
                if t < NX:
                    gained(actT2[:, :, t * P:(t + 1) * P], t, 4).then_inc(turned_out[2], 1)

            def rotate(n):
                p = ROT_JOBS[n]
                _, f, t = JOBS[p]
                r = rows(t)
                dve.wait_ge(proj_copied, p + 1)
                if n:
                    dve.wait_ge(roped, n)
                X = knat[0:r, n % 2, :].rearrange("p (g d) -> p g d", d=HD)[:, :, 0:ROT]
                A = rope[0:r, 0:8 * ROT].rearrange("p (g d) -> p g d", g=8)
                B = rope[0:r, 8 * ROT:16 * ROT].rearrange("p (g d) -> p g d", g=8)
                cc = bcast(cst("cos", r)[:, t * ROT:(t + 1) * ROT], 8, 1)
                ss = bcast(cst("sin", r)[:, t * ROT:(t + 1) * ROT], 8, 1)
                hr = ROT // 2
                order(v.tensor_tensor(A, X, cc, ALU.mult))
                order(v.tensor_tensor(B[:, :, 0:hr], X[:, :, hr:], ss[:, :, 0:hr], ALU.mult))
                order(v.tensor_tensor(B[:, :, hr:], X[:, :, 0:hr], ss[:, :, hr:], ALU.mult))
                v.tensor_tensor(X, A, B, ALU.add).then_inc(roped, 1)

            def take_rot(n):
                kind, f, t = JOBS[ROT_JOBS[n]]
                r = rows(t)
                dve.wait_ge(rot_turned, n + 1)
                dst, a = (kT, cols(t)[0]) if kind == "k" else (actT, t * P)
                src = ps[:, 2 + n % 2, :].rearrange("p (c n) -> p c n", c=4)[:, :, 0:r]
                v.tensor_copy(dst[:, 4 * f:4 * f + 4, a:a + r], src).then_inc(rot_copied, 1)

            for n in range(len(ROT_JOBS)):
                rotate(n)
                if n >= 1:
                    take_rot(n - 1)
            take_rot(len(ROT_JOBS) - 1)

            dve.wait_ge(lam_exp, 1)
            order(v.tensor_tensor(lam[:, 4:5], lam[:, 3:4], lam[:, 2:3], ALU.subtract))
            order(v.tensor_scalar(lam[:, 5:6], lam[:, 4:5], -LAM_INIT, None, ALU.add))

            def maxima(n):
                i = STEPS[n][0]
                s = score_view(n)
                dve.wait_ge(scores_done, n + 1)
                order(v.memset(s[0:HD, :, keys(i) - HD:keys(i)], -3.4028235e38))
                if n:
                    dve.wait_ge(max_ready, n)
                order(v.tensor_reduce(small[:, 0:2], s, AX, ALU.max))
                o = 4 + 2 * (n % 2)
                v.tensor_scalar(small[:, o:o + 2], small[:, 0:2], -HD ** -0.5, None, ALU.mult).then_inc(max_ready, 1)

            def difference(n):
                k = keys(STEPS[n][0])
                o = 8 + 2 * (n % 2)
                dve.wait_ge(exp_done, 2 * n + 2)
                if n:
                    dve.wait_ge(a_ready, n)
                order(v.reciprocal(small[:, 12:14], small[:, o:o + 2]))
                order(v.tensor_tensor(small[:, 14:15], small[:, 13:14], lam[:, 5:6], ALU.mult))
                order(v.tensor_scalar(prob[:, n % 2, 1, 0:k], prob[:, n % 2, 1, 0:k], small[:, 14:15], None, ALU.mult))
                v.scalar_tensor_tensor(prob[:, n % 2, 0, 0:k], prob[:, n % 2, 0, 0:k], small[:, 12:13], prob[:, n % 2, 1, 0:k],
                                       ALU.mult, ALU.add).then_inc(a_ready, 1)

            def norm_heads(i):
                dve.wait_ge(o_squared, i + 1)
                order(v.tensor_reduce(small[:, 16:24], square.rearrange("p (h d) -> p h d", d=P), AX, ALU.add))
                v.tensor_scalar(small[:, 24:32], small[:, 16:24], 1.0 / P, EPS, ALU.mult, ALU.add).then_inc(heads_meaned, 1)
                dve.wait_ge(heads_rooted, i + 1)
                o = nat[:, i % 2, :].rearrange("p (h d) -> p h d", d=P)
                order(v.tensor_tensor(o, o, bcast(small[:, 32:40], P, 2), ALU.mult))
                v.tensor_tensor(o, o, bcast(subln[:, :], NH, 1), ALU.mult).then_inc(o_ready, 1)

            def take_o(i):
                dve.wait_ge(o_turned, i + 1)
                v.tensor_copy(actT[:, :, i * P:(i + 1) * P], flat[:, 4 * W:6 * W].rearrange("p (k n) -> p k n", k=KC)).then_inc(oT_copied, 1)

            for n in range(len(STEPS)):
                maxima(n)
                if n >= 1:
                    difference(n - 1)
                if n >= NH + 3 and n % NH == 3:
                    norm_heads(n // NH - 1)
                if n >= NH + 5 and n % NH == 5:
                    take_o(n // NH - 1)
            difference(len(STEPS) - 1)
            norm_heads(NX - 1)
            take_o(NX - 1)

            moe(1)
            dve.wait_ge(final_landed, 16)
            for t in range(NX):
                combine(1, t)
                dve.wait_ge(squared[4], t + 1)
                order(v.reciprocal(rstd[:, t:t + 1], ssq[:, t:t + 1]))
                v.scalar_tensor_tensor(nat[:, t % 2, :], h[:, t, :], rstd[:, t:t + 1], final_gain, ALU.mult, ALU.mult).then_inc(final_ready, 1)


_INS = ["x", "meta_tokens", "a_norm", "a_w_in", "a_conv", "a_w_out", "kv_norm", "w_kv", "b_norm", "b_w_q", "b_lambda", "b_subln",
        "b_w_out", "ffn_norm", "r_group", "r_group_b", "r_expert", "r_expert_b", "e_gate", "e_up", "e_down", "final_norm"]


def constants():
    import numpy as np

    t = np.zeros((P, NCONST), np.float32)

    def put(name, values):
        a, n = CONST[name]
        t[:, a:a + n] = values

    put("ident", np.eye(P))
    put("upper", np.triu(np.ones((P, P)), 1))
    put("ones", 1.0)
    put("iota", np.arange(E))
    put("iota100", np.arange(EPG) + 100)
    put("more", np.repeat(np.arange(1, NBLK) * C, E))
    half = ROT // 2
    freq = (np.float32(500000.0) ** (-np.arange(half, dtype=np.float32) * np.float32(2.0) / np.float32(ROT))).astype(np.float32)
    pos = np.zeros((5, P), np.float32)
    for i in range(NX):
        pos[i] = META + i * P + np.arange(P)
    pos[NX, :META] = np.arange(META)
    ang = (pos[:, :, None] * freq).astype(np.float32)
    cos, sin = np.cos(ang), np.sin(ang)
    put("cos", np.concatenate([cos, cos], -1).transpose(1, 0, 2).reshape(P, 5 * ROT))
    put("sin", np.concatenate([-sin, sin], -1).transpose(1, 0, 2).reshape(P, 5 * ROT))
    put("eps", EPS)
    put("minus_half", -0.5)
    row = np.arange(5)[None, :] * P + np.arange(P)[:, None]
    put("row", np.concatenate([row, row + SPREAD], 1))
    return t


def kernel(**inputs):
    import numpy as _np
    import concourse.bacc as _bacc
    from concourse.bass_utils import run_bass_kernel_spmd as _run

    nc = _bacc.Bacc("TRN2", target_bir_lowering=False, num_devices=1)
    arrays, args = {}, []
    for name in _INS:
        a = _np.ascontiguousarray(inputs[name])
        arrays[f"in_{name}"] = a
        args.append(nc.dram_tensor(f"in_{name}", a.shape, mybir.dt.from_np(a.dtype), kind="ExternalInput").ap())
    table = constants()
    arrays["in_table"] = table
    args.append(nc.dram_tensor("in_table", table.shape, F32, kind="ExternalInput").ap())
    args.append(nc.dram_tensor("out", (1, SEQ, D), F32, kind="ExternalOutput").ap())
    build(nc, *args)
    r = _run(nc, [arrays], core_ids=[0])
    return r.results[0]["out"]
```

```python
import math
from contextlib import ExitStack

import concourse.bass as bass
from concourse import mybir

F32 = mybir.dt.float32
U32 = mybir.dt.uint32
I32 = mybir.dt.int32
ALU = mybir.AluOpType
ACT = mybir.ActivationFunctionType
AX = mybir.AxisListType.X

P = 128
D = 1024
KC = D // P
SEQ, META = 512, 16
NX = SEQ // P
LEN = SEQ + META
HALF = LEN // 2
W = 512
FE = 512
FC = FE // P
G, EPG = 4, 8
E = G * EPG
HD, NH = 64, 8
ROT = HD // 4
EPS = 1e-6
LAM_INIT = 0.8 - 0.6 * math.exp(-0.3)

C = 64
NBLK = -(-LEN // C)
SPREAD = 1024
EMPTY = 4 * SPREAD
DH = D // 2
MAXMORE = 16

MORE_STEPS = 2 * MAXMORE + 4

RING = 6
UNIT = KC * W
U_IN, U_AOUT, U_MOE0 = 0, 6, 8
U_KV = U_MOE0 + 3 * E
U_Q = U_KV + 4
U_BOUT = U_Q + 2
U_MOE1 = U_BOUT + 2
U_MOE = (U_MOE0, U_MOE1)
ORDER = (("down", "gate", "up"), ("gate", "up", "down"))
PAIRS = E // 2

CONST = {}
_at = 0
for _name, _n in (("ident", P), ("upper", P), ("ones", P), ("iota", E), ("iota100", EPG),
                  ("more", (NBLK - 1) * E), ("cos", 5 * ROT), ("sin", 5 * ROT), ("row", 10), ("slot", C), ("half", 1), ("head", 1), ("eps", 1), ("minus_half", NH)):
    CONST[_name] = (_at, _n)
    _at += _n
NCONST = _at


def rows(t):
    return P if t < NX else META


def cols(t):
    return (META + t * P, META + (t + 1) * P) if t < NX else (0, META)


class Tally:

    def __init__(self, eng, sem):
        self.eng, self.sem, self.n = eng, sem, 0

    def order(self, ins):
        ins.then_inc(self.sem, 1)
        self.n += 1
        self.eng.wait_ge(self.sem, self.n)


def build(nc, x, meta_tokens, a_norm, a_w_in, a_conv, a_w_out, kv_norm, w_kv, b_norm, b_w_q, b_lambda, b_subln,
          b_w_out, ffn_norm, r_group, r_group_b, r_expert, r_expert_b, e_gate, e_up, e_down, final_norm, table, out):
    with ExitStack() as ctx:
        def sb(name, shape, dt=F32):
            return ctx.enter_context(nc.sbuf_tensor(name, shape, dt))

        def sem(name):
            return ctx.enter_context(nc.semaphore(name))

        hn_dram = [nc.dram_tensor(f"hn_rows{l}", [(LEN, SEQ)[l], D], F32).ap() for l in range(2)]
        y_dram = [nc.dram_tensor(f"expert_rows{l}", [2 * SPREAD, D], F32).ap() for l in range(2)]
        hn_halves = [a.rearrange("r (a n) -> (r a) n", a=2) for a in hn_dram]
        y_halves = [a.rearrange("r (a n) -> (r a) n", a=2) for a in y_dram]

        ring = sb("ring", [P, RING, UNIT])
        h = sb("h", [P, NX + 1, D])
        act17 = sb("act17", [P, KC * LEN])
        arena = sb("arena", [P, 2 * KC * LEN + (NX + 1) * D])
        nat = sb("nat", [P, 2, D])
        knat = sb("knat", [P, 2, W])
        const = sb("const", [P, NCONST])
        gain = sb("gain", [P, 5, KC])
        block_gain = sb("block_gain", [P, 2, KC])
        conv = sb("conv", [P, 3 * KC])
        wr = sb("wr", [P, 2, KC, G + E])
        rbias = sb("rbias", [P, 2, G + E])
        subln = sb("subln", [P, 1])
        lam = sb("lam", [P, 8])
        ssq = sb("ssq", [P, 8])
        rstd = sb("rstd", [P, 8])
        gate = sb("gate", [P, 2, NX + 1])
        src_row = sb("src_row", [P, E], U32)
        dst_row = sb("dst_row", [P, E], U32)
        src_now = sb("src_now", [P, 2], U32)
        dst_now = sb("dst_now", [P, 2], U32)
        counted = sb("counted", [1, E])
        n_more = sb("n_more", [1, 2])
        n_more_i = sb("n_more_i", [1, 1], I32)
        more_i = sb("more_i", [1, 2, MAXMORE], I32)
        small = sb("small", [P, 64])
        rope = sb("rope", [P, 16 * ROT])

        actT = act17[:, :].rearrange("p (k n) -> p k n", k=KC)
        y_out = act17[:, 0:2 * DH].rearrange("p (b n) -> p b n", b=2)
        xT = act17[:, 1024:2048].rearrange("p (b n) -> p b n", b=2)
        hT = act17[:, 2048:2560].rearrange("p (b n) -> p b n", b=2)
        silu = act17[:, 2560:3072].rearrange("p (b n) -> p b n", b=2)
        hidden = act17[:, 3072:3584].rearrange("p (b n) -> p b n", b=2)
        logit = act17[:, 0:180].rearrange("p (t n) -> p t n", t=NX + 1)
        chosen = act17[:, 192:512].rearrange("p (c n) -> p c n", n=E)
        work = act17[:, 512:832].rearrange("p (c n) -> p c n", n=E)
        member = act17[:, 832:1024].rearrange("p (c n) -> p c n", n=E)
        at_slot = act17[:, 2048:2048 + 10 * C].rearrange("p (c n) -> p c n", n=C)
        before = act17[:, 1024:1216].rearrange("p (c n) -> p c n", n=E)
        tab = act17[:, 1216:1216 + 3 * E].rearrange("p (c n) -> p c n", c=3)
        leg = act17[:, 1600:1640].rearrange("p (t n) -> p t n", n=EPG)
        hot = act17[:, 1640:1720].rearrange("p (k t n) -> p k t n", k=2, n=EPG)
        cand = act17[:, 1720:1760].rearrange("p (t n) -> p t n", n=EPG)
        rv = act17[:, 1760:1860].rearrange("p (c t) -> p c t", t=NX + 1)
        scan = act17[0:1, 0:(NBLK - 1) * E]
        spread = act17[0:1, 3072:3072 + (NBLK - 1) * E]

        kT = arena[:, 0:KC * LEN].rearrange("p (k n) -> p k n", k=KC)
        V = arena[:, KC * LEN:KC * LEN + 5 * D].rearrange("p (t n) -> p t n", n=D)
        third = arena[:, KC * LEN + 5 * D:]
        actT2 = third.rearrange("p (k n) -> p k n", k=KC)
        y_in = arena[:, 0:8 * D].rearrange("p (s c n) -> p s c n", s=4, c=2)
        more_w = arena[:, 0:3 * UNIT].rearrange("p (u n) -> p u n", u=3)
        tail = arena[:, 3 * UNIT:]
        src_more = tail[:, 0:(NBLK - 1) * E].bitcast(U32)
        dst_more = tail[:, 256:256 + (NBLK - 1) * E].bitcast(U32)
        row_of = tail[:, 512:832].rearrange("p (c n) -> p c n", n=E)
        rank_of = tail[:, 832:842]
        rank_b = tail[:, 842:852]
        tab_more = act17[:, 0:3 * 256].rearrange("p (c n) -> p c n", c=3)
        stage = arena[:, 0:1600]
        stage_r = stage[:, 0:2 * KC * (G + E)].rearrange("p (l n) -> p l n", l=2)
        stage_lam = stage[:, 576:832]
        stage_conv = stage[0:3 * KC, 832:960]
        va = KC * LEN
        c_gate = arena[:, va:va + 2 * LEN].rearrange("p (b n) -> p b n", b=2)
        cu = arena[:, va + 2 * LEN:va + 3 * LEN + 2]
        z = arena[:, va + 3 * LEN + 2:va + 4 * LEN + 2]
        prob = third[:, 0:6 * LEN].rearrange("p (b c n) -> p b c n", b=3, c=2)
        probT = (h[:, NX, 4 * P:8 * P], third[:, 6 * LEN:6 * LEN + 4 * P])
        metaT = third[:, 6 * LEN + 4 * P:6 * LEN + 6 * P].rearrange("p (b n) -> p b n", b=2)
        q_pad = h[:, NX, 0:4 * P].rearrange("p (b c n) -> p b c n", b=2, c=2)
        final_gain = knat[:, :, :].rearrange("p b n -> p (b n)")
        square = final_gain

        def cst(name, r=P):
            a, n = CONST[name]
            return const[0:r, a:a + n]

        ident = cst("ident")

        ps = ctx.enter_context(nc.psum_tensor("ps", [P, 8, W], F32))
        flat = ps[:, :, :].rearrange("p b n -> p (b n)")

        x_landed = [sem(f"x_landed{t}") for t in range(NX + 1)]
        const_landed = sem("const_landed")
        param_landed = sem("param_landed")
        ring_landed = [sem(f"ring_landed{s}") for s in range(RING)]
        unit_used = sem("unit_used")
        passed = sem("passed")
        dve_step, act_step = sem("dve_step"), sem("act_step")
        params_ready, conv_turned, conv_ready = sem("params_ready"), sem("conv_turned"), sem("conv_ready")
        lam_ready, lam_exp = sem("lam_ready"), sem("lam_exp")
        squared = sem("squared")
        scaled = sem("scaled")
        rstd_ready = sem("rstd_ready")
        turned = [sem(f"turned{n}") for n in range(4)]
        turned_out = [sem(f"turned_out{n}") for n in range(4)]
        in_done, c_copied, u_taken, b_taken = sem("in_done"), sem("c_copied"), sem("u_taken"), sem("b_taken")
        out_done = sem("out_done")
        mixed = sem("mixed")
        logits_done = sem("logits_done")
        hn_stored = [[sem(f"hn_stored{l}{b}") for b in range(2)] for l in range(2)]
        shifted, exped = sem("shifted"), sem("exped")
        members, ranked = sem("members"), sem("ranked")
        placed, more_known = sem("placed"), sem("more_known")
        hidden_ready, hidden_turned = sem("hidden_ready"), sem("hidden_turned")
        tabled, rows_ready = sem("tabled"), sem("rows_ready")
        gathered = [[sem(f"gathered{l}{b}") for b in range(2)] for l in range(2)]
        scattered = [[sem(f"scattered{l}{b}") for b in range(2)] for l in range(2)]
        index_set = [sem(f"index_set{l}") for l in range(2)]
        x_turned, xT_ready = sem("x_turned"), sem("xT_ready")
        silu_ready, hT_ready = sem("silu_ready"), sem("hT_ready")
        y_ready = sem("y_ready")
        more_steps = [sem(f"more_steps{l}") for l in range(2)]
        more_index = [sem(f"more_index{l}") for l in range(2)]
        more_gathered, more_w_landed = [sem(f"more_gathered{l}") for l in range(2)], [sem(f"more_w_landed{l}") for l in range(2)]
        more_turned, more_xT = [sem(f"more_turned{l}") for l in range(2)], [sem(f"more_xT{l}") for l in range(2)]
        more_up, more_silu = [sem(f"more_up{l}") for l in range(2)], [sem(f"more_silu{l}") for l in range(2)]
        more_rows = [sem(f"more_rows{l}") for l in range(2)]
        more_hot, more_tabled = [sem(f"more_hot{l}") for l in range(2)], [sem(f"more_tabled{l}") for l in range(2)]
        more_hidden, more_h_turned = [sem(f"more_hidden{l}") for l in range(2)], [sem(f"more_h_turned{l}") for l in range(2)]
        more_hT, more_down = [sem(f"more_hT{l}") for l in range(2)], [sem(f"more_down{l}") for l in range(2)]
        more_y, more_scattered = [sem(f"more_y{l}") for l in range(2)], [sem(f"more_scattered{l}") for l in range(2)]
        y_landed = [[sem(f"y_landed{l}{s}") for s in range(4)] for l in range(2)]
        combined = [sem(f"combined{l}") for l in range(2)]
        proj_done, proj_copied = sem("proj_done"), sem("proj_copied")
        roped, rot_turned, rot_copied = sem("roped"), sem("rot_turned"), sem("rot_copied")
        v_cleared, pads_clear, q_padded = sem("v_cleared"), sem("pads_clear"), sem("q_padded")
        scores_done, max_ready, exp_done = sem("scores_done"), sem("max_ready"), sem("exp_done")
        a_ready, a_turned, aT_copied, av_done = sem("a_ready"), sem("a_turned"), sem("aT_copied"), sem("av_done")
        o_copied, o_squared, o_ready = sem("o_copied"), sem("o_squared"), sem("o_ready")
        heads_meaned, heads_rooted = sem("heads_meaned"), sem("heads_rooted")
        o_turned, oT_copied = sem("o_turned"), sem("oT_copied")
        final_landed, final_ready = sem("final_landed"), sem("final_ready")
        stored = [sem(f"stored{b}") for b in range(2)]

        block = ctx.enter_context(nc.Block())

        N_PARAM = 17

        def tiles_of(layer):
            return NX + 1 if layer == 0 else NX

        JOBS = ([("k", f, t) for f in range(2) for t in range(NX + 1)]
                + [("v", f, t) for f in range(2) for t in range(NX + 1)]
                + [("q", f, t) for f in range(2) for t in range(NX)])
        ROT_JOBS = [p for p, j in enumerate(JOBS) if j[0] != "v"]
        STEPS = [(i, hh) for i in range(NX) for hh in range(NH)]

        def keys(i):
            return META + P * (i + 1)

        def score_view(n):
            i = STEPS[n][0]
            if i < NX - 1:
                return ps[:, 2 * (n % 2):2 * (n % 2) + 2, 0:keys(i)]
            return flat[:, 0:4 * W].rearrange("p (c n) -> p c n", c=2)[:, :, 0:keys(i)]

        def landed(eng, n):
            eng.wait_ge(ring_landed[n % RING], 16 * (n // RING + 1))

        def expert_unit(layer, q, u, part):
            n = U_MOE[layer] + 3 * u + ORDER[layer].index(part)
            return n % RING, 16 * (n // RING + 1) + 16 * q

        def bcast(ap, n, at):
            return ap.unsqueeze(at).to_broadcast([*ap.shape[:at], n, *ap.shape[at:]])

        def load_more(eng, layer):
            eng.wait_ge(more_known, layer + 1)
            return eng.value_load(n_more_i[0:1, 0:1], min_val=0, max_val=MAXMORE)

        @block.sync
        def _(sp):
            free_at = {}

            def unit(n, src, **k):
                if n >= RING:
                    sp.wait_ge(unit_used, free_at[n % RING])
                free_at[n % RING] = n + 1
                sp.dma_start(ring[:, n % RING, :].rearrange("p (k n) -> p k n", **k), src).then_inc(ring_landed[n % RING], 16)

            sp.dma_start(h[:, 0, :], x[0, 0:P, :]).then_inc(x_landed[0], 16)
            sp.dma_start(const[:, :], table).then_inc(const_landed, 16)
            sp.dma_start(gain[:, 0, :], a_norm[0].rearrange("(p k) -> p k", k=KC)).then_inc(const_landed, 16)
            for t in range(1, NX):
                sp.dma_start(h[:, t, :], x[0, t * P:(t + 1) * P, :]).then_inc(x_landed[t], 16)
            sp.dma_start(h[0:META, NX, :], meta_tokens).then_inc(x_landed[NX], 16)

            w_in = a_w_in[0].rearrange("(p k) n -> p k n", k=KC)
            for f in range(2):
                for s, part in enumerate((1, 2, 0)):
                    unit(U_IN + 3 * f + s, w_in[:, :, part * D + f * W:part * D + (f + 1) * W], k=KC)
            w_o = a_w_out[0].rearrange("(k p) n -> p k n", p=P)
            for f in range(2):
                unit(U_AOUT + f, w_o[:, :, f * W:(f + 1) * W], k=KC)

            def expert_load(layer, part, ex, dst, landing):
                w = {"gate": e_gate, "up": e_up, "down": e_down}[part][layer, ex].rearrange("o a b -> (o a) b")
                if part == "down":
                    sp.dma_start(dst.rearrange("p (k n) -> p k n", k=FC), w.rearrange("(f p) n -> p f n", p=P)).then_inc(landing, 16)
                else:
                    sp.dma_start(dst.rearrange("p (a m) -> p a m", a=2),
                                 w.rearrange("(a p c) n -> p a (c n)", a=2, c=KC // 2)).then_inc(landing, 16)

            def experts(layer):
                done = {"gate": 2, "up": 2, "down": 3}

                def pair(q, first):
                    for u in range(2):
                        for part in ORDER[layer] if first else ("gate", "up", "down"):
                            n = U_MOE[layer] + 3 * u + ORDER[layer].index(part)
                            if first:
                                sp.wait_ge(unit_used, free_at[n % RING])
                            else:
                                sp.wait_ge(unit_used, q * 6 + (U_MOE[layer] - 6 + 3 * u + done[part]))
                            expert_load(layer, part, bass.ds(q * 2 + u, 1), ring[:, n % RING, :], ring_landed[n % RING])
                            free_at[n % RING] = U_MOE[layer] + 3 * (E - 2 + u) + done[part]

                pair(0, True)
                with sp.Fori(1, PAIRS) as q:
                    pair(q, False)
                more = load_more(sp, layer)
                with sp.If(more > 0):
                    sp.wait_ge(more_steps[layer], MORE_STEPS)
                    with sp.Fori(0, more) as b:
                        ex = sp.value_load(more_i[0:1, 1, bass.ds(b, 1)], min_val=0, max_val=E - 1)
                        sp.wait_ge(more_down[layer], b + 1)
                        for j, part in enumerate(ORDER[1]):
                            expert_load(layer, part, bass.ds(ex, 1), more_w[:, j, :], more_w_landed[layer])
                sp.nop()

            experts(0)
            wkv = w_kv.rearrange("(p k) n -> p k n", k=KC)
            for f in range(4):
                unit(U_KV + f, wkv[:, :, f * W:(f + 1) * W], k=KC)
            wq = b_w_q[0].rearrange("(p k) n -> p k n", k=KC)
            for f in range(2):
                unit(U_Q + f, wq[:, :, f * W:(f + 1) * W], k=KC)
            wo = b_w_out[0].rearrange("(k p) n -> p k n", p=P)
            for f in range(2):
                unit(U_BOUT + f, wo[:, :, f * W:(f + 1) * W], k=KC)
            experts(1)
            sp.wait_ge(o_ready, NX)
            sp.dma_start(final_gain, final_norm.partition_broadcast(P)).then_inc(final_landed, 16)
            for t in range(NX):
                sp.wait_ge(final_ready, t + 1)
                sp.dma_start(out[0, t * P:(t + 1) * P, :], nat[:, t % 2, :]).then_inc(stored[t % 2], 16)
            for b in range(2):
                sp.wait_ge(stored[b], 16 * NX // 2)

        @block.gpsimd
        def _(pool):
            def alone():
                pool.sem_inc(passed, 1)

            pool.wait_ge(param_landed, 16 * N_PARAM)
            for l in range(2):
                a = l * KC * (G + E)
                nc.gpsimd.tensor_copy(wr[:, l, :, 0:G], stage[:, a:a + KC * G].rearrange("p (k n) -> p k n", k=KC)).then_inc(params_ready, 1)
                nc.gpsimd.tensor_copy(wr[:, l, :, G:], stage[:, a + KC * G:a + KC * (G + E)].rearrange("p (k n) -> p k n", k=KC)).then_inc(params_ready, 1)

            def root_heads(i):
                pool.wait_ge(heads_meaned, i + 1)
                nc.gpsimd.tensor_tensor(small[:, 32:40], small[:, 24:32], cst("minus_half"), ALU.pow).then_inc(heads_rooted, 1)
                pool.wait_ge(heads_rooted, i + 1)

            def moe(layer):
                nt = tiles_of(layer)
                for t in range(nt):
                    pool.wait_ge(scaled, 5 * (1 + 2 * layer) + t + 1)
                    pool.dma_start(hn_dram[layer][t * P:t * P + rows(t), :], nat[0:rows(t), t % 2, :]).then_inc(hn_stored[layer][t % 2], 16)
                for b in range(2):
                    pool.wait_ge(hn_stored[layer][b], 16 * ((nt + 1 - b) // 2))
                pool.wait_ge(rows_ready, 2 * (layer + 1))

                def gather(b, column, n):
                    nc.gpsimd.tensor_copy(src_now[:, b:b + 1], src_row[:, bass.ds(column, 1)]).then_inc(index_set[layer], 1)
                    pool.wait_ge(index_set[layer], n + 1)
                    alone()
                    pool.indirect_dma_start(nat[:, b, 0:DH], None, hn_halves[layer], bass.IndirectOffsetOnAxis(src_now[:, b:b + 1], 0),
                                            bounds_check=2 * (LEN, SEQ)[layer] - 1, oob_is_err=False).then_inc(gathered[layer][b], 16)

                def pair(q, first, last):
                    for u in range(2):
                        n = q * 4 + 2 + 2 * u if not last else q * 4 + 2 + u
                        pool.wait_ge(y_ready, E * layer + q * 2 + u + 1)
                        if not first:
                            pool.wait_ge(scattered[layer][u], q * 16)
                        nc.gpsimd.tensor_copy(dst_now[:, u:u + 1], dst_row[:, bass.ds(q * 2 + u, 1)]).then_inc(index_set[layer], 1)
                        pool.wait_ge(index_set[layer], n + 1)
                        alone()
                        pool.indirect_dma_start(y_halves[layer], bass.IndirectOffsetOnAxis(dst_now[:, u:u + 1], 0), y_out[:, u, :], None,
                                                bounds_check=4 * SPREAD - 1, oob_is_err=False).then_inc(scattered[layer][u], 16)
                        if not last:
                            pool.wait_ge(x_turned, E * layer + q * 2 + u + 1)
                            gather(u, q * 2 + u + 2, n + 1)

                gather(0, 0, 0)
                gather(1, 1, 1)
                pair(0, True, False)
                with pool.Fori(1, PAIRS - 1) as q:
                    pair(q, False, False)
                pair(PAIRS - 1, False, True)
                for b in range(2):
                    pool.wait_ge(scattered[layer][b], 16 * PAIRS)

                more = load_more(pool, layer)
                with pool.If(more > 0):
                    pool.wait_ge(more_steps[layer], MORE_STEPS)
                    pool.wait_ge(more_rows[layer], 2)
                    with pool.Fori(0, more) as b:
                        column = pool.value_load(more_i[0:1, 0, bass.ds(b, 1)], min_val=0, max_val=(NBLK - 1) * E - 1)
                        nc.gpsimd.tensor_copy(src_now[:, 0:1], src_more[:, bass.ds(column, 1)]).then_inc(more_index[layer], 1)
                        nc.gpsimd.tensor_copy(dst_now[:, 0:1], dst_more[:, bass.ds(column, 1)]).then_inc(more_index[layer], 1)
                        pool.wait_ge(more_index[layer], b * 2 + 2)
                        alone()
                        pool.indirect_dma_start(nat[:, 0, 0:DH], None, hn_halves[layer], bass.IndirectOffsetOnAxis(src_now[:, 0:1], 0),
                                                bounds_check=2 * (LEN, SEQ)[layer] - 1, oob_is_err=False).then_inc(more_gathered[layer], 16)
                        pool.wait_ge(more_y[layer], b + 1)
                        alone()
                        pool.indirect_dma_start(y_halves[layer], bass.IndirectOffsetOnAxis(dst_now[:, 0:1], 0), y_out[:, 0, :], None,
                                                bounds_check=4 * SPREAD - 1, oob_is_err=False).then_inc(more_scattered[layer], 16)
                        pool.wait_ge(more_scattered[layer], b * 16 + 16)
                pool.nop()
                for t in range(nt):
                    if t >= 4:
                        pool.wait_ge(combined[layer], t - 3)
                    for k in range(2):
                        pool.dma_start(y_in[0:rows(t), t % 4, k, :], y_dram[layer][k * SPREAD + t * P:k * SPREAD + t * P + rows(t), :]
                                       ).then_inc(y_landed[layer][t % 4], 16)

            moe(0)
            nc.gpsimd.memset(V[:, NX, :], 0.0).then_inc(v_cleared, 1)
            pool.wait_ge(proj_done, len(JOBS))
            nc.gpsimd.memset(metaT, 0.0).then_inc(pads_clear, 1)
            nc.gpsimd.memset(q_pad, 0.0).then_inc(pads_clear, 1)
            pool.wait_ge(pads_clear, 2)
            pool.wait_ge(rot_copied, len(ROT_JOBS))
            for n, (i, hh) in enumerate(STEPS):
                if n >= 2:
                    pool.wait_ge(scores_done, 2 * (n - 1))
                for c in range(2):
                    nc.gpsimd.tensor_copy(q_pad[c * HD:(c + 1) * HD, n % 2, c, :], actT[c * HD:(c + 1) * HD, hh, i * P:(i + 1) * P]
                                          ).then_inc(q_padded, 1)
                if n >= NH and n % NH == 5:
                    pool.wait_ge(q_padded, 2 * n + 2)
                    root_heads(n // NH - 1)
            pool.wait_ge(q_padded, 2 * len(STEPS))
            root_heads(NX - 1)
            moe(1)

        @block.scalar
        def _(act):
            step = Tally(act, act_step)
            for i, g in enumerate((ffn_norm[0], kv_norm, ffn_norm[1], b_norm[0])):
                act.dma_start(gain[:, 1 + i, :], g.rearrange("(p k) -> p k", k=KC)).then_inc(param_landed, 16)
            for l in range(2):
                act.dma_start(block_gain[:, l, :].rearrange("p (a c) -> p a c", a=2),
                              ffn_norm[l].rearrange("(a p c) -> p a c", a=2, c=KC // 2)).then_inc(param_landed, 16)
            for l in range(2):
                a = l * KC * (G + E)
                act.dma_start(stage[:, a:a + KC * G], r_group[l].rearrange("(p k) n -> p (k n)", k=KC)).then_inc(param_landed, 16)
                act.dma_start(stage[:, a + KC * G:a + KC * (G + E)], r_expert[l].rearrange("(p k) n -> p (k n)", k=KC)).then_inc(param_landed, 16)
                act.dma_start(rbias[:, l, 0:G], r_group_b[l].partition_broadcast(P)).then_inc(param_landed, 16)
                act.dma_start(rbias[:, l, G:], r_expert_b[l].partition_broadcast(P)).then_inc(param_landed, 16)
            act.dma_start(stage_conv, a_conv[0].rearrange("w (j p) -> (w j) p", p=P)).then_inc(param_landed, 16)
            act.dma_start(subln[:, :], b_subln[0].rearrange("(p o) -> p o", o=1)).then_inc(param_landed, 16)
            act.dma_start(stage_lam, b_lambda[0].rearrange("a b -> (a b)").partition_broadcast(P)).then_inc(param_landed, 16)

            def root_mean_square(phase, t):
                r = rows(t)
                step.order(nc.scalar.activation(nat[0:r, t % 2, :], h[0:r, t, :], ACT.Square, scale=1.0 / math.sqrt(D),
                                                accum_out=ssq[0:r, t:t + 1]))
                nc.scalar.activation(ssq[0:r, t:t + 1], ssq[0:r, t:t + 1], ACT.Sqrt, bias=cst("eps", r)).then_inc(squared, 1)

            def norm_tile(phase, t):
                r = rows(t)
                if t >= 2:
                    act.wait_ge(turned[phase], t - 1)
                    if phase in (1, 3):
                        act.wait_ge(hn_stored[(phase - 1) // 2][t % 2], 16 * (t // 2))
                root_mean_square(phase, t)
                act.wait_ge(rstd_ready, 5 * phase + t + 1)
                nc.scalar.activation(nat[0:r, t % 2, :], h[0:r, t, :], ACT.Copy, scale=rstd[0:r, t:t + 1]).then_inc(scaled, 1)

            act.wait_ge(const_landed, 32)
            for t in range(NX + 1):
                act.wait_ge(x_landed[t], 16)
                norm_tile(0, t)

            for j in range(KC):
                act.wait_ge(in_done, 3 * j + 1)
                if j >= 2:
                    act.wait_ge(u_taken, j - 1)
                g = 2 * ((3 * j) % 4)
                nc.scalar.copy(c_gate[:, j % 2, :].rearrange("p (a n) -> p a n", a=2), ps[:, g:g + 2, 0:HALF]).then_inc(c_copied, 1)

            def moe(layer):
                for t in range(tiles_of(layer)):
                    act.wait_ge(mixed, (NX + 1) * layer + t + 1)
                    norm_tile(1 + 2 * layer, t)
                for k in range(2):
                    act.wait_ge(shifted, 2 * layer + k + 1)
                    e_view = (cand[:, 0:tiles_of(layer), 0:G], rv[:, 3, 0:tiles_of(layer)])[k]
                    nc.scalar.activation(e_view, e_view, ACT.Exp).then_inc(exped, 1)

                def pair(q, first):
                    for u in range(2):
                        base = U_MOE[layer] + 3 * u
                        act.wait_ge(unit_used, q * 6 + base + 2)
                        nc.scalar.activation(silu[:, u, :], ps[:, 2 + u, 0:FE // 2], ACT.Silu).then_inc(silu_ready, 1)
                        act.wait_ge(hidden_turned, E * layer + q * 2 + u + 1)
                        nc.scalar.copy(hT[:, u, :], ps[:, 4 + u, 0:FE // 2]).then_inc(hT_ready, 1)
                        act.wait_ge(unit_used, q * 6 + base + 3)
                        if not first:
                            act.wait_ge(scattered[layer][u], q * 16)
                        nc.scalar.copy(y_out[:, u, :], ps[:, 6 + u, :]).then_inc(y_ready, 1)

                pair(0, True)
                with act.Fori(1, PAIRS) as q:
                    pair(q, False)
                more = load_more(act, layer)
                with act.If(more > 0):
                    act.wait_ge(scattered[layer][0], 16 * PAIRS)
                    with act.Fori(0, more) as b:
                        act.wait_ge(more_up[layer], b + 1)
                        nc.scalar.activation(silu[:, 0, :], ps[:, 2, 0:FE // 2], ACT.Silu).then_inc(more_silu[layer], 1)
                        act.wait_ge(more_h_turned[layer], b + 1)
                        nc.scalar.copy(hT[:, 0, :], ps[:, 4, 0:FE // 2]).then_inc(more_hT[layer], 1)
                        act.wait_ge(more_down[layer], b + 2)
                        nc.scalar.copy(y_out[:, 0, :], ps[:, 6, :]).then_inc(more_y[layer], 1)
                act.nop()

            moe(0)
            for t in range(NX + 1):
                act.wait_ge(combined[0], t + 1)
                norm_tile(2, t)
                if t == 0:
                    act.wait_ge(lam_ready, 1)
                    nc.scalar.activation(lam[:, 2:4], lam[:, 0:2], ACT.Exp).then_inc(lam_exp, 1)
            for p, (kind, f, t) in enumerate(JOBS):
                r = rows(t)
                act.wait_ge(proj_done, p + 1)
                if kind == "v":
                    if f == 0 and t == NX:
                        act.wait_ge(v_cleared, 1)
                    dst = V[0:r, t, f * W:(f + 1) * W]
                else:
                    n = ROT_JOBS.index(p)
                    if n >= 2:
                        act.wait_ge(rot_turned, n - 1)
                    dst = knat[0:r, n % 2, :]
                nc.scalar.copy(dst, ps[0:r, 4 + p % 4, :]).then_inc(proj_copied, 1)

            def copy_aT(n):
                i = STEPS[n][0]
                act.wait_ge(a_turned, n + 1)
                if n >= 2:
                    act.wait_ge(av_done, n - 1)
                else:
                    act.wait_ge(pads_clear, 2)
                nc.scalar.copy(probT[n % 2][:, 0:(i + 1) * P], flat[:, 4 * W:4 * W + (i + 1) * P]).then_inc(aT_copied, 1)
                nc.scalar.copy(metaT[0:META, n % 2, :], flat[0:META, 5 * W:5 * W + P]).then_inc(aT_copied, 1)

            def copy_o(i):
                act.wait_ge(av_done, NH * (i + 1))
                if i >= 2:
                    act.wait_ge(o_turned, i - 1)
                nc.scalar.copy(nat[:, i % 2, :], flat[:, 6 * W:8 * W]).then_inc(o_copied, 1)
                act.wait_ge(o_copied, i + 1)
                if i == 0:
                    act.wait_ge(rot_turned, len(ROT_JOBS))
                if i >= 1:
                    act.wait_ge(o_ready, i)
                nc.scalar.activation(square, nat[:, i % 2, :], ACT.Square).then_inc(o_squared, 1)

            for n, (i, hh) in enumerate(STEPS):
                if n >= NH and n % NH == 3:
                    copy_o(n // NH - 1)
                if n >= 3:
                    act.wait_ge(a_turned, n - 2)
                s = score_view(n)
                for c in range(2):
                    act.wait_ge(max_ready, 2 * n + c + 1)
                    nc.scalar.activation(prob[:, n % 3, c, 0:keys(i)], s[:, c, :], ACT.Exp, bias=small[:, 4 + 2 * (n % 2) + c:5 + 2 * (n % 2) + c],
                                         scale=HD ** -0.5, accum_out=small[:, 48 + 2 * (n % 3) + c:49 + 2 * (n % 3) + c]).then_inc(exp_done, 1)
                if n >= 2:
                    copy_aT(n - 2)
            for n in range(len(STEPS) - 2, len(STEPS)):
                copy_aT(n)
            copy_o(NX - 1)

            moe(1)
            for t in range(NX):
                act.wait_ge(combined[1], t + 1)
                if t >= 2:
                    act.wait_ge(stored[t % 2], 16 * (t // 2))
                root_mean_square(4, t)

        @block.tensor
        def _(pe):
            mm = nc.tensor.matmul

            def turn(phase, t, free):
                r = rows(t)
                pe.wait_ge(scaled, 5 * phase + t + 1)
                if t >= 1:
                    pe.wait_ge(turned_out[phase], free(t))
                for k in range(KC):
                    last = nc.tensor.transpose(flat[:, k * P:k * P + r], nat[0:r, t % 2, k:D:KC], ident[0:r, 0:r])
                last.then_inc(turned[phase], 1)

            pe.wait_ge(const_landed, 32)
            for t in range(NX + 1):
                turn(0, t, lambda t: t)
            pe.wait_ge(param_landed, 16 * N_PARAM)
            nc.tensor.transpose(ps[:, 2, 0:3 * KC], stage_conv, ident[0:3 * KC, 0:3 * KC]).then_inc(conv_turned, 1)
            pe.wait_ge(turned_out[0], NX + 1)
            pe.wait_ge(conv_ready, 1)

            for j in range(KC):
                for s in range(3):
                    g = 3 * j + s
                    n = U_IN + 3 * (j // 4) + s
                    if j % 4 == 0:
                        landed(pe, n)
                    if g >= 4:
                        jj, ss = divmod(g - 4, 3)
                        pe.wait_ge((c_copied, u_taken, b_taken)[ss], jj + 1)
                    b = 2 * (g % 4)
                    w = ring[:, n % RING, :].rearrange("p (k n) -> p k n", k=KC)
                    for k in range(KC):
                        for a in range(2):
                            last = mm(ps[:, b + a, 0:HALF], w[:, k, (j % 4) * P:(j % 4 + 1) * P], actT[:, k, a * HALF:(a + 1) * HALF],
                                      start=(k == 0), stop=(k == KC - 1))
                    last.then_inc(in_done, 1)
                    if j % 4 == 3:
                        pe.wait_ge(in_done, g + 1)
                        pe.sem_inc(unit_used, 1)

            def out_proj(layer, t, src, col0):
                r, n = rows(t), (U_AOUT, U_BOUT)[layer]
                if t == 0:
                    if layer == 0:
                        pe.wait_ge(b_taken, KC)
                    landed(pe, n)
                    landed(pe, n + 1)
                if t >= 2:
                    pe.wait_ge(mixed, (NX + 1) * layer + t - 1)
                b = 4 + 2 * (t % 2)
                for f in range(2):
                    w = ring[:, (n + f) % RING, :].rearrange("p (k n) -> p k n", k=KC)
                    for k in range(KC):
                        last = mm(ps[0:r, b + f, :], src[:, k, col0:col0 + r], w[:, k, :], start=(k == 0), stop=(k == KC - 1))
                last.then_inc(out_done, 1)

            def logits(layer, t):
                r = rows(t)
                pe.wait_ge(turned_out[1 + 2 * layer], t + 1)
                a = cols(t)[0]
                for k in range(KC):
                    last = mm(ps[0:r, 2, t * (G + E):(t + 1) * (G + E)], actT[:, k, a:a + r], wr[:, layer, k, :],
                              start=(k == 0), stop=(k == KC - 1))
                last.then_inc(logits_done, 1)

            def gate_up(b, pair_w):
                for k in range(KC):
                    a, c = divmod(k, KC // 2)
                    x = xT[:, b, (2 * c + a) * C:(2 * c + a + 1) * C]
                    for f in range(2):
                        w = pair_w[:, :, k * FE + f * FE // 2:k * FE + (f + 1) * FE // 2]
                        last = mm(ps[f * C:(f + 1) * C, 2 + b, :].rearrange("p (g n) -> p g n", g=2), x, w, start=(k == 0), stop=(k == KC - 1))
                return last

            def turn_block(b):
                pe.sem_inc(passed, 1)
                for c in range(KC // 2):
                    last = nc.tensor.transpose(ps[:, b, c * P:(c + 1) * P], nat[:, b, c:DH:KC // 2], ident)
                return last

            def turn_hidden(b):
                pe.sem_inc(passed, 1)
                for c in range(2):
                    last = nc.tensor.transpose(ps[:, 4 + b, c * P:(c + 1) * P], hidden[:, b, c * P:(c + 1) * P], ident)
                return last

            def down(b, w):
                for f in range(FC):
                    a, c = divmod(f, 2)
                    for o in range(2):
                        last = mm(ps[o * C:(o + 1) * C, 6 + b, :], hT[:, b, (2 * c + a) * C:(2 * c + a + 1) * C],
                                  w[:, f * D + o * DH:f * D + (o + 1) * DH], start=(f == 0), stop=(f == FC - 1))
                return last

            def table_rows(column, nt):
                for n in range(2 * nt):
                    for f in range(2):
                        last = mm(ps[f * C:(f + 1) * C, 2, column:column + E], at_slot[:, n, :], row_of[:, n, :],
                                  start=(n == 0), stop=(n == 2 * nt - 1))
                return last

            def moe(layer, src, col):
                nt = tiles_of(layer)
                ph = 1 + 2 * layer
                for t in range(nt):
                    out_proj(layer, t, src, col(t))
                    if t == nt - 1:
                        pe.wait_ge(out_done, (NX + 1) * layer + nt)
                        pe.sem_inc(unit_used, 2)
                    if t == 0:
                        pe.wait_ge(params_ready, 4)
                    if t >= 1:
                        turn(ph, t - 1, lambda t: t)
                    if t >= 2:
                        logits(layer, t - 2)
                turn(ph, nt - 1, lambda t: t)
                logits(layer, nt - 2)
                logits(layer, nt - 1)

                pe.wait_ge(members, layer + 1)
                span = (nt + 1) * E
                mm(ps[:, 3, 0:span], cst("upper"), member[:, 0:nt + 1, :].rearrange("p t e -> p (t e)"), start=True, stop=False)
                mm(ps[:, 3, 0:span], cst("ones"), before[:, 0:nt + 1, :].rearrange("p t e -> p (t e)"), start=False, stop=True
                   ).then_inc(ranked, 1)
                pe.wait_ge(placed, layer + 1)
                table_rows(0, nt).then_inc(tabled, 1)

                def pair(q, first, last_pair):
                    for u in range(2):
                        (gs, gv), (us, uv), (ds, dv) = (expert_unit(layer, q, u, part) for part in ("gate", "up", "down"))
                        pe.wait_ge(ring_landed[gs], gv)
                        pe.wait_ge(ring_landed[us], uv)
                        pe.wait_ge(xT_ready, E * layer + q * 2 + u + 1)
                        gate_up(u, ring[:, gs:us + 1, :]).then_inc(unit_used, 2)
                        if not (last_pair and u == 1):
                            pe.wait_ge(gathered[layer][1 - u], q * 16 + 16 * (1 + u))
                            turn_block(1 - u).then_inc(x_turned, 1)
                        pe.wait_ge(hidden_ready, E * layer + q * 2 + u + 1)
                        turn_hidden(u).then_inc(hidden_turned, 1)
                        pe.wait_ge(ring_landed[ds], dv)
                        if not first:
                            pe.wait_ge(y_ready, E * layer + q * 2 + u - 1)
                        pe.wait_ge(hT_ready, E * layer + q * 2 + u + 1)
                        down(u, ring[:, ds, :]).then_inc(unit_used, 1)

                pe.wait_ge(gathered[layer][0], 16)
                turn_block(0).then_inc(x_turned, 1)
                pair(0, True, False)
                with pe.Fori(1, PAIRS - 1) as q:
                    pair(q, False, False)
                pair(PAIRS - 1, False, True)

                more = load_more(pe, layer)
                with pe.If(more > 0):
                    pe.wait_ge(y_ready, E * layer + E)
                    pe.sem_inc(more_down[layer], 1)
                    for b in range(1, NBLK):
                        pe.wait_ge(more_hot[layer], b)
                        table_rows((b - 1) * E, nt).then_inc(more_tabled[layer], 1)
                    with pe.Fori(0, more) as b:
                        pe.wait_ge(more_gathered[layer], b * 16 + 16)
                        turn_block(0).then_inc(more_turned[layer], 1)
                        pe.wait_ge(more_xT[layer], b + 1)
                        pe.wait_ge(more_w_landed[layer], b * 48 + 48)
                        gate_up(0, more_w[:, 0:2, :]).then_inc(more_up[layer], 1)
                        pe.wait_ge(more_hidden[layer], b + 1)
                        turn_hidden(0).then_inc(more_h_turned[layer], 1)
                        pe.wait_ge(more_hT[layer], b + 1)
                        down(0, more_w[:, 2, :]).then_inc(more_down[layer], 1)
                pe.nop()

            moe(0, actT2, lambda t: cols(t)[0])

            def project(p):
                kind, f, t = JOBS[p]
                r = rows(t)
                n = {"k": U_KV, "v": U_KV + 2, "q": U_Q}[kind] + f
                src, a = (actT2, t * P) if kind == "q" else (actT, cols(t)[0])
                if t == 0:
                    landed(pe, n)
                if p >= 4:
                    pe.wait_ge(proj_copied, p - 3)
                if kind == "k" and f == 0:
                    pe.wait_ge(turned_out[2], min(2 * t + 2, 2 * NX + 1))
                w = ring[:, n % RING, :].rearrange("p (k n) -> p k n", k=KC)
                for k in range(KC):
                    last = mm(ps[0:r, 4 + p % 4, :], src[:, k, a:a + r], w[:, k, :], start=(k == 0), stop=(k == KC - 1))
                last.then_inc(proj_done, 1)
                if t == (NX - 1 if kind == "q" else NX):
                    pe.wait_ge(proj_done, p + 1)
                    pe.sem_inc(unit_used, 1)

            def turn_rot(n):
                _, f, t = JOBS[ROT_JOBS[n]]
                r = rows(t)
                pe.wait_ge(roped, n + 1)
                if n >= 2:
                    pe.wait_ge(rot_copied, n - 1)
                for c in range(4):
                    last = nc.tensor.transpose(ps[:, 2 + n % 2, c * P:c * P + r], knat[0:r, n % 2, c * P:(c + 1) * P], ident[0:r, 0:r])
                last.then_inc(rot_turned, 1)

            turn(2, 0, None)
            turn(2, 1, lambda t: 2 * t)
            nrot = 0
            for p in range(len(JOBS)):
                project(p)
                if p + 2 <= NX:
                    turn(2, p + 2, lambda t: 2 * t)
                while p >= NX - 1 and nrot < len(ROT_JOBS) and ROT_JOBS[nrot] <= p - 1:
                    turn_rot(nrot)
                    nrot += 1
            while nrot < len(ROT_JOBS):
                turn_rot(nrot)
                nrot += 1

            def scores(n):
                i, hh = STEPS[n]
                s = score_view(n)
                pe.wait_ge(q_padded, 2 * n + 2)
                for c in range(2):
                    if i == NX - 1:
                        pe.wait_ge(exp_done, 2 * n - 1 + c)
                    elif n >= 2 and c == 0:
                        pe.wait_ge(exp_done, 2 * (n - 1))
                    q = q_pad[:, n % 2, c, :]
                    for a in range(0, keys(i), W):
                        b = min(a + W, keys(i))
                        last = mm(s[:, c, a:b], q, kT[:, hh, a:b], start=True, stop=True)
                    last.then_inc(scores_done, 1)

            def turn_a(n):
                i = STEPS[n][0]
                pe.wait_ge(a_ready, n + 1)
                if n >= 1:
                    pe.wait_ge(aT_copied, 2 * n)
                for j in range(i + 1):
                    nc.tensor.transpose(flat[:, 4 * W + j * P:4 * W + (j + 1) * P], prob[:, n % 3, 0, META + j * P:META + (j + 1) * P], ident)
                nc.tensor.transpose(ps[:, 5, 0:P], prob[:, n % 3, 0, 0:P], ident).then_inc(a_turned, 1)

            def weigh(n):
                i, hh = STEPS[n]
                pe.wait_ge(aT_copied, 2 * n + 2)
                if hh == 0 and i >= 1:
                    pe.wait_ge(o_copied, i)
                o = flat[:, 6 * W + hh * P:6 * W + (hh + 1) * P]
                mm(o, metaT[:, n % 2, :], V[:, NX, hh * P:(hh + 1) * P], start=True, stop=False)
                for j in range(i + 1):
                    last = mm(o, probT[n % 2][:, j * P:(j + 1) * P], V[:, j, hh * P:(hh + 1) * P], start=False, stop=(j == i))
                last.then_inc(av_done, 1)

            def turn_o(i):
                pe.wait_ge(o_ready, i + 1)
                for k in range(KC):
                    last = nc.tensor.transpose(flat[:, 4 * W + k * P:4 * W + (k + 1) * P], nat[:, i % 2, k * P:(k + 1) * P], ident)
                last.then_inc(o_turned, 1)

            pe.wait_ge(rot_copied, len(ROT_JOBS))
            pe.wait_ge(proj_copied, len(JOBS))
            last_n = len(STEPS) - 1
            for n in range(len(STEPS) + 3):
                if n <= last_n:
                    scores(n)
                if NH <= n <= last_n and n % NH == 7:
                    pe.wait_ge(aT_copied, 2 * (n - 2))
                    turn_o(n // NH - 1)
                    pe.wait_ge(oT_copied, n // NH)
                if 2 <= n <= last_n + 2:
                    turn_a(n - 2)
                if n >= 3:
                    weigh(n - 3)
            turn_o(NX - 1)
            pe.wait_ge(oT_copied, NX)
            pe.wait_ge(o_copied, NX)
            moe(1, actT, lambda t: t * P)

        @block.vector
        def _(dve):
            v = nc.vector
            step = Tally(dve, dve_step)
            order = step.order

            def rstd_tile(phase, t):
                r = rows(t)
                dve.wait_ge(squared, 5 * phase + t + 1)
                v.reciprocal(rstd[0:r, t:t + 1], ssq[0:r, t:t + 1]).then_inc(rstd_ready, 1)

            def gained(dst, t, g):
                r = rows(t)
                return v.tensor_tensor(dst, flat[:, 0:KC * P].rearrange("p (k n) -> p k n", k=KC)[:, :, 0:r],
                                       bcast(gain[:, g, :], r, 2), ALU.mult)

            dve.wait_ge(const_landed, 32)
            for t in range(NX + 1):
                rstd_tile(0, t)
                dve.wait_ge(turned[0], t + 1)
                gained(actT[:, :, cols(t)[0]:cols(t)[1]], t, 0).then_inc(turned_out[0], 1)
            dve.wait_ge(conv_turned, 1)
            v.tensor_copy(conv[:, :], ps[:, 2, 0:3 * KC]).then_inc(conv_ready, 1)
            dve.wait_ge(param_landed, 16 * N_PARAM)
            lp = stage_lam.rearrange("p (a b d) -> p a b d", a=2, b=2)
            order(v.tensor_tensor(lp[:, :, 0, :], lp[:, :, 0, :], lp[:, :, 1, :], ALU.mult))
            v.tensor_reduce(lam[:, 0:2], lp[:, :, 0, :], AX, ALU.add).then_inc(lam_ready, 1)
            order(v.tensor_scalar(subln[:, :], subln[:, :], 1.0 - LAM_INIT, None, ALU.mult))

            order(v.memset(cu[:, 0:2], 0.0))
            dve.wait_ge(conv_ready, 1)
            halves = lambda ap: ap.rearrange("p (a n) -> p a n", a=2)
            for j in range(KC):
                g = 3 * j + 1
                b = 2 * (g % 4)
                dve.wait_ge(c_copied, j + 1)
                dve.wait_ge(in_done, g + 1)
                v.tensor_tensor(halves(cu[:, 2:]), halves(c_gate[:, j % 2, :]), ps[:, b:b + 2, 0:HALF], ALU.mult).then_inc(u_taken, 1)
                dve.wait_ge(u_taken, j + 1)
                order(v.tensor_scalar(z, cu[:, 0:LEN], conv[:, j:j + 1], None, ALU.mult))
                for k in (1, 2):
                    order(v.scalar_tensor_tensor(z, cu[:, k:k + LEN], conv[:, k * KC + j:k * KC + j + 1], z, ALU.mult, ALU.add))
                b = 2 * ((g + 1) % 4)
                dve.wait_ge(in_done, g + 2)
                v.tensor_tensor(halves(actT2[:, j, :]), halves(z), ps[:, b:b + 2, 0:HALF], ALU.mult).then_inc(b_taken, 1)
                dve.wait_ge(b_taken, j + 1)

            def first_max(vals, n, width, top, index, onehot):
                tmp = work[:, 0:n, 0:width]
                iota = bcast(cst("iota")[:, 0:width], n, 1)
                order(v.tensor_reduce(top, vals, AX, ALU.max))
                order(v.tensor_tensor(tmp, vals, bcast(top, width, 2), ALU.is_equal))
                order(v.scalar_tensor_tensor(tmp, tmp, -100.0, bcast(cst("iota100")[:, 0:width], n, 1), ALU.mult, ALU.add))
                order(v.tensor_reduce(index, tmp, AX, ALU.min))
                order(v.tensor_tensor(onehot, iota, bcast(index, width, 2), ALU.is_equal))

            def moe(layer):
                nt = tiles_of(layer)
                ph = 1 + 2 * layer

                def add_tile(t):
                    r, b = rows(t), 4 + 2 * (t % 2)
                    dve.wait_ge(out_done, (NX + 1) * layer + t + 1)
                    v.tensor_tensor(h[0:r, t, :], h[0:r, t, :], flat[0:r, b * W:(b + 2) * W], ALU.add).then_inc(mixed, 1)

                def norm_rest(t):
                    rstd_tile(ph, t)
                    dve.wait_ge(turned[ph], t + 1)
                    gained(actT[:, :, cols(t)[0]:cols(t)[1]], t, ph).then_inc(turned_out[ph], 1)

                for t in range(nt):
                    add_tile(t)
                    norm_rest(t)

                dve.wait_ge(logits_done, (NX + 1) * layer + nt)
                lg = ps[:, 2, 0:nt * (G + E)].rearrange("p (t n) -> p t n", t=nt)
                if nt > NX:
                    order(v.memset(logit[:, NX, :], 0.0))
                    v.tensor_tensor(logit[0:META, NX, :], lg[0:META, NX, :], rbias[0:META, layer, :], ALU.add).then_inc(dve_step, 1)
                    step.n += 1
                order(v.tensor_tensor(logit[:, 0:NX, :], lg[:, 0:NX, :], bcast(rbias[:, layer, :], NX, 1), ALU.add))
                L = logit[:, 0:nt, :]
                gtop, gidx, psum_g, e1 = rv[:, 0, 0:nt], rv[:, 1, 0:nt], rv[:, 2, 0:nt], rv[:, 3, 0:nt]
                v0, v1, i0, i1, pg = (rv[:, c, 0:nt] for c in range(4, 9))
                ghot = hot[:, 0, 0:nt, 0:G]
                first_max(L[:, :, 0:G], nt, G, gtop, gidx, ghot)
                ex = cand[:, 0:nt, 0:G]
                v.tensor_tensor(ex, L[:, :, 0:G], bcast(gtop, G, 2), ALU.subtract).then_inc(shifted, 1)
                prod = work[:, 0:nt, :]
                order(v.tensor_tensor(prod.rearrange("p t (g e) -> p t g e", g=G), L[:, :, G:].rearrange("p t (g e) -> p t g e", g=G),
                                      bcast(ghot, EPG, 3), ALU.mult))
                sel = leg[:, 0:nt, :]
                order(v.tensor_reduce(sel, prod.rearrange("p t (g e) -> p t e g", g=G), AX, ALU.add))
                oh = hot[:, 0, 0:nt, :]
                first_max(sel, nt, EPG, v0, i0, oh)
                order(v.scalar_tensor_tensor(sel, oh, -3.0e38, sel, ALU.mult, ALU.add))
                first_max(sel, nt, EPG, v1, i1, oh)
                v.tensor_tensor(e1, v1, v0, ALU.subtract).then_inc(shifted, 1)
                eid = rv[:, 10:12, 0:nt]
                for k, ik in enumerate((i0, i1)):
                    order(v.scalar_tensor_tensor(eid[:, k, :], gidx, float(EPG), ik, ALU.mult, ALU.add))
                ch = chosen[:, 0:2 * nt, :]
                for k in range(2):
                    order(v.tensor_tensor(ch[:, k * nt:(k + 1) * nt, :], bcast(cst("iota"), nt, 1), bcast(eid[:, k, :], E, 2), ALU.is_equal))
                order(v.tensor_tensor(member[:, 0:nt, :], ch[:, 0:nt, :], ch[:, nt:2 * nt, :], ALU.add))
                if nt > NX:
                    order(v.tensor_scalar(member[:, NX, :], member[:, NX, :], cst("head"), None, ALU.mult))
                order(v.memset(member[:, nt, :], 0.0))
                order(v.memset(before[:, 0, :], 0.0))
                for t in range(nt):
                    order(v.tensor_tensor(before[:, t + 1, :], before[:, t, :], member[:, t, :], ALU.add))
                dve.sem_inc(members, 1)
                for k in range(2):
                    order(v.tensor_tensor(row_of[:, k * nt:(k + 1) * nt, :], ch[:, k * nt:(k + 1) * nt, :],
                                          bcast(cst("row")[:, 5 * k:5 * k + nt], E, 2), ALU.mult))
                    if nt > NX:
                        order(v.tensor_scalar(row_of[:, k * nt + NX, :], row_of[:, k * nt + NX, :], cst("head"), None, ALU.mult))
                dve.wait_ge(exped, 2 * layer + 1)
                order(v.tensor_reduce(psum_g, ex, AX, ALU.add))
                order(v.reciprocal(pg, psum_g))
                dve.wait_ge(exped, 2 * layer + 2)
                den = rv[:, 9, 0:nt]
                order(v.tensor_scalar(den, e1, 1.0, None, ALU.add))
                order(v.reciprocal(den, den))
                order(v.tensor_tensor(gate[:, 0, 0:nt], pg, den, ALU.mult))
                order(v.tensor_tensor(gate[:, 1, 0:nt], gate[:, 0, 0:nt], e1, ALU.mult))
                dve.wait_ge(ranked, layer + 1)
                rank = ps[:, 3, 0:nt * E].rearrange("p (t e) -> p t e", t=nt)
                for k in range(2):
                    order(v.tensor_tensor(work[:, k * nt:(k + 1) * nt, :], ch[:, k * nt:(k + 1) * nt, :], rank, ALU.mult))
                ranks = rank_of[:, 0:2 * nt]
                order(v.tensor_reduce(ranks, work[:, 0:2 * nt, :], AX, ALU.add))
                v.tensor_tensor(at_slot[:, 0:2 * nt, :], bcast(cst("slot"), 2 * nt, 1), bcast(ranks, C, 2), ALU.is_equal).then_inc(placed, 1)
                order(v.tensor_copy(counted[:, :], ps[0:1, 3, nt * E:(nt + 1) * E]))
                flags = spread.rearrange("p (b e) -> p b e", e=E)
                order(v.tensor_tensor(flags, cst("more", 1).rearrange("p (b e) -> p b e", e=E), bcast(counted[:, :], NBLK - 1, 1), ALU.is_lt))
                order(v.tensor_reduce(n_more[:, 0:1], spread, AX, ALU.add))
                v.tensor_copy(n_more_i[:, :], n_more[:, 0:1]).then_inc(more_known, 1)
                def row_numbers(table, t3, dst, src, note):
                    add, row, fold = (t3[:, c, :] for c in range(3))
                    note(v.tensor_scalar(add, table, 0.0, float(EMPTY), ALU.is_equal, ALU.mult))
                    note(v.scalar_tensor_tensor(row, table, -1.0, add, ALU.add, ALU.add))
                    note(v.tensor_scalar(fold, row, float(SPREAD), -2.0 * SPREAD, ALU.is_ge, ALU.mult))
                    note(v.tensor_scalar(row, row, 2.0, cst("half"), ALU.mult, ALU.add))
                    return v.tensor_copy(dst, row), v.tensor_tensor(src, row, fold, ALU.add)

                dve.wait_ge(tabled, layer + 1)
                for ins in row_numbers(ps[:, 2, 0:E], tab, dst_row[:, :], src_row[:, :], order):
                    ins.then_inc(rows_ready, 1)

                def take_x(b):
                    shape = dict(c=KC // 2, a=2)
                    g = block_gain[:, layer, :].rearrange("p (a c) -> p c a", a=2)
                    return v.tensor_tensor(xT[:, b, :].rearrange("p (c a n) -> p c a n", **shape),
                                           ps[:, b, :].rearrange("p (c a n) -> p c a n", **shape), bcast(g, C, 3), ALU.mult)

                def pair(q, last):
                    for u in range(2):
                        dve.wait_ge(silu_ready, E * layer + q * 2 + u + 1)
                        v.tensor_tensor(hidden[:, u, :], silu[:, u, :], ps[:, 2 + u, FE // 2:], ALU.mult).then_inc(hidden_ready, 1)
                        if not (last and u == 1):
                            dve.wait_ge(x_turned, E * layer + q * 2 + u + 2)
                            take_x(1 - u).then_inc(xT_ready, 1)

                dve.wait_ge(x_turned, E * layer + 1)
                take_x(0).then_inc(xT_ready, 1)
                with dve.Fori(0, PAIRS - 1) as q:
                    pair(q, False)
                pair(PAIRS - 1, True)

                dve.wait_ge(more_known, layer + 1)
                more = load_more(dve, layer)
                with dve.If(more > 0):
                    dve.wait_ge(scattered[layer][0], 16 * PAIRS)
                    dve.wait_ge(scattered[layer][1], 16 * PAIRS)
                    run = scan
                    n0 = 0
                    more_order = more_steps[layer]
                    def mo(ins):
                        nonlocal n0
                        ins.then_inc(more_order, 1)
                        n0 += 1
                        dve.wait_ge(more_order, n0)
                    mo(v.tensor_tensor(flags, cst("more", 1).rearrange("p (b e) -> p b e", e=E), bcast(counted[:, :], NBLK - 1, 1), ALU.is_lt))
                    mo(v.tensor_tensor_scan(run, spread, spread, 0.0, ALU.add, ALU.bypass))
                    for b in range(MAXMORE):
                        mo(v.tensor_scalar(spread, run, float(b), None, ALU.is_le))
                        mo(v.tensor_reduce(small[0:1, 16 + b:17 + b], spread, AX, ALU.add))
                    mo(v.tensor_copy(more_i[:, 0, :], small[0:1, 16:16 + MAXMORE]))
                    mo(v.tensor_scalar(more_i[:, 1, :], more_i[:, 0, :], E - 1, None, ALU.bitwise_and))
                    assert n0 == MORE_STEPS
                    for b in range(1, NBLK):
                        if b > 1:
                            dve.wait_ge(more_tabled[layer], b - 1)
                        mo(v.tensor_scalar(rank_b[:, 0:2 * nt], ranks, -float(b * C), None, ALU.add))
                        v.tensor_tensor(at_slot[:, 0:2 * nt, :], bcast(cst("slot"), 2 * nt, 1), bcast(rank_b[:, 0:2 * nt], C, 2),
                                        ALU.is_equal).then_inc(more_hot[layer], 1)
                    dve.wait_ge(more_tabled[layer], NBLK - 1)
                    for ins in row_numbers(ps[:, 2, 0:(NBLK - 1) * E], tab_more, dst_more, src_more, mo):
                        ins.then_inc(more_rows[layer], 1)
                    with dve.Fori(0, more) as b:
                        dve.wait_ge(more_turned[layer], b + 1)
                        take_x(0).then_inc(more_xT[layer], 1)
                        dve.wait_ge(more_silu[layer], b + 1)
                        v.tensor_tensor(hidden[:, 0, :], silu[:, 0, :], ps[:, 2, FE // 2:], ALU.mult).then_inc(more_hidden[layer], 1)
                dve.nop()

            def combine(layer, t):
                r, n = rows(t), t % 4
                dve.wait_ge(y_landed[layer][n], 32 * (t // 4 + 1))
                order(v.scalar_tensor_tensor(h[0:r, t, :], y_in[0:r, n, 0, :], gate[0:r, 0, t:t + 1], h[0:r, t, :], ALU.mult, ALU.add))
                v.scalar_tensor_tensor(h[0:r, t, :], y_in[0:r, n, 1, :], gate[0:r, 1, t:t + 1], h[0:r, t, :], ALU.mult, ALU.add
                                       ).then_inc(combined[layer], 1)

            moe(0)

            for t in range(NX + 1):
                combine(0, t)
                rstd_tile(2, t)
                dve.wait_ge(turned[2], t + 1)
                gained(actT[:, :, cols(t)[0]:cols(t)[1]], t, 2).then_inc(turned_out[2], 1)
                if t < NX:
                    gained(actT2[:, :, t * P:(t + 1) * P], t, 4).then_inc(turned_out[2], 1)

            def rotate(n):
                p = ROT_JOBS[n]
                _, f, t = JOBS[p]
                r = rows(t)
                dve.wait_ge(proj_copied, p + 1)
                if n:
                    dve.wait_ge(roped, n)
                X = knat[0:r, n % 2, :].rearrange("p (g d) -> p g d", d=HD)[:, :, 0:ROT]
                A = rope[0:r, 0:8 * ROT].rearrange("p (g d) -> p g d", g=8)
                B = rope[0:r, 8 * ROT:16 * ROT].rearrange("p (g d) -> p g d", g=8)
                cc = bcast(cst("cos", r)[:, t * ROT:(t + 1) * ROT], 8, 1)
                ss = bcast(cst("sin", r)[:, t * ROT:(t + 1) * ROT], 8, 1)
                hr = ROT // 2
                order(v.tensor_tensor(A, X, cc, ALU.mult))
                order(v.tensor_tensor(B[:, :, 0:hr], X[:, :, hr:], ss[:, :, 0:hr], ALU.mult))
                order(v.tensor_tensor(B[:, :, hr:], X[:, :, 0:hr], ss[:, :, hr:], ALU.mult))
                v.tensor_tensor(X, A, B, ALU.add).then_inc(roped, 1)

            def take_rot(n):
                kind, f, t = JOBS[ROT_JOBS[n]]
                r = rows(t)
                dve.wait_ge(rot_turned, n + 1)
                dst, a = (kT, cols(t)[0]) if kind == "k" else (actT, t * P)
                src = ps[:, 2 + n % 2, :].rearrange("p (c n) -> p c n", c=4)[:, :, 0:r]
                v.tensor_copy(dst[:, 4 * f:4 * f + 4, a:a + r], src).then_inc(rot_copied, 1)

            for n in range(len(ROT_JOBS)):
                rotate(n)
                if n >= 1:
                    take_rot(n - 1)
            take_rot(len(ROT_JOBS) - 1)

            dve.wait_ge(lam_exp, 1)
            order(v.tensor_tensor(lam[:, 4:5], lam[:, 3:4], lam[:, 2:3], ALU.subtract))
            order(v.tensor_scalar(lam[:, 5:6], lam[:, 4:5], -LAM_INIT, None, ALU.add))

            def maxima(n):
                i = STEPS[n][0]
                s = score_view(n)
                for c0, c1 in ((0, 2),) if i < NX - 1 else ((0, 1), (1, 2)):
                    dve.wait_ge(scores_done, 2 * n + c1)
                    order(v.memset(s[0:HD, c0:c1, keys(i) - HD:keys(i)], -3.4028235e38))
                    if n:
                        dve.wait_ge(max_ready, 2 * n + c0)
                    order(v.tensor_reduce(small[:, c0:c1], s[:, c0:c1, :], AX, ALU.max))
                    o = 4 + 2 * (n % 2)
                    v.tensor_scalar(small[:, o + c0:o + c1], small[:, c0:c1], -HD ** -0.5, None, ALU.mult).then_inc(max_ready, c1 - c0)

            def difference(n):
                k = keys(STEPS[n][0])
                o = 48 + 2 * (n % 3)
                dve.wait_ge(exp_done, 2 * n + 2)
                if n:
                    dve.wait_ge(a_ready, n)
                order(v.reciprocal(small[:, 12:14], small[:, o:o + 2]))
                order(v.tensor_tensor(small[:, 14:15], small[:, 13:14], lam[:, 5:6], ALU.mult))
                order(v.tensor_scalar(prob[:, n % 3, 1, 0:k], prob[:, n % 3, 1, 0:k], small[:, 14:15], None, ALU.mult))
                v.scalar_tensor_tensor(prob[:, n % 3, 0, 0:k], prob[:, n % 3, 0, 0:k], small[:, 12:13], prob[:, n % 3, 1, 0:k],
                                       ALU.mult, ALU.add).then_inc(a_ready, 1)

            def mean_heads(i):
                dve.wait_ge(o_squared, i + 1)
                order(v.tensor_reduce(small[:, 16:24], square.rearrange("p (h d) -> p h d", d=P), AX, ALU.add))
                v.tensor_scalar(small[:, 24:32], small[:, 16:24], 1.0 / P, EPS, ALU.mult, ALU.add).then_inc(heads_meaned, 1)

            def norm_heads(i):
                dve.wait_ge(heads_rooted, i + 1)
                o = nat[:, i % 2, :].rearrange("p (h d) -> p h d", d=P)
                v.tensor_tensor(o, o, bcast(small[:, 32:40], P, 2), ALU.mult).then_inc(o_ready, 1)

            def take_o(i):
                dve.wait_ge(o_turned, i + 1)
                v.tensor_scalar(actT[:, :, i * P:(i + 1) * P], flat[:, 4 * W:6 * W].rearrange("p (k n) -> p k n", k=KC), subln[:, :], None,
                                ALU.mult).then_inc(oT_copied, 1)

            for n in range(len(STEPS)):
                maxima(n)
                if n >= 1:
                    difference(n - 1)
                if n >= NH and n % NH == 4:
                    mean_heads(n // NH - 1)
                if n >= NH and n % NH == 5:
                    norm_heads(n // NH - 1)
                if n >= NH and n % NH == 7:
                    take_o(n // NH - 1)
            difference(len(STEPS) - 1)
            mean_heads(NX - 1)
            norm_heads(NX - 1)
            take_o(NX - 1)

            moe(1)
            dve.wait_ge(final_landed, 16)
            for t in range(NX):
                combine(1, t)
                dve.wait_ge(squared, 5 * 3 + NX + t + 1)
                order(v.reciprocal(rstd[:, t:t + 1], ssq[:, t:t + 1]))
                v.scalar_tensor_tensor(nat[:, t % 2, :], h[:, t, :], rstd[:, t:t + 1], final_gain, ALU.mult, ALU.mult).then_inc(final_ready, 1)


_INS = ["x", "meta_tokens", "a_norm", "a_w_in", "a_conv", "a_w_out", "kv_norm", "w_kv", "b_norm", "b_w_q", "b_lambda", "b_subln",
        "b_w_out", "ffn_norm", "r_group", "r_group_b", "r_expert", "r_expert_b", "e_gate", "e_up", "e_down", "final_norm"]


def constants():
    import numpy as np

    t = np.zeros((P, NCONST), np.float32)

    def put(name, values):
        a, n = CONST[name]
        t[:, a:a + n] = values

    put("ident", np.eye(P))
    put("upper", np.triu(np.ones((P, P)), 1))
    put("ones", 1.0)
    put("iota", np.arange(E))
    put("iota100", np.arange(EPG) + 100)
    put("more", np.repeat(np.arange(1, NBLK) * C, E))
    half = ROT // 2
    freq = (np.float32(500000.0) ** (-np.arange(half, dtype=np.float32) * np.float32(2.0) / np.float32(ROT))).astype(np.float32)
    pos = np.zeros((5, P), np.float32)
    for i in range(NX):
        pos[i] = META + i * P + np.arange(P)
    pos[NX, :META] = np.arange(META)
    ang = (pos[:, :, None] * freq).astype(np.float32)
    cos, sin = np.cos(ang), np.sin(ang)
    put("cos", np.concatenate([cos, cos], -1).transpose(1, 0, 2).reshape(P, 5 * ROT))
    put("sin", np.concatenate([-sin, sin], -1).transpose(1, 0, 2).reshape(P, 5 * ROT))
    put("eps", EPS)
    put("minus_half", -0.5)
    row = np.arange(5)[None, :] * P + np.arange(P)[:, None]
    put("row", np.concatenate([row, row + SPREAD], 1) + 1)
    put("slot", np.arange(C))
    put("half", (np.arange(P)[:, None] >= C))
    put("head", (np.arange(P)[:, None] < META))
    return t


def kernel(**inputs):
    import numpy as _np
    import concourse.bacc as _bacc
    from concourse.bass_utils import run_bass_kernel_spmd as _run

    nc = _bacc.Bacc("TRN2", target_bir_lowering=False, num_devices=1)
    arrays, args = {}, []
    for name in _INS:
        a = _np.ascontiguousarray(inputs[name])
        arrays[f"in_{name}"] = a
        args.append(nc.dram_tensor(f"in_{name}", a.shape, mybir.dt.from_np(a.dtype), kind="ExternalInput").ap())
    table = constants()
    arrays["in_table"] = table
    args.append(nc.dram_tensor("in_table", table.shape, F32, kind="ExternalInput").ap())
    args.append(nc.dram_tensor("out", (1, SEQ, D), F32, kind="ExternalOutput").ap())
    build(nc, *args)
    r = _run(nc, [arrays], core_ids=[0])
    return r.results[0]["out"]
```

```python
import math
from contextlib import ExitStack

import concourse.bass as bass
from concourse import mybir

F32 = mybir.dt.float32
F32R = mybir.dt.float32r
U32 = mybir.dt.uint32
I32 = mybir.dt.int32
ALU = mybir.AluOpType
ACT = mybir.ActivationFunctionType
AX = mybir.AxisListType.X

P = 128
D = 1024
KC = D // P
SEQ, META = 512, 16
NX = SEQ // P
LEN = SEQ + META
HALF = LEN // 2
W = 512
FE = 512
FC = FE // P
G, EPG = 4, 8
E = G * EPG
HD, NH = 64, 8
ROT = HD // 4
EPS = 1e-6
LAM_INIT = 0.8 - 0.6 * math.exp(-0.3)

C = 64
NBLK = -(-LEN // C)
SPREAD = 1024
EMPTY = 4 * SPREAD
DH = D // 2
MAXMORE = 16

MORE_STEPS = 2 * MAXMORE + 4

RING = 6
UNIT = KC * W
U_IN, U_AOUT = 0, 6
U_MOE0 = U_AOUT + 4
U_KVQ = U_MOE0 + 3 * (E - 1)
U_QT = U_KVQ + 12
U_BOUT = U_QT + 1
U_MOE1 = U_BOUT + 4
U_MOE = (U_MOE0, U_MOE1)
ORDER = ("gate", "up", "down")
assert all((U_MOE[l] + 3 * u) % RING < RING - 1 for l in range(2) for u in range(2))

QUARTERS = 4
S_AOUT = 3 * KC
S_KVQ = S_AOUT + 2 * QUARTERS
S_BOUT = S_KVQ + 6 * QUARTERS
T_OUT, T_KVQ, T_BOUT = NX + 1, 2 * (NX + 1), 3 * (NX + 1)
PAIRS = E // 2

CONST = {}
_at = 0
for _name, _n in (("ident", P), ("upper", P), ("ones", P), ("iota", E), ("iota100", EPG),
                  ("more", (NBLK - 1) * E), ("cos", 5 * ROT), ("sin", 5 * ROT), ("row", 10), ("slot", C), ("half", 1), ("head", 1), ("eps", 1), ("minus_half", NH)):
    CONST[_name] = (_at, _n)
    _at += _n
NCONST = _at


def rows(t):
    return P if t < NX else META


def cols(t):
    return (META + t * P, META + (t + 1) * P) if t < NX else (0, META)


class Tally:

    def __init__(self, eng, sem):
        self.eng, self.sem, self.n = eng, sem, 0

    def order(self, ins):
        ins.then_inc(self.sem, 1)
        self.n += 1
        self.eng.wait_ge(self.sem, self.n)


def build(nc, x, meta_tokens, a_norm, a_w_in, a_conv, a_w_out, kv_norm, w_kv, b_norm, b_w_q, b_lambda, b_subln,
          b_w_out, ffn_norm, r_group, r_group_b, r_expert, r_expert_b, e_gate, e_up, e_down, final_norm, table, out):
    with ExitStack() as ctx:
        def sb(name, shape, dt=F32):
            return ctx.enter_context(nc.sbuf_tensor(name, shape, dt))

        def sem(name):
            return ctx.enter_context(nc.semaphore(name))

        hn_dram = [nc.dram_tensor(f"hn_rows{l}", [(LEN, SEQ)[l], D], F32).ap() for l in range(2)]
        y_dram = [nc.dram_tensor(f"expert_rows{l}", [2 * SPREAD, D], F32).ap() for l in range(2)]
        hn_halves = [a.rearrange("r (a n) -> (r a) n", a=2) for a in hn_dram]
        y_halves = [a.rearrange("r (a n) -> (r a) n", a=2) for a in y_dram]

        with ExitStack() as names:
            parts = [names.enter_context(nc.sbuf_tensor(f"parts{i}", [P, n], F32R))
                     for i, n in enumerate([UNIT] * RING + [KC * LEN, KC * LEN, (NX + 1) * D, KC * LEN])]
        ring_parts, (act17_parts, front_parts, middle_parts, third_parts) = parts[:RING], parts[RING:]
        ring = sb("ring", [P, RING, UNIT])
        act17 = sb("act17", [P, KC * LEN])
        arena = sb("arena", [P, 2 * KC * LEN + (NX + 1) * D])
        h = sb("h", [P, NX + 1, D])
        nat = sb("nat", [P, 2, D])
        knat = sb("knat", [P, 2, W])
        const = sb("const", [P, NCONST])
        gain = sb("gain", [P, 5, KC])
        block_gain = sb("block_gain", [P, 2, KC])
        conv = sb("conv", [P, 3 * KC])
        wr = sb("wr", [P, 2, KC, G + E])
        rbias = sb("rbias", [P, 2, G + E])
        subln = sb("subln", [P, 1])
        lam = sb("lam", [P, 8])
        ssq = sb("ssq", [P, 8])
        rstd = sb("rstd", [P, 8])
        gate = sb("gate", [P, 2, NX + 1])
        src_row = sb("src_row", [P, E], U32)
        dst_row = sb("dst_row", [P, E], U32)
        src_now = sb("src_now", [P, 2], U32)
        dst_now = sb("dst_now", [P, 2], U32)
        counted = sb("counted", [1, E])
        n_more = sb("n_more", [1, 2])
        n_more_i = sb("n_more_i", [1, 1], I32)
        more_i = sb("more_i", [1, 2, MAXMORE], I32)
        small = sb("small", [P, 64])
        rope = sb("rope", [P, 16 * ROT])

        actT = act17[:, :].rearrange("p (k n) -> p k n", k=KC)
        y_out = act17[:, 0:2 * DH].rearrange("p (b n) -> p b n", b=2)
        xT = act17[:, 1024:2048].rearrange("p (b n) -> p b n", b=2)
        hT = act17[:, 2048:2560].rearrange("p (b n) -> p b n", b=2)
        silu = act17[:, 2560:3072].rearrange("p (b n) -> p b n", b=2)
        hidden = act17[:, 3072:3584].rearrange("p (b n) -> p b n", b=2)
        result = act17[:, 0:NX * D].rearrange("p (t n) -> p t n", t=NX)
        logit = act17[:, 0:180].rearrange("p (t n) -> p t n", t=NX + 1)
        chosen = act17[:, 192:512].rearrange("p (c n) -> p c n", n=E)
        work = act17[:, 512:832].rearrange("p (c n) -> p c n", n=E)
        member = act17[:, 832:1024].rearrange("p (c n) -> p c n", n=E)
        at_slot = act17[:, 2048:2048 + 10 * C].rearrange("p (c n) -> p c n", n=C)
        before = act17[:, 1024:1216].rearrange("p (c n) -> p c n", n=E)
        tab = act17[:, 1216:1216 + 3 * E].rearrange("p (c n) -> p c n", c=3)
        leg = act17[:, 1600:1640].rearrange("p (t n) -> p t n", n=EPG)
        hot = act17[:, 1640:1720].rearrange("p (k t n) -> p k t n", k=2, n=EPG)
        cand = act17[:, 1720:1760].rearrange("p (t n) -> p t n", n=EPG)
        rv = act17[:, 1760:1860].rearrange("p (c t) -> p c t", t=NX + 1)
        scan = act17[0:1, 0:(NBLK - 1) * E]
        spread = act17[0:1, 3072:3072 + (NBLK - 1) * E]

        kT = arena[:, 0:KC * LEN].rearrange("p (k n) -> p k n", k=KC)
        V = arena[:, KC * LEN:KC * LEN + 5 * D].rearrange("p (t n) -> p t n", n=D)
        third = arena[:, KC * LEN + 5 * D:]
        actT2 = third.rearrange("p (k n) -> p k n", k=KC)
        lead_w = arena[:, 0:2 * KC * LEN].rearrange("p (u n) -> p u n", u=2)[:, :, 0:UNIT]
        lead_down = arena[:, KC * LEN + 5 * D:KC * LEN + 5 * D + UNIT]
        tail = arena[:, KC * LEN + UNIT:KC * LEN + 5 * D]
        src_more = tail[:, 0:(NBLK - 1) * E].bitcast(U32)
        dst_more = tail[:, 256:256 + (NBLK - 1) * E].bitcast(U32)
        row_of = tail[:, 512:832].rearrange("p (c n) -> p c n", n=E)
        rank_of = tail[:, 832:842]
        rank_b = tail[:, 842:852]
        tab_more = act17[:, 0:3 * 256].rearrange("p (c n) -> p c n", c=3)
        stage = knat[:, :, :].rearrange("p b n -> p (b n)")
        stage_lam = stage[:, 576:832]
        stage_conv = stage[0:3 * KC, 832:960]
        va = KC * LEN
        c_gate = arena[:, va:va + 2 * LEN].rearrange("p (b n) -> p b n", b=2)
        cu = arena[:, va + 2 * LEN:va + 3 * LEN + 2]
        z = arena[:, va + 3 * LEN + 2:va + 4 * LEN + 2]
        chunks = lambda ap: ap.rearrange("p (k n) -> p k n", k=KC)
        act17_low = chunks(act17_parts[:, :])
        front_high = chunks(front_parts[:, :])
        third_part = chunks(third_parts[:, :])
        w_high = middle_parts[:, 4 * LEN + 2:4 * LEN + 2 + 2 * UNIT // 4].rearrange("p (b k n) -> p b k n", b=2, k=KC)
        qT = chunks(ring[:, U_QT % RING, :])
        prob = third[:, 0:6 * LEN].rearrange("p (b c n) -> p b c n", b=3, c=2)
        probT = (h[:, NX, 4 * P:8 * P], third[:, 6 * LEN:6 * LEN + 4 * P])
        metaT = third[:, 6 * LEN + 4 * P:6 * LEN + 6 * P].rearrange("p (b n) -> p b n", b=2)
        q_pad = h[:, NX, 0:4 * P].rearrange("p (b c n) -> p b c n", b=2, c=2)
        final_gain = knat[:, :, :].rearrange("p b n -> p (b n)")
        square = final_gain

        def y_in(t, k):
            if t == NX and k == 1:
                return square[0:META, :]
            return arena[0:rows(t), (2 * t + k) * D:(2 * t + k + 1) * D]

        def cst(name, r=P):
            a, n = CONST[name]
            return const[0:r, a:a + n]

        ident = cst("ident")

        ps = ctx.enter_context(nc.psum_tensor("ps", [P, 8, W], F32))
        flat = ps[:, :, :].rearrange("p b n -> p (b n)")

        x_landed = [sem(f"x_landed{t}") for t in range(NX + 1)]
        const_landed = sem("const_landed")
        param_landed = sem("param_landed")
        ring_landed = [sem(f"ring_landed{s}") for s in range(RING)]
        unit_used = sem("unit_used")
        lead_landed, lead_down_landed, lead_used = sem("lead_landed"), sem("lead_down_landed"), sem("lead_used")
        passed = sem("passed")
        dve_step, act_step = sem("dve_step"), sem("act_step")
        params_ready, conv_turned, conv_ready = sem("params_ready"), sem("conv_turned"), sem("conv_ready")
        w_high_ready, w_low_ready = sem("w_high_ready"), sem("w_low_ready")
        act_high_ready, act_low_ready = sem("act_high_ready"), sem("act_low_ready")
        lam_ready, lam_exp = sem("lam_ready"), sem("lam_exp")
        squared = sem("squared")
        scaled = sem("scaled")
        rstd_ready = sem("rstd_ready")
        turned = [sem(f"turned{n}") for n in range(4)]
        turned_out = [sem(f"turned_out{n}") for n in range(4)]
        in_done, c_copied, u_taken, b_taken = sem("in_done"), sem("c_copied"), sem("u_taken"), sem("b_taken")
        out_done = sem("out_done")
        mixed = sem("mixed")
        logits_done = sem("logits_done")
        hn_stored = [[sem(f"hn_stored{l}{b}") for b in range(2)] for l in range(2)]
        shifted, exped = sem("shifted"), sem("exped")
        members, ranked = sem("members"), sem("ranked")
        placed, more_known = sem("placed"), sem("more_known")
        hidden_ready, hidden_turned = sem("hidden_ready"), sem("hidden_turned")
        tabled, rows_ready = sem("tabled"), sem("rows_ready")
        gathered = [[sem(f"gathered{l}{b}") for b in range(2)] for l in range(2)]
        scattered = [[sem(f"scattered{l}{b}") for b in range(2)] for l in range(2)]
        index_set = [sem(f"index_set{l}") for l in range(2)]
        x_turned, xT_ready = sem("x_turned"), sem("xT_ready")
        silu_ready, hT_ready = sem("silu_ready"), sem("hT_ready")
        y_ready = sem("y_ready")
        more_steps = [sem(f"more_steps{l}") for l in range(2)]
        more_index = [sem(f"more_index{l}") for l in range(2)]
        more_gathered, more_w_landed = [sem(f"more_gathered{l}") for l in range(2)], [sem(f"more_w_landed{l}") for l in range(2)]
        more_turned, more_xT = [sem(f"more_turned{l}") for l in range(2)], [sem(f"more_xT{l}") for l in range(2)]
        more_up, more_silu = [sem(f"more_up{l}") for l in range(2)], [sem(f"more_silu{l}") for l in range(2)]
        more_rows = [sem(f"more_rows{l}") for l in range(2)]
        more_hot, more_tabled = [sem(f"more_hot{l}") for l in range(2)], [sem(f"more_tabled{l}") for l in range(2)]
        more_hidden, more_h_turned = [sem(f"more_hidden{l}") for l in range(2)], [sem(f"more_h_turned{l}") for l in range(2)]
        more_hT, more_down = [sem(f"more_hT{l}") for l in range(2)], [sem(f"more_down{l}") for l in range(2)]
        more_y, more_scattered = [sem(f"more_y{l}") for l in range(2)], [sem(f"more_scattered{l}") for l in range(2)]
        y_landed = [[sem(f"y_landed{l}{s}") for s in range(NX + 1 - l)] for l in range(2)]
        combined = [sem(f"combined{l}") for l in range(2)]
        proj_done, proj_copied = sem("proj_done"), sem("proj_copied")
        roped, rot_turned, rot_copied = sem("roped"), sem("rot_turned"), sem("rot_copied")
        v_cleared, pads_clear, q_padded = sem("v_cleared"), sem("pads_clear"), sem("q_padded")
        scores_done, max_ready, exp_done = sem("scores_done"), sem("max_ready"), sem("exp_done")
        a_ready, a_turned, aT_copied, av_done = sem("a_ready"), sem("a_turned"), sem("aT_copied"), sem("av_done")
        o_copied, o_squared, o_ready = sem("o_copied"), sem("o_squared"), sem("o_ready")
        heads_meaned, heads_rooted = sem("heads_meaned"), sem("heads_rooted")
        o_turned, oT_copied = sem("o_turned"), sem("oT_copied")
        final_landed, final_ready = sem("final_landed"), sem("final_ready")
        stored = [sem(f"stored{b}") for b in range(2)]

        block = ctx.enter_context(nc.Block())

        N_PARAM = 17

        def tiles_of(layer):
            return NX + 1 if layer == 0 else NX

        A_OUT_AT = {KC - 3: (0,), KC - 2: (1,), KC - 1: (2, 3)}
        SPLIT_ORDER = [0, 1]
        for j in range(KC):
            SPLIT_ORDER += [i for i in range(3 * j + 2, 3 * j + 5) if i < S_AOUT] + [S_AOUT + q for q in A_OUT_AT.get(j, ())]
        SPLIT_ORDER += list(range(S_AOUT + QUARTERS, S_BOUT + 2 * QUARTERS))
        SPLITS = {i: n + 1 for n, i in enumerate(SPLIT_ORDER)}
        B_OUT_AT = {n: S_BOUT + i for i, n in enumerate((1, 3, 5, 7, 9, 11, 13, 15))}

        JOBS = ([("k", f, t) for f in range(2) for t in range(NX + 1)]
                + [("v", f, t) for f in range(2) for t in range(NX + 1)]
                + [("q", f, t) for f in range(2) for t in range(NX)])
        O_BANK = [4] * (NX - 1) + [0]
        SPLIT_AFTER = {5 * u + q: S_KVQ + (u + 1) * QUARTERS + q for u in range(5) for q in range(QUARTERS)}
        ROT_JOBS = [p for p, j in enumerate(JOBS) if j[0] != "v"]
        STEPS = [(i, hh) for i in range(NX) for hh in range(NH)]

        def keys(i):
            return META + P * (i + 1)

        def score_view(n):
            i = STEPS[n][0]
            if i < NX - 1:
                return ps[:, 2 * (n % 2):2 * (n % 2) + 2, 0:keys(i)]
            return flat[:, 0:4 * W].rearrange("p (c n) -> p c n", c=2)[:, :, 0:keys(i)]

        MADE = {m + 1 for m in range(U_AOUT, U_MOE0, 2)} | {m + 1 for m in range(U_KVQ, U_QT, 2)} | {m + 1 for m in range(U_BOUT, U_MOE1, 2)} | {U_QT}

        def landing(n):
            return 16 * sum(m not in MADE for m in range(n % RING, n + 1, RING))

        def landed(eng, n):
            eng.wait_ge(ring_landed[n % RING], landing(n))

        def weight_piece(i):
            if i < S_AOUT:
                j, s = divmod(i, 3)
                n = U_IN + 3 * (j // 4) + s
                at = lambda ap: chunks(ap)[:, :, (j % 4) * P:(j % 4 + 1) * P]
                return at(ring[:, n % RING, :]), at(ring_parts[n % RING][:, :]), w_high[:, i % 2], n, None
            base, first = (U_AOUT, S_AOUT) if i < S_KVQ else (U_KVQ, S_KVQ) if i < S_BOUT else (U_BOUT, S_BOUT)
            f, q = divmod(i - first, QUARTERS)
            n = base + 2 * f
            a, b = q * UNIT // QUARTERS, (q + 1) * UNIT // QUARTERS
            return ring[:, n % RING, a:b], ring_parts[n % RING][:, a:b], ring_parts[(n + 1) % RING][:, a:b], n, n + 1

        def act_tile(i):
            group, t = divmod(i, NX + 1)
            a, b = cols(t)
            if group == 3:
                a, b = t * P, (t + 1) * P
            src = (actT, actT2, flat[:, 0:KC * P].rearrange("p (k n) -> p k n", k=KC), actT)[group]
            src = src[:, :, 0:rows(t)] if group == 2 else src[:, :, a:b]
            high = (front_high, front_high, third_part, front_high)[group][:, :, a:b]
            low = (act17_low, third_part, act17_low, act17_low)[group][:, :, a:b]
            return src, high, low

        def expert_unit(layer, q, u, part):
            n = U_MOE[layer] + 3 * (1 - u) + ORDER.index(part)
            return n % RING, landing(n) + 16 * q - (0 if u else 16)

        def bcast(ap, n, at):
            return ap.unsqueeze(at).to_broadcast([*ap.shape[:at], n, *ap.shape[at:]])

        def load_more(eng, layer):
            eng.wait_ge(more_known, layer + 1)
            return eng.value_load(n_more_i[0:1, 0:1], min_val=0, max_val=MAXMORE)

        @block.sync
        def _(sp):
            free_at = {}

            def unit(n, src, **k):
                if n >= RING:
                    sp.wait_ge(unit_used, free_at[n % RING])
                free_at[n % RING] = n + 1
                sp.dma_start(ring[:, n % RING, :].rearrange("p (k n) -> p k n", **k), src).then_inc(ring_landed[n % RING], 16)

            def split_unit(n, src):
                unit(n, src, k=KC)
                free_at[(n + 1) % RING] = n + 2

            sp.dma_start(h[:, 0, :], x[0, 0:P, :]).then_inc(x_landed[0], 16)
            sp.dma_start(const[:, :], table).then_inc(const_landed, 16)
            sp.dma_start(gain[:, 0, :], a_norm[0].rearrange("(p k) -> p k", k=KC)).then_inc(const_landed, 16)
            for t in range(1, NX):
                sp.dma_start(h[:, t, :], x[0, t * P:(t + 1) * P, :]).then_inc(x_landed[t], 16)
            sp.dma_start(h[0:META, NX, :], meta_tokens).then_inc(x_landed[NX], 16)

            w_in = a_w_in[0].rearrange("(p k) n -> p k n", k=KC)
            for f in range(2):
                if f == 1:
                    sp.wait_ge(param_landed, 16 * N_PARAM)
                for s, part in enumerate((1, 2, 0)):
                    unit(U_IN + 3 * f + s, w_in[:, :, part * D + f * W:part * D + (f + 1) * W], k=KC)
            w_o = a_w_out[0].rearrange("(k p) n -> p k n", p=P)
            for f in range(2):
                split_unit(U_AOUT + 2 * f, w_o[:, :, f * W:(f + 1) * W])

            def expert_load(layer, part, ex, dst, landing):
                w = {"gate": e_gate, "up": e_up, "down": e_down}[part][layer, ex].rearrange("o a b -> (o a) b")
                if part == "down":
                    sp.dma_start(dst.rearrange("p (k n) -> p k n", k=FC), w.rearrange("(f p) n -> p f n", p=P)).then_inc(landing, 16)
                else:
                    sp.dma_start(dst.rearrange("p (a m) -> p a m", a=2),
                                 w.rearrange("(a p c) n -> p a (c n)", a=2, c=KC // 2)).then_inc(landing, 16)

            def experts(layer):
                done = {"gate": 2, "up": 2, "down": 3}

                def load(e, part, wait):
                    q, u = e
                    n = U_MOE[layer] + 3 * u + ORDER.index(part)
                    sp.wait_ge(unit_used, free_at[n % RING] if wait is None else wait)
                    expert_load(layer, part, bass.ds(q * 2 + 1 + u, 1), ring[:, n % RING, :], ring_landed[n % RING])
                    free_at[n % RING] = U_MOE[layer] + 3 * (E - 2 - u) + done[part]

                def pair(q):
                    for u in range(2):
                        for part in ORDER:
                            load((q, u), part, q * 6 + (U_MOE[layer] - 6 + 3 * u + done[part]))

                load((0, 0), "gate", None)
                load((0, 0), "up", None)
                if layer == 0:
                    sp.wait_ge(b_taken, KC)
                else:
                    sp.wait_ge(av_done, len(STEPS))
                    expert_load(layer, "down", bass.ds(0, 1), lead_down, lead_down_landed)
                expert_load(layer, "up", bass.ds(0, 1), lead_w[:, 1, :], lead_landed)
                sp.wait_ge(unit_used, U_MOE[layer])
                expert_load(layer, "gate", bass.ds(0, 1), lead_w[:, 0, :], lead_landed)
                if layer == 0:
                    expert_load(layer, "down", bass.ds(0, 1), lead_down, lead_down_landed)
                nt = tiles_of(layer)
                sp.wait_ge(hn_stored[layer][(nt - 1) % 2], 16 * ((nt + 1) // 2))
                load((0, 0), "down", None)
                for b in range(2):
                    sp.wait_ge(gathered[layer][b], 16)
                for part in ORDER:
                    load((0, 1), part, None)
                with sp.Fori(1, PAIRS - 1) as q:
                    pair(q)
                for part in ORDER:
                    load((PAIRS - 1, 0), part, (PAIRS - 1) * 6 + U_MOE[layer] - 6 + done[part])
                more = load_more(sp, layer)
                with sp.If(more > 0):
                    sp.wait_ge(more_steps[layer], MORE_STEPS)
                    with sp.Fori(0, more) as b:
                        ex = sp.value_load(more_i[0:1, 1, bass.ds(b, 1)], min_val=0, max_val=E - 1)
                        sp.wait_ge(more_down[layer], b + 1)
                        for j, part in enumerate(ORDER):
                            expert_load(layer, part, bass.ds(ex, 1), (lead_w[:, 0, :], lead_w[:, 1, :], lead_down)[j], more_w_landed[layer])
                sp.nop()

            experts(0)
            wkv = w_kv.rearrange("(p k) n -> p k n", k=KC)
            for f in range(4):
                if f == 1:
                    for t in range(NX + 1):
                        sp.wait_ge(y_landed[0][t], 32)
                split_unit(U_KVQ + 2 * f, wkv[:, :, f * W:(f + 1) * W])
            wq = b_w_q[0].rearrange("(p k) n -> p k n", k=KC)
            for f in range(2):
                split_unit(U_KVQ + 8 + 2 * f, wq[:, :, f * W:(f + 1) * W])
            free_at[U_QT % RING] = U_QT + 1
            wo = b_w_out[0].rearrange("(k p) n -> p k n", p=P)
            for f in range(2):
                split_unit(U_BOUT + 2 * f, wo[:, :, f * W:(f + 1) * W])
            experts(1)
            sp.wait_ge(o_ready, NX)
            sp.dma_start(final_gain, final_norm.partition_broadcast(P)).then_inc(final_landed, 16)
            for t in range(NX):
                sp.wait_ge(final_ready, t + 1)
                sp.dma_start(out[0, t * P:(t + 1) * P, :], result[:, t, :]).then_inc(stored[t % 2], 16)
            for b in range(2):
                sp.wait_ge(stored[b], 16 * NX // 2)

        @block.gpsimd
        def _(pool):
            def alone():
                pool.sem_inc(passed, 1)

            for i, g in enumerate((ffn_norm[0], kv_norm, ffn_norm[1], b_norm[0])):
                pool.dma_start(gain[:, 1 + i, :], g.rearrange("(p k) -> p k", k=KC)).then_inc(param_landed, 16)
            for l in range(2):
                pool.dma_start(block_gain[:, l, :].rearrange("p (a c) -> p a c", a=2),
                              ffn_norm[l].rearrange("(a p c) -> p a c", a=2, c=KC // 2)).then_inc(param_landed, 16)
            for l in range(2):
                a = l * KC * (G + E)
                pool.dma_start(stage[:, a:a + KC * G], r_group[l].rearrange("(p k) n -> p (k n)", k=KC)).then_inc(param_landed, 16)
                pool.dma_start(stage[:, a + KC * G:a + KC * (G + E)], r_expert[l].rearrange("(p k) n -> p (k n)", k=KC)).then_inc(param_landed, 16)
                pool.dma_start(rbias[:, l, 0:G], r_group_b[l].partition_broadcast(P)).then_inc(param_landed, 16)
                pool.dma_start(rbias[:, l, G:], r_expert_b[l].partition_broadcast(P)).then_inc(param_landed, 16)
            pool.dma_start(stage_conv, a_conv[0].rearrange("w (j p) -> (w j) p", p=P)).then_inc(param_landed, 16)
            pool.dma_start(subln[:, :], b_subln[0].rearrange("(p o) -> p o", o=1)).then_inc(param_landed, 16)
            pool.dma_start(stage_lam, b_lambda[0].rearrange("a b -> (a b)").partition_broadcast(P)).then_inc(param_landed, 16)

            pool.wait_ge(param_landed, 16 * N_PARAM)
            for l in range(2):
                a = l * KC * (G + E)
                nc.gpsimd.tensor_copy(wr[:, l, :, 0:G], stage[:, a:a + KC * G].rearrange("p (k n) -> p k n", k=KC)).then_inc(params_ready, 1)
                nc.gpsimd.tensor_copy(wr[:, l, :, G:], stage[:, a + KC * G:a + KC * (G + E)].rearrange("p (k n) -> p k n", k=KC)).then_inc(params_ready, 1)

            def root_heads(i):
                pool.wait_ge(heads_meaned, i + 1)
                nc.gpsimd.tensor_tensor(small[:, 32:40], small[:, 24:32], cst("minus_half"), ALU.pow).then_inc(heads_rooted, 1)
                pool.wait_ge(heads_rooted, i + 1)

            def moe(layer):
                nt = tiles_of(layer)
                for t in range(nt):
                    pool.wait_ge(scaled, 5 * (1 + 2 * layer) + t + 1)
                    pool.dma_start(hn_dram[layer][t * P:t * P + rows(t), :], nat[0:rows(t), t % 2, :]).then_inc(hn_stored[layer][t % 2], 16)
                for b in range(2):
                    pool.wait_ge(hn_stored[layer][b], 16 * ((nt + 1 - b) // 2))
                pool.wait_ge(rows_ready, 2 * (layer + 1))

                def gather(b, column, n):
                    nc.gpsimd.tensor_copy(src_now[:, b:b + 1], src_row[:, bass.ds(column, 1)]).then_inc(index_set[layer], 1)
                    pool.wait_ge(index_set[layer], n + 1)
                    alone()
                    pool.indirect_dma_start(nat[:, b, 0:DH], None, hn_halves[layer], bass.IndirectOffsetOnAxis(src_now[:, b:b + 1], 0),
                                            bounds_check=2 * (LEN, SEQ)[layer] - 1, oob_is_err=False).then_inc(gathered[layer][b], 16)

                def pair(q, first, last):
                    for u in range(2):
                        n = q * 4 + 2 + 2 * u if not last else q * 4 + 2 + u
                        pool.wait_ge(y_ready, E * layer + q * 2 + u + 1)
                        if not first:
                            pool.wait_ge(scattered[layer][u], q * 16)
                        nc.gpsimd.tensor_copy(dst_now[:, u:u + 1], dst_row[:, bass.ds(q * 2 + u, 1)]).then_inc(index_set[layer], 1)
                        pool.wait_ge(index_set[layer], n + 1)
                        alone()
                        pool.indirect_dma_start(y_halves[layer], bass.IndirectOffsetOnAxis(dst_now[:, u:u + 1], 0), y_out[:, u, :], None,
                                                bounds_check=4 * SPREAD - 1, oob_is_err=False).then_inc(scattered[layer][u], 16)
                        if not last:
                            pool.wait_ge(x_turned, E * layer + q * 2 + u + 1)
                            gather(u, q * 2 + u + 2, n + 1)

                gather(0, 0, 0)
                gather(1, 1, 1)
                pair(0, True, False)
                with pool.Fori(1, PAIRS - 1) as q:
                    pair(q, False, False)
                pair(PAIRS - 1, False, True)
                for b in range(2):
                    pool.wait_ge(scattered[layer][b], 16 * PAIRS)

                more = load_more(pool, layer)
                with pool.If(more > 0):
                    pool.wait_ge(more_steps[layer], MORE_STEPS)
                    pool.wait_ge(more_rows[layer], 2)
                    with pool.Fori(0, more) as b:
                        column = pool.value_load(more_i[0:1, 0, bass.ds(b, 1)], min_val=0, max_val=(NBLK - 1) * E - 1)
                        nc.gpsimd.tensor_copy(src_now[:, 0:1], src_more[:, bass.ds(column, 1)]).then_inc(more_index[layer], 1)
                        nc.gpsimd.tensor_copy(dst_now[:, 0:1], dst_more[:, bass.ds(column, 1)]).then_inc(more_index[layer], 1)
                        pool.wait_ge(more_index[layer], b * 2 + 2)
                        alone()
                        pool.indirect_dma_start(nat[:, 0, 0:DH], None, hn_halves[layer], bass.IndirectOffsetOnAxis(src_now[:, 0:1], 0),
                                                bounds_check=2 * (LEN, SEQ)[layer] - 1, oob_is_err=False).then_inc(more_gathered[layer], 16)
                        pool.wait_ge(more_y[layer], b + 1)
                        alone()
                        pool.indirect_dma_start(y_halves[layer], bass.IndirectOffsetOnAxis(dst_now[:, 0:1], 0), y_out[:, 0, :], None,
                                                bounds_check=4 * SPREAD - 1, oob_is_err=False).then_inc(more_scattered[layer], 16)
                        pool.wait_ge(more_scattered[layer], b * 16 + 16)
                pool.nop()
                for t in range(nt):
                    for k in range(2):
                        pool.dma_start(y_in(t, k), y_dram[layer][k * SPREAD + t * P:k * SPREAD + t * P + rows(t), :]
                                       ).then_inc(y_landed[layer][t], 16)

            moe(0)
            pool.wait_ge(combined[0], NX + 1)
            nc.gpsimd.memset(V[:, NX, :], 0.0).then_inc(v_cleared, 1)
            pool.wait_ge(proj_done, len(JOBS))
            nc.gpsimd.memset(metaT, 0.0).then_inc(pads_clear, 1)
            nc.gpsimd.memset(q_pad, 0.0).then_inc(pads_clear, 1)
            pool.wait_ge(pads_clear, 2)
            pool.wait_ge(rot_copied, len(ROT_JOBS))
            for n, (i, hh) in enumerate(STEPS):
                if n >= 2:
                    pool.wait_ge(scores_done, 2 * (n - 1))
                for c in range(2):
                    nc.gpsimd.tensor_copy(q_pad[c * HD:(c + 1) * HD, n % 2, c, :], qT[c * HD:(c + 1) * HD, hh, i * P:(i + 1) * P]
                                          ).then_inc(q_padded, 1)
                if n >= NH and n % NH == 5:
                    pool.wait_ge(q_padded, 2 * n + 2)
                    root_heads(n // NH - 1)
            pool.wait_ge(q_padded, 2 * len(STEPS))
            root_heads(NX - 1)
            moe(1)

        @block.scalar
        def _(act):
            step = Tally(act, act_step)
            def root_mean_square(phase, t):
                r = rows(t)
                step.order(nc.scalar.activation(nat[0:r, t % 2, :], h[0:r, t, :], ACT.Square, scale=1.0 / math.sqrt(D),
                                                accum_out=ssq[0:r, t:t + 1]))
                nc.scalar.activation(ssq[0:r, t:t + 1], ssq[0:r, t:t + 1], ACT.Sqrt, bias=cst("eps", r)).then_inc(squared, 1)

            def norm_tile(phase, t):
                measure_tile(phase, t)
                scale_tile(phase, t)

            def measure_tile(phase, t):
                if t >= 2:
                    act.wait_ge(turned[phase], t - 1)
                    if phase in (1, 3):
                        act.wait_ge(hn_stored[(phase - 1) // 2][t % 2], 16 * (t // 2))
                root_mean_square(phase, t)

            def scale_tile(phase, t):
                r = rows(t)
                act.wait_ge(rstd_ready, 5 * phase + t + 1)
                nc.scalar.activation(nat[0:r, t % 2, :], h[0:r, t, :], ACT.Copy, scale=rstd[0:r, t:t + 1]).then_inc(scaled, 1)

            def weight_high(i):
                src, _, high, n, n_high = weight_piece(i)
                landed(act, n)
                if n_high is None:
                    if i >= 2:
                        act.wait_ge(in_done, i - 1)
                elif n_high >= RING:
                    act.wait_ge(unit_used, n_high - RING + 1)
                if S_KVQ <= i < S_BOUT:
                    f, q = divmod(i - S_KVQ, QUARTERS)
                    for k in range(2):
                        part = src[:, k * W:(k + 1) * W]
                        nc.scalar.activation(part, part, ACT.Copy, scale=gain[:, 2 if f < 4 else 4, 2 * q + k:2 * q + k + 1]).then_inc(act_step, 1)
                    step.n += 2
                    act.wait_ge(act_step, step.n)
                nc.scalar.copy(high, src).then_inc(w_high_ready, 1)

            def act_high(i):
                group, t = divmod(i, NX + 1)
                if group == 0:
                    act.wait_ge(turned_out[0], t + 1)
                elif group == 1:
                    act.wait_ge(b_taken, KC)
                elif group == 2:
                    act.wait_ge(turned[2], t + 1)
                else:
                    act.wait_ge(oT_copied, t + 1)
                src, high, _ = act_tile(i)
                nc.scalar.copy(high, src).then_inc(act_high_ready, 1)

            act.wait_ge(const_landed, 32)
            for t in range(NX + 1):
                act.wait_ge(x_landed[t], 16)
                measure_tile(0, t)
                if t >= 2:
                    act_high(t - 2)
                scale_tile(0, t)
            act_high(NX - 1)
            weight_high(0)
            act_high(NX)
            weight_high(1)

            for j in range(KC):
                weight_high(3 * j + 2)
                act.wait_ge(in_done, 3 * j + 1)
                if j >= 2:
                    act.wait_ge(u_taken, j - 1)
                g = 2 * ((3 * j) % 4)
                nc.scalar.copy(c_gate[:, j % 2, :].rearrange("p (a n) -> p a n", a=2), ps[:, g:g + 2, 0:HALF]).then_inc(c_copied, 1)
                for i in (3 * j + 3, 3 * j + 4):
                    if i < S_AOUT:
                        weight_high(i)
                for q in A_OUT_AT.get(j, ()):
                    weight_high(S_AOUT + q)
            act_high(T_OUT)
            for q in range(QUARTERS):
                weight_high(S_AOUT + QUARTERS + q)

            def moe(layer):
                for t in range(tiles_of(layer)):
                    if t + 1 < tiles_of(layer):
                        act_high((T_OUT, T_BOUT)[layer] + t + 1)
                    act.wait_ge(mixed, (NX + 1) * layer + t + 1)
                    norm_tile(1 + 2 * layer, t)
                for k in range(2):
                    act.wait_ge(shifted, 2 * layer + k + 1)
                    e_view = (cand[:, 0:tiles_of(layer), 0:G], rv[:, 3, 0:tiles_of(layer)])[k]
                    nc.scalar.activation(e_view, e_view, ACT.Exp).then_inc(exped, 1)
                    if (layer, k) == (0, 0):
                        act.wait_ge(lam_ready, 1)
                        nc.scalar.activation(lam[:, 2:4], lam[:, 0:2], ACT.Exp).then_inc(lam_exp, 1)

                def pair(q, first):
                    for u in range(2):
                        base, lead = U_MOE[layer] + 3 * (u - 1), first and u == 0
                        if lead:
                            act.wait_ge(lead_used, 2 * layer + 1)
                        else:
                            act.wait_ge(unit_used, q * 6 + base + 2)
                        nc.scalar.activation(silu[:, u, :], ps[:, 2 + u, 0:FE // 2], ACT.Silu).then_inc(silu_ready, 1)
                        act.wait_ge(hidden_turned, E * layer + q * 2 + u + 1)
                        nc.scalar.copy(hT[:, u, :], ps[:, 4 + u, 0:FE // 2]).then_inc(hT_ready, 1)
                        if lead:
                            act.wait_ge(lead_used, 2 * layer + 2)
                        else:
                            act.wait_ge(unit_used, q * 6 + base + 3)
                        if not first:
                            act.wait_ge(scattered[layer][u], q * 16)
                        nc.scalar.copy(y_out[:, u, :], ps[:, 6 + u, :]).then_inc(y_ready, 1)

                pair(0, True)
                with act.Fori(1, PAIRS) as q:
                    pair(q, False)
                more = load_more(act, layer)
                with act.If(more > 0):
                    act.wait_ge(scattered[layer][0], 16 * PAIRS)
                    with act.Fori(0, more) as b:
                        act.wait_ge(more_up[layer], b + 1)
                        nc.scalar.activation(silu[:, 0, :], ps[:, 2, 0:FE // 2], ACT.Silu).then_inc(more_silu[layer], 1)
                        act.wait_ge(more_h_turned[layer], b + 1)
                        nc.scalar.copy(hT[:, 0, :], ps[:, 4, 0:FE // 2]).then_inc(more_hT[layer], 1)
                        act.wait_ge(more_down[layer], b + 2)
                        nc.scalar.copy(y_out[:, 0, :], ps[:, 6, :]).then_inc(more_y[layer], 1)
                act.nop()

            moe(0)
            for q in range(QUARTERS):
                weight_high(S_KVQ + q)
            for t in range(NX + 1):
                act.wait_ge(combined[0], t + 1)
                norm_tile(2, t)
                act_high(T_KVQ + t)
            for p, (kind, f, t) in enumerate(JOBS):
                r = rows(t)
                act.wait_ge(proj_done, p + 1)
                if kind == "v":
                    if f == 0 and t == NX:
                        act.wait_ge(v_cleared, 1)
                    dst = V[0:r, t, f * W:(f + 1) * W]
                else:
                    n = ROT_JOBS.index(p)
                    if n >= 2:
                        act.wait_ge(rot_turned, n - 1)
                    dst = knat[0:r, n % 2, :]
                nc.scalar.copy(dst, ps[0:r, 4 + p % 4, :]).then_inc(proj_copied, 1)
                if p in SPLIT_AFTER:
                    weight_high(SPLIT_AFTER[p])

            def copy_aT(n):
                i = STEPS[n][0]
                act.wait_ge(a_turned, n + 1)
                if n >= 2:
                    act.wait_ge(av_done, n - 1)
                else:
                    act.wait_ge(pads_clear, 2)
                nc.scalar.copy(probT[n % 2][:, 0:(i + 1) * P], flat[:, 4 * W:4 * W + (i + 1) * P]).then_inc(aT_copied, 1)
                nc.scalar.copy(metaT[0:META, n % 2, :], flat[0:META, 5 * W:5 * W + P]).then_inc(aT_copied, 1)

            def copy_o(i):
                act.wait_ge(av_done, NH * (i + 1))
                if i >= 2:
                    act.wait_ge(o_turned, i - 1)
                nc.scalar.copy(nat[:, i % 2, :], flat[:, 6 * W:8 * W]).then_inc(o_copied, 1)
                act.wait_ge(o_copied, i + 1)
                if i == 0:
                    act.wait_ge(rot_turned, len(ROT_JOBS))
                if i >= 1:
                    act.wait_ge(o_ready, i)
                nc.scalar.activation(square, nat[:, i % 2, :], ACT.Square).then_inc(o_squared, 1)

            for n, (i, hh) in enumerate(STEPS):
                if n >= NH and n % NH == 3:
                    copy_o(n // NH - 1)
                if n >= 3:
                    act.wait_ge(a_turned, n - 2)
                s = score_view(n)
                for c in range(2):
                    act.wait_ge(max_ready, 2 * n + c + 1)
                    nc.scalar.activation(prob[:, n % 3, c, 0:keys(i)], s[:, c, :], ACT.Exp, bias=small[:, 4 + 2 * (n % 2) + c:5 + 2 * (n % 2) + c],
                                         accum_out=small[:, 48 + 2 * (n % 3) + c:49 + 2 * (n % 3) + c]).then_inc(exp_done, 1)
                if n >= 2:
                    copy_aT(n - 2)
                if n in B_OUT_AT:
                    weight_high(B_OUT_AT[n])
            for n in range(len(STEPS) - 2, len(STEPS)):
                copy_aT(n)
            act.wait_ge(scores_done, 2 * len(STEPS))
            act_high(T_BOUT)
            copy_o(NX - 1)
            moe(1)
            for t in range(NX):
                act.wait_ge(combined[1], t + 1)
                if t >= 2:
                    act.wait_ge(act_step, step.n)
                root_mean_square(4, t)

        @block.tensor
        def _(pe):
            mm = nc.tensor.matmul

            def turn(phase, t):
                r = rows(t)
                pe.wait_ge(scaled, 5 * phase + t + 1)
                if t >= 1:
                    if phase == 2:
                        pe.wait_ge(act_low_ready, T_KVQ + t)
                    else:
                        pe.wait_ge(turned_out[phase], t)
                for k in range(KC):
                    last = nc.tensor.transpose(flat[:, k * P:k * P + r], nat[0:r, t % 2, k:D:KC], ident[0:r, 0:r])
                last.then_inc(turned[phase], 1)

            pe.wait_ge(const_landed, 32)
            for t in range(NX + 1):
                turn(0, t)
            pe.wait_ge(act_low_ready, NX + 1)

            for j in range(KC):
                for s in range(3):
                    g = 3 * j + s
                    if g == 2:
                        pe.wait_ge(param_landed, 16 * N_PARAM)
                        nc.tensor.transpose(ps[:, 7, 0:3 * KC], stage_conv, ident[0:3 * KC, 0:3 * KC]).then_inc(conv_turned, 1)
                    if g == 3:
                        pe.wait_ge(conv_ready, 1)
                    pe.wait_ge(w_low_ready, SPLITS[g])
                    if g >= 4:
                        jj, ss = divmod(g - 4, 3)
                        pe.wait_ge((c_copied, u_taken, b_taken)[ss], jj + 1)
                    b = 2 * (g % 4)
                    _, low, high, _, _ = weight_piece(g)
                    for k in range(KC):
                        for i, (w, acts) in enumerate(((high, front_high), (high, act17_low), (low, front_high))):
                            for a in range(2):
                                last = mm(ps[:, b + a, 0:HALF], w[:, k, :], acts[:, k, a * HALF:(a + 1) * HALF],
                                          start=(k == 0 and i == 0), stop=(k == KC - 1 and i == 2))
                    last.then_inc(in_done, 1)
                    if j % 4 == 3:
                        pe.wait_ge(in_done, g + 1)
                        pe.sem_inc(unit_used, 1)

            def product(bank, high, low, n, first_piece):
                w_low, w_high = (chunks(ring_parts[m % RING][:, :]) for m in (n, n + 1))
                for k in range(KC):
                    if first_piece is not None and k % 2 == 0:
                        pe.wait_ge(w_low_ready, SPLITS[first_piece + k // 2])
                    for i, (x, w) in enumerate(((high, w_high), (high, w_low), (low, w_high))):
                        last = mm(bank, x[:, k, :], w[:, k, :], start=(k == 0 and i == 0), stop=(k == KC - 1 and i == 2))
                return last

            def out_proj(layer, t):
                r, n = rows(t), (U_AOUT, U_BOUT)[layer]
                tile = (T_OUT, T_BOUT)[layer] + t
                pe.wait_ge(act_low_ready, tile + 1)
                if t >= 2:
                    pe.wait_ge(mixed, (NX + 1) * layer + t - 1)
                b = 4 + 2 * (t % 2)
                _, high, low = act_tile(tile)
                for f in range(2):
                    last = product(ps[0:r, b + f, :], high, low, n + 2 * f, (S_AOUT, S_BOUT)[layer] + f * QUARTERS if t == 0 else None)
                last.then_inc(out_done, 1)

            def logits(layer, t):
                r = rows(t)
                pe.wait_ge(turned_out[1 + 2 * layer], t + 1)
                a = cols(t)[0]
                for k in range(KC):
                    last = mm(ps[0:r, 2, t * (G + E):(t + 1) * (G + E)], actT[:, k, a:a + r], wr[:, layer, k, :],
                              start=(k == 0), stop=(k == KC - 1))
                last.then_inc(logits_done, 1)

            def gate_up(b, pair_w):
                for k in range(KC):
                    a, c = divmod(k, KC // 2)
                    x = xT[:, b, (2 * c + a) * C:(2 * c + a + 1) * C]
                    for f in range(2):
                        w = pair_w[:, :, k * FE + f * FE // 2:k * FE + (f + 1) * FE // 2]
                        last = mm(ps[f * C:(f + 1) * C, 2 + b, :].rearrange("p (g n) -> p g n", g=2), x, w, start=(k == 0), stop=(k == KC - 1))
                return last

            def turn_block(b):
                pe.sem_inc(passed, 1)
                for c in range(KC // 2):
                    last = nc.tensor.transpose(ps[:, b, c * P:(c + 1) * P], nat[:, b, c:DH:KC // 2], ident)
                return last

            def turn_hidden(b):
                pe.sem_inc(passed, 1)
                for c in range(2):
                    last = nc.tensor.transpose(ps[:, 4 + b, c * P:(c + 1) * P], hidden[:, b, c * P:(c + 1) * P], ident)
                return last

            def down(b, w):
                for f in range(FC):
                    a, c = divmod(f, 2)
                    for o in range(2):
                        last = mm(ps[o * C:(o + 1) * C, 6 + b, :], hT[:, b, (2 * c + a) * C:(2 * c + a + 1) * C],
                                  w[:, f * D + o * DH:f * D + (o + 1) * DH], start=(f == 0), stop=(f == FC - 1))
                return last

            def table_rows(column, nt):
                for n in range(2 * nt):
                    for f in range(2):
                        last = mm(ps[f * C:(f + 1) * C, 2, column:column + E], at_slot[:, n, :], row_of[:, n, :],
                                  start=(n == 0), stop=(n == 2 * nt - 1))
                return last

            def moe(layer):
                nt = tiles_of(layer)
                ph = 1 + 2 * layer
                for t in range(nt):
                    out_proj(layer, t)
                    if layer == 1 and t == 0:
                        pe.wait_ge(exp_done, 2 * len(STEPS))
                        turn_o(NX - 1)
                        pe.wait_ge(o_copied, NX)
                    if layer == 1 and t == 1:
                        pe.wait_ge(oT_copied, NX)
                    if t == nt - 1:
                        pe.wait_ge(out_done, (NX + 1) * layer + nt)
                        pe.sem_inc(unit_used, 4)
                    if t == 0:
                        pe.wait_ge(params_ready, 4)
                    if t >= 1:
                        turn(ph, t - 1)
                    if t >= 2:
                        logits(layer, t - 2)
                turn(ph, nt - 1)
                logits(layer, nt - 2)
                logits(layer, nt - 1)

                pe.wait_ge(members, layer + 1)
                span = (nt + 1) * E
                mm(ps[:, 3, 0:span], cst("upper"), member[:, 0:nt + 1, :].rearrange("p t e -> p (t e)"), start=True, stop=False)
                mm(ps[:, 3, 0:span], cst("ones"), before[:, 0:nt + 1, :].rearrange("p t e -> p (t e)"), start=False, stop=True
                   ).then_inc(ranked, 1)
                pe.wait_ge(placed, layer + 1)
                table_rows(0, nt).then_inc(tabled, 1)

                def pair(q, first, last_pair):
                    for u in range(2):
                        lead = first and u == 0
                        (gs, gv), (us, uv), (ds, dv) = (expert_unit(layer, q, u, part) for part in ORDER)
                        if lead:
                            pe.wait_ge(lead_landed, 32 * (layer + 1))
                            pe.wait_ge(xT_ready, E * layer + 1)
                            gate_up(0, lead_w).then_inc(lead_used, 1)
                        else:
                            pe.wait_ge(ring_landed[gs], gv)
                            pe.wait_ge(ring_landed[us], uv)
                            pe.wait_ge(xT_ready, E * layer + q * 2 + u + 1)
                            gate_up(u, ring[:, gs:us + 1, :]).then_inc(unit_used, 2)
                        if not (last_pair and u == 1):
                            pe.wait_ge(gathered[layer][1 - u], q * 16 + 16 * (1 + u))
                            turn_block(1 - u).then_inc(x_turned, 1)
                        pe.wait_ge(hidden_ready, E * layer + q * 2 + u + 1)
                        turn_hidden(u).then_inc(hidden_turned, 1)
                        if lead:
                            pe.wait_ge(lead_down_landed, 16 * (layer + 1))
                        else:
                            pe.wait_ge(ring_landed[ds], dv)
                        if not first:
                            pe.wait_ge(y_ready, E * layer + q * 2 + u - 1)
                        pe.wait_ge(hT_ready, E * layer + q * 2 + u + 1)
                        if lead:
                            down(0, lead_down).then_inc(lead_used, 1)
                        else:
                            down(u, ring[:, ds, :]).then_inc(unit_used, 1)

                pe.wait_ge(gathered[layer][0], 16)
                turn_block(0).then_inc(x_turned, 1)
                pair(0, True, False)
                with pe.Fori(1, PAIRS - 1) as q:
                    pair(q, False, False)
                pair(PAIRS - 1, False, True)

                more = load_more(pe, layer)
                with pe.If(more > 0):
                    pe.wait_ge(y_ready, E * layer + E)
                    pe.sem_inc(more_down[layer], 1)
                    for b in range(1, NBLK):
                        pe.wait_ge(more_hot[layer], b)
                        table_rows((b - 1) * E, nt).then_inc(more_tabled[layer], 1)
                    with pe.Fori(0, more) as b:
                        pe.wait_ge(more_gathered[layer], b * 16 + 16)
                        turn_block(0).then_inc(more_turned[layer], 1)
                        pe.wait_ge(more_xT[layer], b + 1)
                        pe.wait_ge(more_w_landed[layer], b * 48 + 48)
                        gate_up(0, lead_w).then_inc(more_up[layer], 1)
                        pe.wait_ge(more_hidden[layer], b + 1)
                        turn_hidden(0).then_inc(more_h_turned[layer], 1)
                        pe.wait_ge(more_hT[layer], b + 1)
                        down(0, lead_down).then_inc(more_down[layer], 1)
                pe.nop()

            moe(0)

            def project(p):
                kind, f, t = JOBS[p]
                r = rows(t)
                u = p // 5 if kind != "q" else 4 + f
                if p >= 4:
                    pe.wait_ge(proj_copied, p - 3)
                if p <= NX:
                    pe.wait_ge(act_low_ready, T_KVQ + t + 1)
                _, high, low = act_tile(T_KVQ + t)
                last = product(ps[0:r, 4 + p % 4, :], high, low, U_KVQ + 2 * u, S_KVQ + u * QUARTERS if t == 0 else None)
                last.then_inc(proj_done, 1)
                if t == (NX - 1 if kind == "q" else NX):
                    pe.wait_ge(proj_done, p + 1)
                    pe.sem_inc(unit_used, 2)

            def turn_rot(n):
                _, f, t = JOBS[ROT_JOBS[n]]
                r = rows(t)
                pe.wait_ge(roped, n + 1)
                if n >= 2:
                    pe.wait_ge(rot_copied, n - 1)
                for c in range(4):
                    last = nc.tensor.transpose(ps[:, 2 + n % 2, c * P:c * P + r], knat[0:r, n % 2, c * P:(c + 1) * P], ident[0:r, 0:r])
                last.then_inc(rot_turned, 1)

            turn(2, 0)
            turn(2, 1)
            nrot = 0
            for p in range(len(JOBS)):
                project(p)
                if p + 2 <= NX:
                    turn(2, p + 2)
                while p >= NX - 1 and nrot < len(ROT_JOBS) and ROT_JOBS[nrot] <= p - 1:
                    turn_rot(nrot)
                    nrot += 1
            while nrot < len(ROT_JOBS):
                turn_rot(nrot)
                nrot += 1

            def scores(n):
                i, hh = STEPS[n]
                s = score_view(n)
                pe.wait_ge(q_padded, 2 * n + 2)
                for c in range(2):
                    if i == NX - 1:
                        pe.wait_ge(exp_done, 2 * n - 1 + c)
                    elif n >= 2 and c == 0:
                        pe.wait_ge(exp_done, 2 * (n - 1))
                    q = q_pad[:, n % 2, c, :]
                    for a in range(0, keys(i), W):
                        b = min(a + W, keys(i))
                        last = mm(s[:, c, a:b], q, kT[:, hh, a:b], start=True, stop=True)
                    last.then_inc(scores_done, 1)

            def turn_a(n):
                i = STEPS[n][0]
                pe.wait_ge(a_ready, n + 1)
                if n >= 1:
                    pe.wait_ge(aT_copied, 2 * n)
                for j in range(i + 1):
                    nc.tensor.transpose(flat[:, 4 * W + j * P:4 * W + (j + 1) * P], prob[:, n % 3, 0, META + j * P:META + (j + 1) * P], ident)
                nc.tensor.transpose(ps[:, 5, 0:P], prob[:, n % 3, 0, 0:P], ident).then_inc(a_turned, 1)

            def weigh(n):
                i, hh = STEPS[n]
                pe.wait_ge(aT_copied, 2 * n + 2)
                if hh == 0 and i >= 1:
                    pe.wait_ge(o_copied, i)
                o = flat[:, 6 * W + hh * P:6 * W + (hh + 1) * P]
                mm(o, metaT[:, n % 2, :], V[:, NX, hh * P:(hh + 1) * P], start=True, stop=False)
                for j in range(i + 1):
                    last = mm(o, probT[n % 2][:, j * P:(j + 1) * P], V[:, j, hh * P:(hh + 1) * P], start=False, stop=(j == i))
                last.then_inc(av_done, 1)

            def turn_o(i):
                pe.wait_ge(o_ready, i + 1)
                b = O_BANK[i]
                for k in range(KC):
                    last = nc.tensor.transpose(flat[:, b * W + k * P:b * W + (k + 1) * P], nat[:, i % 2, k * P:(k + 1) * P], ident)
                last.then_inc(o_turned, 1)

            pe.wait_ge(rot_copied, len(ROT_JOBS))
            pe.wait_ge(proj_copied, len(JOBS))
            last_n = len(STEPS) - 1
            for n in range(len(STEPS) + 3):
                if n <= last_n:
                    scores(n)
                if n == last_n:
                    pe.sem_inc(unit_used, 1)
                if NH <= n <= last_n and n % NH == 7:
                    pe.wait_ge(aT_copied, 2 * (n - 2))
                    turn_o(n // NH - 1)
                    pe.wait_ge(oT_copied, n // NH)
                if 2 <= n <= last_n + 2:
                    turn_a(n - 2)
                if n >= 3:
                    weigh(n - 3)
            moe(1)

        @block.vector
        def _(dve):
            v = nc.vector
            step = Tally(dve, dve_step)
            order = step.order

            def rstd_tile(phase, t):
                r = rows(t)
                dve.wait_ge(squared, 5 * phase + t + 1)
                v.reciprocal(rstd[0:r, t:t + 1], ssq[0:r, t:t + 1]).then_inc(rstd_ready, 1)

            def gained(dst, t, g):
                r = rows(t)
                return v.tensor_tensor(dst, flat[:, 0:KC * P].rearrange("p (k n) -> p k n", k=KC)[:, :, 0:r],
                                       bcast(gain[:, g, :], r, 2), ALU.mult)

            def weight_low(i):
                src, low, high, _, _ = weight_piece(i)
                dve.wait_ge(w_high_ready, SPLITS[i])
                v.tensor_tensor(low, src, high, ALU.subtract).then_inc(w_low_ready, 1)

            def act_low(i):
                src, high, low = act_tile(i)
                dve.wait_ge(act_high_ready, i + 1)
                return v.tensor_tensor(low, src, high, ALU.subtract).then_inc(act_low_ready, 1)

            dve.wait_ge(const_landed, 32)
            rstd_tile(0, 0)
            for t in range(NX + 1):
                if t < NX:
                    rstd_tile(0, t + 1)
                dve.wait_ge(turned[0], t + 1)
                gained(actT[:, :, cols(t)[0]:cols(t)[1]], t, 0).then_inc(turned_out[0], 1)
                if t >= 1:
                    act_low(t - 1)
            act_low(NX)
            weight_low(0)
            weight_low(1)
            dve.wait_ge(param_landed, 16 * N_PARAM)
            order(v.tensor_scalar(gain[:, 4, :], gain[:, 4, :], HD ** -0.5, None, ALU.mult))
            lp = stage_lam.rearrange("p (a b d) -> p a b d", a=2, b=2)
            order(v.tensor_tensor(lp[:, :, 0, :], lp[:, :, 0, :], lp[:, :, 1, :], ALU.mult))
            v.tensor_reduce(lam[:, 0:2], lp[:, :, 0, :], AX, ALU.add).then_inc(lam_ready, 1)
            order(v.tensor_scalar(subln[:, :], subln[:, :], 1.0 - LAM_INIT, None, ALU.mult))

            order(v.memset(cu[:, 0:2], 0.0))
            halves = lambda ap: ap.rearrange("p (a n) -> p a n", a=2)
            for j in range(KC):
                g = 3 * j + 1
                b = 2 * (g % 4)
                weight_low(3 * j + 2)
                if j == 0:
                    dve.wait_ge(conv_turned, 1)
                    v.tensor_copy(conv[:, :], ps[:, 7, 0:3 * KC]).then_inc(conv_ready, 1)
                    dve.wait_ge(conv_ready, 1)
                dve.wait_ge(c_copied, j + 1)
                dve.wait_ge(in_done, g + 1)
                v.tensor_tensor(halves(cu[:, 2:]), halves(c_gate[:, j % 2, :]), ps[:, b:b + 2, 0:HALF], ALU.mult).then_inc(u_taken, 1)
                if 3 * j + 3 < S_AOUT:
                    weight_low(3 * j + 3)
                dve.wait_ge(u_taken, j + 1)
                order(v.tensor_scalar(z, cu[:, 0:LEN], conv[:, j:j + 1], None, ALU.mult))
                for k in (1, 2):
                    order(v.scalar_tensor_tensor(z, cu[:, k:k + LEN], conv[:, k * KC + j:k * KC + j + 1], z, ALU.mult, ALU.add))
                if 3 * j + 4 < S_AOUT:
                    weight_low(3 * j + 4)
                for q in A_OUT_AT.get(j, ()):
                    weight_low(S_AOUT + q)
                b = 2 * ((g + 1) % 4)
                dve.wait_ge(in_done, g + 2)
                v.tensor_tensor(halves(actT2[:, j, :]), halves(z), ps[:, b:b + 2, 0:HALF], ALU.mult).then_inc(b_taken, 1)
                dve.wait_ge(b_taken, j + 1)

            act_low(T_OUT)
            for q in range(QUARTERS):
                weight_low(S_AOUT + QUARTERS + q)

            def first_max(vals, n, width, top, index, onehot):
                tmp = work[:, 0:n, 0:width]
                iota = bcast(cst("iota")[:, 0:width], n, 1)
                order(v.tensor_reduce(top, vals, AX, ALU.max))
                order(v.tensor_tensor(tmp, vals, bcast(top, width, 2), ALU.is_equal))
                order(v.scalar_tensor_tensor(tmp, tmp, -100.0, bcast(cst("iota100")[:, 0:width], n, 1), ALU.mult, ALU.add))
                order(v.tensor_reduce(index, tmp, AX, ALU.min))
                order(v.tensor_tensor(onehot, iota, bcast(index, width, 2), ALU.is_equal))

            def moe(layer):
                nt = tiles_of(layer)
                ph = 1 + 2 * layer

                def add_tile(t):
                    r, b = rows(t), 4 + 2 * (t % 2)
                    dve.wait_ge(out_done, (NX + 1) * layer + t + 1)
                    v.tensor_tensor(h[0:r, t, :], h[0:r, t, :], flat[0:r, b * W:(b + 2) * W], ALU.add).then_inc(mixed, 1)

                def take_tile(t):
                    dve.wait_ge(turned[ph], t + 1)
                    gained(actT[:, :, cols(t)[0]:cols(t)[1]], t, ph).then_inc(turned_out[ph], 1)

                for t in range(nt):
                    if t + 1 < nt:
                        act_low((T_OUT, T_BOUT)[layer] + t + 1)
                    add_tile(t)
                    if t >= 1:
                        take_tile(t - 1)
                    rstd_tile(ph, t)
                take_tile(nt - 1)

                dve.wait_ge(logits_done, (NX + 1) * layer + nt)
                lg = ps[:, 2, 0:nt * (G + E)].rearrange("p (t n) -> p t n", t=nt)
                if nt > NX:
                    order(v.memset(logit[:, NX, :], 0.0))
                    v.tensor_tensor(logit[0:META, NX, :], lg[0:META, NX, :], rbias[0:META, layer, :], ALU.add).then_inc(dve_step, 1)
                    step.n += 1
                order(v.tensor_tensor(logit[:, 0:NX, :], lg[:, 0:NX, :], bcast(rbias[:, layer, :], NX, 1), ALU.add))
                L = logit[:, 0:nt, :]
                gtop, gidx, psum_g, e1 = rv[:, 0, 0:nt], rv[:, 1, 0:nt], rv[:, 2, 0:nt], rv[:, 3, 0:nt]
                v0, v1, i0, i1, pg = (rv[:, c, 0:nt] for c in range(4, 9))
                ghot = hot[:, 0, 0:nt, 0:G]
                first_max(L[:, :, 0:G], nt, G, gtop, gidx, ghot)
                ex = cand[:, 0:nt, 0:G]
                v.tensor_tensor(ex, L[:, :, 0:G], bcast(gtop, G, 2), ALU.subtract).then_inc(shifted, 1)
                prod = work[:, 0:nt, :]
                order(v.tensor_tensor(prod.rearrange("p t (g e) -> p t g e", g=G), L[:, :, G:].rearrange("p t (g e) -> p t g e", g=G),
                                      bcast(ghot, EPG, 3), ALU.mult))
                sel = leg[:, 0:nt, :]
                order(v.tensor_reduce(sel, prod.rearrange("p t (g e) -> p t e g", g=G), AX, ALU.add))
                oh = hot[:, 0, 0:nt, :]
                first_max(sel, nt, EPG, v0, i0, oh)
                order(v.scalar_tensor_tensor(sel, oh, -3.0e38, sel, ALU.mult, ALU.add))
                first_max(sel, nt, EPG, v1, i1, oh)
                v.tensor_tensor(e1, v1, v0, ALU.subtract).then_inc(shifted, 1)
                eid = rv[:, 10:12, 0:nt]
                for k, ik in enumerate((i0, i1)):
                    order(v.scalar_tensor_tensor(eid[:, k, :], gidx, float(EPG), ik, ALU.mult, ALU.add))
                ch = chosen[:, 0:2 * nt, :]
                for k in range(2):
                    order(v.tensor_tensor(ch[:, k * nt:(k + 1) * nt, :], bcast(cst("iota"), nt, 1), bcast(eid[:, k, :], E, 2), ALU.is_equal))
                order(v.tensor_tensor(member[:, 0:nt, :], ch[:, 0:nt, :], ch[:, nt:2 * nt, :], ALU.add))
                if nt > NX:
                    order(v.tensor_scalar(member[:, NX, :], member[:, NX, :], cst("head"), None, ALU.mult))
                order(v.memset(member[:, nt, :], 0.0))
                order(v.memset(before[:, 0, :], 0.0))
                for t in range(nt):
                    order(v.tensor_tensor(before[:, t + 1, :], before[:, t, :], member[:, t, :], ALU.add))
                dve.sem_inc(members, 1)
                for k in range(2):
                    order(v.tensor_tensor(row_of[:, k * nt:(k + 1) * nt, :], ch[:, k * nt:(k + 1) * nt, :],
                                          bcast(cst("row")[:, 5 * k:5 * k + nt], E, 2), ALU.mult))
                dve.wait_ge(ranked, layer + 1)
                rank = ps[:, 3, 0:nt * E].rearrange("p (t e) -> p t e", t=nt)
                for k in range(2):
                    order(v.tensor_tensor(work[:, k * nt:(k + 1) * nt, :], ch[:, k * nt:(k + 1) * nt, :], rank, ALU.mult))
                ranks = rank_of[:, 0:2 * nt]
                order(v.tensor_reduce(ranks, work[:, 0:2 * nt, :], AX, ALU.add))
                v.tensor_tensor(at_slot[:, 0:2 * nt, :], bcast(cst("slot"), 2 * nt, 1), bcast(ranks, C, 2), ALU.is_equal).then_inc(placed, 1)
                order(v.tensor_copy(counted[:, :], ps[0:1, 3, nt * E:(nt + 1) * E]))
                flags = spread.rearrange("p (b e) -> p b e", e=E)
                order(v.tensor_tensor(flags, cst("more", 1).rearrange("p (b e) -> p b e", e=E), bcast(counted[:, :], NBLK - 1, 1), ALU.is_lt))
                order(v.tensor_reduce(n_more[:, 0:1], spread, AX, ALU.add))
                v.tensor_copy(n_more_i[:, :], n_more[:, 0:1]).then_inc(more_known, 1)
                dve.wait_ge(exped, 2 * layer + 1)
                order(v.tensor_reduce(psum_g, ex, AX, ALU.add))
                order(v.reciprocal(pg, psum_g))
                dve.wait_ge(exped, 2 * layer + 2)
                den = rv[:, 9, 0:nt]
                order(v.tensor_scalar(den, e1, 1.0, None, ALU.add))
                order(v.reciprocal(den, den))
                order(v.tensor_tensor(gate[:, 0, 0:nt], pg, den, ALU.mult))
                order(v.tensor_tensor(gate[:, 1, 0:nt], gate[:, 0, 0:nt], e1, ALU.mult))
                def row_numbers(table, t3, dst, src, note):
                    add, row, fold = (t3[:, c, :] for c in range(3))
                    note(v.tensor_scalar(add, table, 0.0, float(EMPTY), ALU.is_equal, ALU.mult))
                    note(v.scalar_tensor_tensor(row, table, -1.0, add, ALU.add, ALU.add))
                    note(v.tensor_scalar(fold, row, float(SPREAD), -2.0 * SPREAD, ALU.is_ge, ALU.mult))
                    note(v.tensor_scalar(row, row, 2.0, cst("half"), ALU.mult, ALU.add))
                    return v.tensor_copy(dst, row), v.tensor_tensor(src, row, fold, ALU.add)

                dve.wait_ge(tabled, layer + 1)
                for ins in row_numbers(ps[:, 2, 0:E], tab, dst_row[:, :], src_row[:, :], order):
                    ins.then_inc(rows_ready, 1)

                def take_x(b):
                    shape = dict(c=KC // 2, a=2)
                    g = block_gain[:, layer, :].rearrange("p (a c) -> p c a", a=2)
                    return v.tensor_tensor(xT[:, b, :].rearrange("p (c a n) -> p c a n", **shape),
                                           ps[:, b, :].rearrange("p (c a n) -> p c a n", **shape), bcast(g, C, 3), ALU.mult)

                def pair(q, last):
                    for u in range(2):
                        dve.wait_ge(silu_ready, E * layer + q * 2 + u + 1)
                        v.tensor_tensor(hidden[:, u, :], silu[:, u, :], ps[:, 2 + u, FE // 2:], ALU.mult).then_inc(hidden_ready, 1)
                        if not (last and u == 1):
                            dve.wait_ge(x_turned, E * layer + q * 2 + u + 2)
                            take_x(1 - u).then_inc(xT_ready, 1)

                dve.wait_ge(x_turned, E * layer + 1)
                take_x(0).then_inc(xT_ready, 1)
                with dve.Fori(0, PAIRS - 1) as q:
                    pair(q, False)
                pair(PAIRS - 1, True)

                dve.wait_ge(more_known, layer + 1)
                more = load_more(dve, layer)
                with dve.If(more > 0):
                    dve.wait_ge(scattered[layer][0], 16 * PAIRS)
                    dve.wait_ge(scattered[layer][1], 16 * PAIRS)
                    run = scan
                    n0 = 0
                    more_order = more_steps[layer]
                    def mo(ins):
                        nonlocal n0
                        ins.then_inc(more_order, 1)
                        n0 += 1
                        dve.wait_ge(more_order, n0)
                    mo(v.tensor_tensor(flags, cst("more", 1).rearrange("p (b e) -> p b e", e=E), bcast(counted[:, :], NBLK - 1, 1), ALU.is_lt))
                    mo(v.tensor_tensor_scan(run, spread, spread, 0.0, ALU.add, ALU.bypass))
                    for b in range(MAXMORE):
                        mo(v.tensor_scalar(spread, run, float(b), None, ALU.is_le))
                        mo(v.tensor_reduce(small[0:1, 16 + b:17 + b], spread, AX, ALU.add))
                    mo(v.tensor_copy(more_i[:, 0, :], small[0:1, 16:16 + MAXMORE]))
                    mo(v.tensor_scalar(more_i[:, 1, :], more_i[:, 0, :], E - 1, None, ALU.bitwise_and))
                    assert n0 == MORE_STEPS
                    for b in range(1, NBLK):
                        if b > 1:
                            dve.wait_ge(more_tabled[layer], b - 1)
                        mo(v.tensor_scalar(rank_b[:, 0:2 * nt], ranks, -float(b * C), None, ALU.add))
                        v.tensor_tensor(at_slot[:, 0:2 * nt, :], bcast(cst("slot"), 2 * nt, 1), bcast(rank_b[:, 0:2 * nt], C, 2),
                                        ALU.is_equal).then_inc(more_hot[layer], 1)
                    dve.wait_ge(more_tabled[layer], NBLK - 1)
                    for ins in row_numbers(ps[:, 2, 0:(NBLK - 1) * E], tab_more, dst_more, src_more, mo):
                        ins.then_inc(more_rows[layer], 1)
                    with dve.Fori(0, more) as b:
                        dve.wait_ge(more_turned[layer], b + 1)
                        take_x(0).then_inc(more_xT[layer], 1)
                        dve.wait_ge(more_silu[layer], b + 1)
                        v.tensor_tensor(hidden[:, 0, :], silu[:, 0, :], ps[:, 2, FE // 2:], ALU.mult).then_inc(more_hidden[layer], 1)
                dve.nop()

            def combine(layer, t):
                r = rows(t)
                dve.wait_ge(y_landed[layer][t], 32)
                order(v.scalar_tensor_tensor(h[0:r, t, :], y_in(t, 0), gate[0:r, 0, t:t + 1], h[0:r, t, :], ALU.mult, ALU.add))
                v.scalar_tensor_tensor(h[0:r, t, :], y_in(t, 1), gate[0:r, 1, t:t + 1], h[0:r, t, :], ALU.mult, ALU.add
                                       ).then_inc(combined[layer], 1)

            moe(0)

            for q in range(QUARTERS):
                weight_low(S_KVQ + q)
            for t in range(NX + 1):
                combine(0, t)
                if t >= 1:
                    act_low(T_KVQ + t - 1)
                rstd_tile(2, t)
            act_low(T_KVQ + NX)

            def rotate(n):
                p = ROT_JOBS[n]
                _, f, t = JOBS[p]
                r = rows(t)
                dve.wait_ge(proj_copied, p + 1)
                if n:
                    dve.wait_ge(roped, n)
                X = knat[0:r, n % 2, :].rearrange("p (g d) -> p g d", d=HD)[:, :, 0:ROT]
                A = rope[0:r, 0:8 * ROT].rearrange("p (g d) -> p g d", g=8)
                B = rope[0:r, 8 * ROT:16 * ROT].rearrange("p (g d) -> p g d", g=8)
                cc = bcast(cst("cos", r)[:, t * ROT:(t + 1) * ROT], 8, 1)
                ss = bcast(cst("sin", r)[:, t * ROT:(t + 1) * ROT], 8, 1)
                hr = ROT // 2
                order(v.tensor_tensor(A, X, cc, ALU.mult))
                order(v.tensor_tensor(B[:, :, 0:hr], X[:, :, hr:], ss[:, :, 0:hr], ALU.mult))
                order(v.tensor_tensor(B[:, :, hr:], X[:, :, 0:hr], ss[:, :, hr:], ALU.mult))
                v.tensor_tensor(X, A, B, ALU.add).then_inc(roped, 1)

            def take_rot(n):
                kind, f, t = JOBS[ROT_JOBS[n]]
                r = rows(t)
                dve.wait_ge(rot_turned, n + 1)
                dst, a = (kT, cols(t)[0]) if kind == "k" else (qT, t * P)
                src = ps[:, 2 + n % 2, :].rearrange("p (c n) -> p c n", c=4)[:, :, 0:r]
                v.tensor_copy(dst[:, 4 * f:4 * f + 4, a:a + r], src).then_inc(rot_copied, 1)

            for p in range(len(JOBS)):
                if p in ROT_JOBS:
                    n = ROT_JOBS.index(p)
                    rotate(n)
                    if n >= 1:
                        take_rot(n - 1)
                if p in SPLIT_AFTER:
                    weight_low(SPLIT_AFTER[p])
            take_rot(len(ROT_JOBS) - 1)

            dve.wait_ge(lam_exp, 1)
            order(v.tensor_tensor(lam[:, 4:5], lam[:, 3:4], lam[:, 2:3], ALU.subtract))
            order(v.tensor_scalar(lam[:, 5:6], lam[:, 4:5], -LAM_INIT, None, ALU.add))

            def maxima(n):
                i = STEPS[n][0]
                s = score_view(n)
                for c0, c1 in ((0, 2),) if i < NX - 1 else ((0, 1), (1, 2)):
                    dve.wait_ge(scores_done, 2 * n + c1)
                    order(v.memset(s[0:HD, c0:c1, keys(i) - HD:keys(i)], -3.4028235e38))
                    o = 4 + 2 * (n % 2)
                    v.tensor_reduce(small[:, o + c0:o + c1], s[:, c0:c1, :], AX, ALU.max, negate=True).then_inc(max_ready, c1 - c0)

            def difference(n):
                k = keys(STEPS[n][0])
                o = 48 + 2 * (n % 3)
                dve.wait_ge(exp_done, 2 * n + 2)
                if n:
                    dve.wait_ge(a_ready, n)
                order(v.reciprocal(small[:, 12:14], small[:, o:o + 2]))
                order(v.tensor_scalar(prob[:, n % 3, 1, 0:k], prob[:, n % 3, 1, 0:k], small[:, 13:14], lam[:, 5:6], ALU.mult, ALU.mult))
                v.scalar_tensor_tensor(prob[:, n % 3, 0, 0:k], prob[:, n % 3, 0, 0:k], small[:, 12:13], prob[:, n % 3, 1, 0:k],
                                       ALU.mult, ALU.add).then_inc(a_ready, 1)

            def mean_heads(i):
                dve.wait_ge(o_squared, i + 1)
                order(v.tensor_reduce(small[:, 16:24], square.rearrange("p (h d) -> p h d", d=P), AX, ALU.add))
                v.tensor_scalar(small[:, 24:32], small[:, 16:24], 1.0 / P, EPS, ALU.mult, ALU.add).then_inc(heads_meaned, 1)

            def norm_heads(i):
                dve.wait_ge(heads_rooted, i + 1)
                o = nat[:, i % 2, :].rearrange("p (h d) -> p h d", d=P)
                v.tensor_tensor(o, o, bcast(small[:, 32:40], P, 2), ALU.mult).then_inc(o_ready, 1)

            def take_o(i):
                dve.wait_ge(o_turned, i + 1)
                v.tensor_scalar(actT[:, :, i * P:(i + 1) * P], flat[:, O_BANK[i] * W:(O_BANK[i] + 2) * W].rearrange("p (k n) -> p k n", k=KC), subln[:, :], None,
                                ALU.mult).then_inc(oT_copied, 1)

            for n in range(len(STEPS)):
                maxima(n)
                if n >= 1:
                    difference(n - 1)
                if n >= NH and n % NH == 4:
                    mean_heads(n // NH - 1)
                if n >= NH and n % NH == 5:
                    norm_heads(n // NH - 1)
                if n >= NH and n % NH == 7:
                    take_o(n // NH - 1)
                if n - 1 in B_OUT_AT:
                    weight_low(B_OUT_AT[n - 1])
            difference(len(STEPS) - 1)
            act_low(T_BOUT)
            mean_heads(NX - 1)
            norm_heads(NX - 1)
            take_o(NX - 1)

            moe(1)
            dve.wait_ge(final_landed, 16)
            combine(1, 0)
            for t in range(NX):
                if t + 1 < NX:
                    combine(1, t + 1)
                dve.wait_ge(squared, 5 * 3 + NX + t + 1)
                order(v.reciprocal(rstd[:, t:t + 1], ssq[:, t:t + 1]))
                v.scalar_tensor_tensor(result[:, t, :], h[:, t, :], rstd[:, t:t + 1], final_gain, ALU.mult, ALU.mult).then_inc(final_ready, 1)


_INS = ["x", "meta_tokens", "a_norm", "a_w_in", "a_conv", "a_w_out", "kv_norm", "w_kv", "b_norm", "b_w_q", "b_lambda", "b_subln",
        "b_w_out", "ffn_norm", "r_group", "r_group_b", "r_expert", "r_expert_b", "e_gate", "e_up", "e_down", "final_norm"]


def constants():
    import numpy as np

    t = np.zeros((P, NCONST), np.float32)

    def put(name, values):
        a, n = CONST[name]
        t[:, a:a + n] = values

    put("ident", np.eye(P))
    put("upper", np.triu(np.ones((P, P)), 1))
    put("ones", 1.0)
    put("iota", np.arange(E))
    put("iota100", np.arange(EPG) + 100)
    put("more", np.repeat(np.arange(1, NBLK) * C, E))
    half = ROT // 2
    freq = (np.float32(500000.0) ** (-np.arange(half, dtype=np.float32) * np.float32(2.0) / np.float32(ROT))).astype(np.float32)
    pos = np.zeros((5, P), np.float32)
    for i in range(NX):
        pos[i] = META + i * P + np.arange(P)
    pos[NX, :META] = np.arange(META)
    ang = (pos[:, :, None] * freq).astype(np.float32)
    cos, sin = np.cos(ang), np.sin(ang)
    put("cos", np.concatenate([cos, cos], -1).transpose(1, 0, 2).reshape(P, 5 * ROT))
    put("sin", np.concatenate([-sin, sin], -1).transpose(1, 0, 2).reshape(P, 5 * ROT))
    put("eps", EPS)
    put("minus_half", -0.5)
    row = np.arange(5)[None, :] * P + np.arange(P)[:, None]
    there = row < LEN
    put("row", np.concatenate([(row + 1) * there, (row + SPREAD + 1) * there], 1))
    put("slot", np.arange(C))
    put("half", (np.arange(P)[:, None] >= C))
    put("head", (np.arange(P)[:, None] < META))
    return t


def kernel(**inputs):
    import numpy as _np
    import concourse.bacc as _bacc
    from concourse.bass_utils import run_bass_kernel_spmd as _run

    nc = _bacc.Bacc("TRN2", target_bir_lowering=False, num_devices=1)
    arrays, args = {}, []
    for name in _INS:
        a = _np.ascontiguousarray(inputs[name])
        arrays[f"in_{name}"] = a
        args.append(nc.dram_tensor(f"in_{name}", a.shape, mybir.dt.from_np(a.dtype), kind="ExternalInput").ap())
    table = constants()
    arrays["in_table"] = table
    args.append(nc.dram_tensor("in_table", table.shape, F32, kind="ExternalInput").ap())
    args.append(nc.dram_tensor("out", (1, SEQ, D), F32, kind="ExternalOutput").ap())
    build(nc, *args)
    r = _run(nc, [arrays], core_ids=[0])
    return r.results[0]["out"]
```
